# Optimizing a Trainium2 kernel written in Bass

```python
import math
import jax, jax.numpy as jnp
from jax import lax
import numpy as np

D_MODEL = 2048
BATCH = 1
SEQ = 256
DEPTH = 1
DEC_BATCH = 8
DEC_SEQ = 1
PAST_LEN = 2048
PAGE_SIZE = 128

HEAD_DIM = 128
HEADS_PER_GROUP = 4
ATT_GROUPS = ((128, 1), (512, 4), (2048, 16))
N_ATT_GROUPS = len(ATT_GROUPS)
N_ATT_HEADS = N_ATT_GROUPS * HEADS_PER_GROUP
ATT_WIDTH = N_ATT_HEADS * HEAD_DIM
ATT_OUT_WIDTH = HEADS_PER_GROUP * HEAD_DIM
ATT_SCALE = HEAD_DIM ** -0.5
ROPE_THETA = 10000.0
QBLOCK = 128
SSM_WIDTH = D_MODEL // 2
SSM_GROUP = 16
SSM_GROUPS = SSM_WIDTH // SSM_GROUP
SSM_STATE = 64
D_FF = ((8 * D_MODEL // 3 + 127) // 128) * 128
IN_WIDTH = 3 * ATT_WIDTH + SSM_WIDTH + 2 * D_MODEL
RMS_EPS = 1e-6

kernel_name = "dilated_attn_s5_gated_macaron_step"

def rmsnorm(x, gain):
    xf = x.astype(jnp.float32)
    y = xf * lax.rsqrt(jnp.mean(xf * xf, axis=-1, keepdims=True) + RMS_EPS)
    return (y * gain.astype(jnp.float32)).astype(x.dtype)

def rope(x, pos):
    half = HEAD_DIM // 2
    inv = jnp.power(ROPE_THETA, -jnp.arange(half, dtype=jnp.float32) * (2.0 / HEAD_DIM))
    ang = pos.astype(jnp.float32)[:, None] * inv[None, :]
    cos, sin = jnp.cos(ang)[:, None, :], jnp.sin(ang)[:, None, :]
    xf = x.astype(jnp.float32)
    x1, x2 = xf[..., :half], xf[..., half:]
    return jnp.concatenate([x1 * cos - x2 * sin, x2 * cos + x1 * sin], axis=-1).astype(x.dtype)

def swiglu(x, w_gate, w_up, w_down):
    return (jax.nn.silu(x @ w_gate) * (x @ w_up)) @ w_down

def masked_softmax_lse(s, mask):
    s = jnp.where(mask, s, -jnp.inf)
    mx = jnp.max(s, axis=-1, keepdims=True)
    p = jnp.exp(s - mx)
    den = jnp.sum(p, axis=-1, keepdims=True)
    return p / den, (mx + jnp.log(den))[..., 0]

def dilated_attn_prompt(q, k, v, dil, n_back):
    B, L, H, E = q.shape
    M = L // dil
    bq = math.gcd(M, QBLOCK)
    nblk = M // bq
    bk = bq + n_back
    qr = q.reshape(B, nblk, bq, dil, H, E)
    pad = ((0, 0), (n_back, 0), (0, 0), (0, 0), (0, 0))
    kp = jnp.pad(k.reshape(B, M, dil, H, E), pad)
    vp = jnp.pad(v.reshape(B, M, dil, H, E), pad)
    idx = jnp.arange(nblk)[:, None] * bq + jnp.arange(bk)[None, :]
    kb, vb = kp[:, idx], vp[:, idx]
    s = jnp.einsum('bnqrhe,bnkrhe->bnrhqk', qr, kb, preferred_element_type=jnp.float32) * ATT_SCALE
    qi = jnp.arange(bq)[:, None]
    ki = jnp.arange(bk)[None, :]
    rel = qi - ki + n_back
    kpos = jnp.arange(nblk)[:, None, None] * bq + ki[None] - n_back
    mask = (rel >= 0) & (rel <= n_back) & (kpos >= 0)
    p, lse = masked_softmax_lse(s, mask[None, :, None, None])
    o = jnp.einsum('bnrhqk,bnkrhe->bnqrhe', p, vb.astype(jnp.float32))
    return o.reshape(B, L, H, E), lse.transpose(0, 1, 4, 2, 3).reshape(B, L, H)

def dilated_attn_decode(q, k_all, v_all, buf_len, dil, n_back):
    S = q.shape[1]
    idx = buf_len + jnp.arange(S)[:, None] - jnp.arange(n_back + 1)[None, :] * dil
    valid = idx >= 0
    idxc = jnp.maximum(idx, 0)
    kg, vg = k_all[:, idxc], v_all[:, idxc]
    s = jnp.einsum('bshe,bsjhe->bhsj', q, kg, preferred_element_type=jnp.float32) * ATT_SCALE
    p, lse = masked_softmax_lse(s, valid[None, None])
    o = jnp.einsum('bhsj,bsjhe->bshe', p, vg.astype(jnp.float32))
    return o, lse.transpose(0, 2, 1)

def _ssm_combine(e1, e2):
    a1r, a1i, b1r, b1i = e1
    a2r, a2i, b2r, b2i = e2
    ar = a2r * a1r - a2i * a1i
    ai = a2r * a1i + a2i * a1r
    a2rb, a2ib = a2r[:, None], a2i[:, None]
    br = a2rb * b1r - a2ib * b1i + b2r
    bi = a2rb * b1i + a2ib * b1r + b2i
    return ar, ai, br, bi

def s5_ssm(u, x0, lam_re, lam_im, log_dt, b_re, b_im, c_re, c_im, d_skip):
    f32 = jnp.float32
    Bn, L, _ = u.shape
    uf = u.astype(f32).reshape(Bn, L, SSM_GROUPS, SSM_GROUP)
    lr, li = lam_re.astype(f32), lam_im.astype(f32)
    dt = jnp.exp(log_dt.astype(f32))[:, None]
    mag = jnp.exp(lr * dt)
    ar, ai = mag * jnp.cos(li * dt), mag * jnp.sin(li * dt)
    den = lr * lr + li * li
    fr = ((ar - 1.0) * lr + ai * li) / den
    fi = (ai * lr - (ar - 1.0) * li) / den
    br, bi = b_re.astype(f32), b_im.astype(f32)
    bbr = fr[..., None] * br - fi[..., None] * bi
    bbi = fr[..., None] * bi + fi[..., None] * br
    bu_r = jnp.einsum('blgc,gpc->lbgp', uf, bbr)
    bu_i = jnp.einsum('blgc,gpc->lbgp', uf, bbi)
    a_r = jnp.broadcast_to(ar, (L,) + ar.shape)
    a_i = jnp.broadcast_to(ai, (L,) + ai.shape)
    acc_r, acc_i, xr, xi = lax.associative_scan(_ssm_combine, (a_r, a_i, bu_r, bu_i), axis=0)
    if x0 is not None:
        x0r, x0i = x0[0].astype(f32)[None], x0[1].astype(f32)[None]
        pr, pi = acc_r[:, None], acc_i[:, None]
        xr, xi = xr + pr * x0r - pi * x0i, xi + pr * x0i + pi * x0r
    y = (jnp.einsum('lbgp,gcp->blgc', xr, c_re.astype(f32))
         - jnp.einsum('lbgp,gcp->blgc', xi, c_im.astype(f32))
         + d_skip.astype(f32).reshape(SSM_GROUPS, SSM_GROUP) * uf)
    return y.reshape(Bn, L, SSM_WIDTH).astype(u.dtype), xr[-1], xi[-1]

def layer(x, pos, kv_cache, ssm_state, p):
    B, L, _ = x.shape
    x = x + 0.5 * swiglu(rmsnorm(x, p['ffn1_norm']), p['ffn1_w_gate'], p['ffn1_w_up'], p['ffn1_w_down'])
    h = rmsnorm(x, p['mix_norm'])
    z = h @ p['w_in']
    q = z[..., :ATT_WIDTH].reshape(B, L, N_ATT_HEADS, HEAD_DIM)
    k = z[..., ATT_WIDTH:2 * ATT_WIDTH].reshape(B, L, N_ATT_HEADS, HEAD_DIM)
    v = z[..., 2 * ATT_WIDTH:3 * ATT_WIDTH].reshape(B, L, N_ATT_HEADS, HEAD_DIM)
    o_u = 3 * ATT_WIDTH
    u = z[..., o_u:o_u + SSM_WIDTH]
    gate_a = z[..., o_u + SSM_WIDTH:o_u + SSM_WIDTH + D_MODEL]
    gate_s = z[..., o_u + SSM_WIDTH + D_MODEL:]
    q = rope(rmsnorm(q, p['q_norm']), pos)
    k = rope(rmsnorm(k, p['k_norm']), pos)

    outs, lses, new_kv = [], [], []
    for g, (window, dil) in enumerate(ATT_GROUPS):
        hs = slice(g * HEADS_PER_GROUP, (g + 1) * HEADS_PER_GROUP)
        qg, kg, vg = q[:, :, hs], k[:, :, hs], v[:, :, hs]
        n_back = window // dil
        if kv_cache is None:
            o, lse = dilated_attn_prompt(qg, kg, vg, dil, n_back)
            keep = min(window, L)
            new_kv.append(jnp.stack([kg[:, L - keep:], vg[:, L - keep:]], axis=1))
        else:
            buf = kv_cache[g]
            buf_len = buf.shape[2]
            k_all = jnp.concatenate([buf[:, 0].astype(kg.dtype), kg], axis=1)
            v_all = jnp.concatenate([buf[:, 1].astype(vg.dtype), vg], axis=1)
            o, lse = dilated_attn_decode(qg, k_all, v_all, buf_len, dil, n_back)
            new_kv.append(jnp.stack([k_all[:, L:], v_all[:, L:]], axis=1))
        outs.append(o)
        lses.append(lse)
    w_grp = jax.nn.softmax(jnp.stack(lses, axis=-1), axis=-1)
    att = jnp.einsum('blhg,blhge->blhe', w_grp, jnp.stack(outs, axis=3))
    att = att.reshape(B, L, ATT_OUT_WIDTH).astype(x.dtype)

    y_ssm, s_re, s_im = s5_ssm(u, ssm_state, p['ssm_lambda_re'], p['ssm_lambda_im'], p['ssm_log_dt'],
                               p['ssm_b_re'], p['ssm_b_im'], p['ssm_c_re'], p['ssm_c_im'], p['ssm_d'])
    zs = jax.nn.gelu(y_ssm)
    s_out = zs * jax.nn.sigmoid(zs @ p['glu_w'] + p['glu_b'])

    merged = (jax.nn.sigmoid(gate_a) * (att @ p['w_attn_branch'])
              + jax.nn.sigmoid(gate_s) * (s_out @ p['w_ssm_branch']))
    x = x + merged @ p['w_out']
    x = x + 0.5 * swiglu(rmsnorm(x, p['ffn2_norm']), p['ffn2_w_gate'], p['ffn2_w_up'], p['ffn2_w_down'])
    return x, new_kv, (s_re.astype(x.dtype), s_im.astype(x.dtype))

def setup_inputs(seed: int = 0) -> dict:
    key = jax.random.key(seed)
    ks = iter(jax.random.split(key, 64))
    f32 = jnp.float32

    def normal(shape, scale):
        return jax.random.normal(next(ks), shape, f32) * scale

    def gain(shape):
        return 1.0 + normal(shape, 0.05)

    buf = [min(w, PAST_LEN) for (w, _) in ATT_GROUPS]
    kv_shape = lambda n: (DEPTH, DEC_BATCH, 2, n, HEADS_PER_GROUP, HEAD_DIM)
    n_idx = jnp.arange(SSM_STATE, dtype=f32)
    gp = (DEPTH, SSM_GROUPS, SSM_STATE)
    return {
        "x_prompt": normal((BATCH, SEQ, D_MODEL), 1.0),
        "x_sample": normal((DEC_BATCH, DEC_SEQ, D_MODEL), 1.0),
        "cache_kv_w128": normal(kv_shape(buf[0]), 1.0),
        "cache_kv_w512": normal(kv_shape(buf[1]), 1.0),
        "cache_kv_w2048": normal(kv_shape(buf[2]), 1.0),
        "state_ssm_re": normal((DEPTH, DEC_BATCH, SSM_GROUPS, SSM_STATE), 0.3),
        "state_ssm_im": normal((DEPTH, DEC_BATCH, SSM_GROUPS, SSM_STATE), 0.3),
        "ffn1_norm": gain((DEPTH, D_MODEL)),
        "ffn1_w_gate": normal((DEPTH, D_MODEL, D_FF), D_MODEL ** -0.5),
        "ffn1_w_up": normal((DEPTH, D_MODEL, D_FF), D_MODEL ** -0.5),
        "ffn1_w_down": normal((DEPTH, D_FF, D_MODEL), D_FF ** -0.5),
        "mix_norm": gain((DEPTH, D_MODEL)),
        "w_in": normal((DEPTH, D_MODEL, IN_WIDTH), D_MODEL ** -0.5),
        "q_norm": gain((DEPTH, N_ATT_HEADS, HEAD_DIM)),
        "k_norm": gain((DEPTH, N_ATT_HEADS, HEAD_DIM)),
        "ssm_lambda_re": -0.5 + normal(gp, 0.01),
        "ssm_lambda_im": math.pi * n_idx + normal(gp, 0.01),
        "ssm_log_dt": jax.random.uniform(next(ks), (DEPTH, SSM_GROUPS), f32, math.log(1e-3), math.log(1e-1)),
        "ssm_b_re": normal((DEPTH, SSM_GROUPS, SSM_STATE, SSM_GROUP), (2 * SSM_GROUP) ** -0.5),
        "ssm_b_im": normal((DEPTH, SSM_GROUPS, SSM_STATE, SSM_GROUP), (2 * SSM_GROUP) ** -0.5),
        "ssm_c_re": normal((DEPTH, SSM_GROUPS, SSM_GROUP, SSM_STATE), SSM_STATE ** -0.5),
        "ssm_c_im": normal((DEPTH, SSM_GROUPS, SSM_GROUP, SSM_STATE), SSM_STATE ** -0.5),
        "ssm_d": normal((DEPTH, SSM_WIDTH), 1.0),
        "glu_w": normal((DEPTH, SSM_WIDTH, SSM_WIDTH), SSM_WIDTH ** -0.5),
        "glu_b": normal((DEPTH, SSM_WIDTH), 0.01),
        "w_attn_branch": normal((DEPTH, ATT_OUT_WIDTH, D_MODEL), ATT_OUT_WIDTH ** -0.5),
        "w_ssm_branch": normal((DEPTH, SSM_WIDTH, D_MODEL), SSM_WIDTH ** -0.5),
        "w_out": normal((DEPTH, D_MODEL, D_MODEL), D_MODEL ** -0.5),
        "ffn2_norm": gain((DEPTH, D_MODEL)),
        "ffn2_w_gate": normal((DEPTH, D_MODEL, D_FF), D_MODEL ** -0.5),
        "ffn2_w_up": normal((DEPTH, D_MODEL, D_FF), D_MODEL ** -0.5),
        "ffn2_w_down": normal((DEPTH, D_FF, D_MODEL), D_FF ** -0.5),
    }

def reference(x_prompt, x_sample, cache_kv_w128, cache_kv_w512, cache_kv_w2048, state_ssm_re, state_ssm_im,
              ffn1_norm, ffn1_w_gate, ffn1_w_up, ffn1_w_down, mix_norm, w_in, q_norm, k_norm,
              ssm_lambda_re, ssm_lambda_im, ssm_log_dt, ssm_b_re, ssm_b_im, ssm_c_re, ssm_c_im, ssm_d,
              glu_w, glu_b, w_attn_branch, w_ssm_branch, w_out,
              ffn2_norm, ffn2_w_gate, ffn2_w_up, ffn2_w_down):
    pos_p = jnp.arange(x_prompt.shape[1], dtype=jnp.int32)
    pos_s = PAST_LEN + jnp.arange(x_sample.shape[1], dtype=jnp.int32)
    yp, ys = x_prompt, x_sample
    new_p = [[] for _ in range(5)]
    new_s = [[] for _ in range(5)]
    for l in range(DEPTH):
        p = dict(ffn1_norm=ffn1_norm[l], ffn1_w_gate=ffn1_w_gate[l], ffn1_w_up=ffn1_w_up[l],
                 ffn1_w_down=ffn1_w_down[l], mix_norm=mix_norm[l], w_in=w_in[l],
                 q_norm=q_norm[l], k_norm=k_norm[l],
                 ssm_lambda_re=ssm_lambda_re[l], ssm_lambda_im=ssm_lambda_im[l], ssm_log_dt=ssm_log_dt[l],
                 ssm_b_re=ssm_b_re[l], ssm_b_im=ssm_b_im[l], ssm_c_re=ssm_c_re[l], ssm_c_im=ssm_c_im[l],
                 ssm_d=ssm_d[l], glu_w=glu_w[l], glu_b=glu_b[l],
                 w_attn_branch=w_attn_branch[l], w_ssm_branch=w_ssm_branch[l], w_out=w_out[l],
                 ffn2_norm=ffn2_norm[l], ffn2_w_gate=ffn2_w_gate[l], ffn2_w_up=ffn2_w_up[l],
                 ffn2_w_down=ffn2_w_down[l])
        yp, kv_p, st_p = layer(yp, pos_p, None, None, p)
        ys, kv_s, st_s = layer(ys, pos_s, (cache_kv_w128[l], cache_kv_w512[l], cache_kv_w2048[l]),
                               (state_ssm_re[l], state_ssm_im[l]), p)
        for i, a in enumerate(kv_p + list(st_p)):
            new_p[i].append(a)
        for i, a in enumerate(kv_s + list(st_s)):
            new_s[i].append(a)
    kv128_p, kv512_p, kv2048_p, ssm_re_p, ssm_im_p = [jnp.stack(a) for a in new_p]
    kv128_s, kv512_s, kv2048_s, ssm_re_s, ssm_im_s = [jnp.stack(a) for a in new_s]
    return (yp, ys, kv128_p, kv512_p, kv2048_p, ssm_re_p, ssm_im_p,
            kv128_s, kv512_s, kv2048_s, ssm_re_s, ssm_im_s)


_drawn_inputs = setup_inputs


def setup_inputs(seed=0):
    import zlib

    import numpy as np

    out = dict(_drawn_inputs(seed))
    spreads = {}
    factors = {'q_norm': 8.0, 'ssm_lambda_re': 17.392, 'glu_b': 52.193, 'ffn2_norm': 2.799}
    for name, (base, spread) in spreads.items():
        noise = np.random.default_rng([zlib.crc32(name.encode()), seed]).standard_normal(out[name].shape)
        drawn = base * np.exp(spread * noise) if base else spread * noise
        out[name] = __import__('jax').numpy.asarray(drawn.astype(out[name].dtype))
    for name, factor in factors.items():
        out[name] = (out[name] * factor).astype(out[name].dtype)
    return out
```

```python
import numpy as np
import concourse.bass as bass
from concourse import mybir

D = 2048
P = 128
KD = D // P
NT = 256
NS = 8
T = NT + NS
FF = 5504
HD = 128
NSLOT = 4
GROUPS = ((128, 1), (512, 4), (2048, 16))
NG = len(GROUPS)
NH = NG * NSLOT
BACK = 128
SW = 1024
SC = SW // P
NTILE = 32
STEP = 4
NB = NT // STEP
LAGS = STEP + 1
UOFF = 3 * NH * HD
GOFF = UOFF + SW
EPS = 1e-6
SCALE = float(HD) ** -0.5
NEG = -1e30

RING = 4
LEAD = 3
KS = 4

BLOCK_TILE0 = (0, 16, 32)


def ffn_phases(f):
    return [(f"up{f}0", 8, 8, 2), (f"down{f}0", 4, 8, 2), (f"up{f}1", 8, 8, 2), (f"down{f}1", 4, 8, 2),
            (f"up{f}2", 5, 8, 2), (f"single{f}", 1, 4, 2), (f"down{f}2", 2, 12, 4)]


MIX_PHASES = [("u", 4, 4, 1), ("q", 6, 4, 1), ("k", 6, 4, 1), ("v", 6, 4, 1), ("gates_a", 8, 4, 1),
              ("gates_b", 4, 8, 2), ("attn_branch", 2, 4, 4), ("glu", 2, 4, 2), ("ssm_branch", 4, 4, 2),
              ("w_out", 4, 8, 2)]
ORDER = ffn_phases(0) + MIX_PHASES + ffn_phases(1)

ACT0 = {"up00": 0, "up01": 8, "up02": 16, "single0": 21, "ssm_branch": 22,
        "up10": 30, "up11": 38, "up12": 46, "single1": 51}
HID0 = {"up00": 0, "up01": 8, "up02": 16, "single0": 21, "up10": 22, "up11": 30, "up12": 38, "single1": 43}
NORM_AFTER = {"down02": 1, "w_out": 2}
LAST = ORDER[-1][0]

VEC_LOADS = (("ffn1_norm", 0, 16), ("mix_norm", 16, 16), ("ffn2_norm", 32, 16), ("q_norm", 48, 12),
             ("k_norm", 60, 12), ("glu_b", 72, 8))
V_NORM, V_HEAD, V_GLU, NV = (0, 16, 32), 48, 72, 80

C_COS, C_SIN, C_GM, C_MASK0 = 0, T, 2 * T, 2 * T + 2
C_MASK1 = C_MASK0 + NG * P
NC = C_MASK1 + NG * NT

TB_B, TB_C, TB_K, TB_E, TB_M, TB = 0, 1024, 2048, 2560, 3072, 3328
MAGIC = 1.5 * 2.0 ** 23
TWO_PI = (6.28125, 0.0019350051879882812, 3.0199157663e-07)


def shape_constants():
    past = 2048
    pos = np.concatenate([np.arange(NT), np.full(NS, past)]).astype(np.float32)
    inv = np.power(np.float32(10000.0), -np.arange(HD // 2, dtype=np.float32) * np.float32(2.0 / HD))
    ang = (pos[None, :] * inv[:, None]).astype(np.float32)
    c = np.zeros((P, NC), np.float32)
    c[:, C_COS:C_COS + T] = np.concatenate([np.cos(ang), np.cos(ang)], 0)
    c[:, C_SIN:C_SIN + T] = np.concatenate([np.sin(ang), -np.sin(ang)], 0)
    c[:, C_GM + 1] = (np.arange(P) // 16) % 2
    c[:, C_GM] = 1 - c[:, C_GM + 1]
    for first, width, base in ((0, P, C_MASK0), (P, NT, C_MASK1)):
        q, k = np.arange(first, first + P)[:, None], np.arange(width)[None, :]
        for g, (_, dil) in enumerate(GROUPS):
            ok = (k <= q) & (q - k <= BACK * dil) & ((q - k) % dil == 0)
            c[:, base + g * width:base + (g + 1) * width] = np.where(ok, 0.0, NEG)
    return c


class Phase:

    def __init__(self, name, iters, slabs, groups, slab0, group0):
        self.name, self.iters, self.slabs, self.groups = name, iters, slabs, groups
        self.slab0, self.group0 = slab0, group0

    def slab(self, i, j):
        return (self.slab0 + j) % RING, (self.slab0 + j) // RING + i * (self.slabs // RING), self.slab0 + j + i * self.slabs

    def banks(self, i, g):
        return (self.group0 + g + (i * self.groups if self.groups % 2 else 0)) % 2

    def group(self, i, g):
        return self.group0 + g + i * self.groups


def plan():
    phases, slab, group = {}, 0, 0
    for name, iters, slabs, groups in ORDER:
        phases[name] = Phase(name, iters, slabs, groups, slab, group)
        slab, group = slab + iters * slabs, group + iters * groups
    return phases, slab


def pair_slabs(name):
    if name in ("down02", "down12"):
        return (4, 4, 3)
    return {"attn_branch": (4,), "glu": (4, 4), "ssm_branch": (4, 4)}.get(name, (4, 4, 4, 4))


def below(n, limit):
    return isinstance(n, int) and n < limit


def loop(eng, ph, body, peel=0):
    if ph.iters - peel == 1:
        peel = ph.iters
    for i in range(peel):
        body(i)
    if ph.iters > peel:
        with eng.Fori(peel, ph.iters) as i:
            body(i)


class Chain:

    def __init__(self, eng, sem):
        self.eng, self.sem, self.n = eng, sem, 0

    def __call__(self, ins):
        self.n += 1
        ins.then_inc(self.sem, 1)
        self.eng.wait_ge(self.sem, self.n)


def build_layer(nc, A, O):
    f32, f32r = mybir.dt.float32, mybir.dt.float32r
    ALU, ACT, AX = mybir.AluOpType, mybir.ActivationFunctionType, mybir.AxisListType
    PH, TOTAL = plan()

    END = 229344
    top = [16512]

    def region(nbytes):
        at = top[0]
        top[0] += (nbytes + 31) // 32 * 32
        assert top[0] <= END, top[0]
        return at

    def tile(name, shape, dt=f32, at=None):
        if at is None:
            at = region(4 * int(np.prod(shape[1:])))
        return nc.alloc_sbuf_tensor_at(name, shape, dt, offset=at)

    def tiles(at, limit, *specs):
        out, start = [], at
        for name, shape, *dt in specs:
            out.append(tile(name, shape, dt[0] if dt else f32, at))
            at += (4 * int(np.prod(shape[1:])) + 31) // 32 * 32
        assert at - start <= limit, (specs[0][0], at - start, limit)
        return out

    CH = 4 * KD * T
    raw = tile("raw", [P, RING, KS, 256])
    w_hi = tile("w_hi", [P, RING, KS, 256], f32r)
    w_lo = tile("w_lo", [P, RING, KS, 256], f32r)
    rstd = tile("rstd", [P, T])
    sd = tile("sd", [P, T])
    ident, mean_w, head_w, ones = (tile(n, [P, P]) for n in ("ident", "mean_w", "head_w", "ones"))
    vec = tile("vec", [P, NV])
    small = tile("small", [P, 4])
    eps_t, halfpi_t = small[:, 0:1], small[:, 1:2]

    RX = region(CH)
    x_t = tile("x_t", [P, KD, T], f32, RX)
    u4, att_v, qb1 = tiles(RX, CH, ("u4", [P, NTILE, NS + NB + NS]),
                           ("att_v", [P, NSLOT, T]),
                           ("qb1", [P, NSLOT * HD]))
    RG = region(2 * CH)
    xg_hi, xg_lo = tiles(RG, 2 * CH, ("xg_hi", [P, KD, T], f32r), ("xg_lo", [P, KD, T], f32r))
    s_hi, s_lo, zs_v = tiles(RG, 2 * CH, ("s_hi", [P, SC, T], f32r), ("s_lo", [P, SC, T], f32r), ("zs_v", [P, SC, T]))
    y_rows = tile("y_rows", [P, 3, D], f32, RG)
    RA = region(2 * CH)
    act_hi, act_lo = tiles(RA, 2 * CH, ("act_hi", [P, KD, T], f32r), ("act_lo", [P, KD, T], f32r))
    x_rows = tile("x_rows", [P, 3, D], f32, RA)
    gates = tile("gates", [P, 2 * KD, T], f32, RA)
    masks, probs, probs_t, dec_p, dec_diag = tiles(
        RA + CH, CH, ("masks", [P, NG * (P + NT)]), ("probs", [P, NG * (P + NT)]),
        ("probs_t", [P, 9, P]), ("dec_p", [NS * NSLOT, NG * P + NG]), ("dec_diag", [NS * NSLOT, NG, NS * NSLOT]))
    RT = region(5 * 8 * T)
    gate_v, up_v, silu_v, hid_v, sq_v = tiles(RT, 40 * T, *((n, [P, 2, T]) for n in ("gate_v", "up_v", "silu_v", "hid_v", "sq_v")))
    prod = [tile(f"prod{k}", [P, NSLOT, HD], f32, RT + 8 * T * (k + 1)) for k in range(2)]
    sv = tile("sv", [P, 2, 4 * NB], f32, RT + 24 * T)
    att_hi, att_lo = tiles(RT + 8 * T, 32 * T, ("att_hi", [P, NSLOT, T], f32r), ("att_lo", [P, NSLOT, T], f32r))
    RQ = region(8 * T)
    ssq = tile("ssq", [P, 2, T], f32, RQ)
    qb0 = tile("qb0", [P, NSLOT * HD], f32, RT + 32 * T)
    qb = [qb0, qb1]
    head_sd = tile("head_sd", [P, 2, T], f32, RQ)
    QKV = 4 * (2 * NH * T + 2 * NH * HD)
    RM = region(QKV)
    qk, v_tok = tiles(RM, QKV, ("qk", [P, 2 * NH, T]),
                      ("v_tok", [P, 2, NH * HD]))
    tab0, tab1, z_out, d_tmp, z_in, xs, p_tmp = tiles(
        RM, QKV, ("tab0", [P, TB]), ("tab1", [P, TB]), ("z_out", [P, 2, 4 * NB]), ("d_tmp", [P, 2, 4 * NB]), ("z_in", [P, 2, 4 * NB]),
        ("xs", [P, 2, 4, NS + 1 + NB]), ("p_tmp", [P, 2, 4 * NB]))
    tab = [tab0, tab1]
    zs_hi, zs_lo, yt_v = tiles(RM, QKV, ("zs_hi", [P, SC, T], f32r), ("zs_lo", [P, SC, T], f32r), ("yt_v", [P, SC, T]))
    RR = region(4 * (SC * T + 2 * T + 2 * 512 + 512))
    RRN = top[0] - RR
    u_t, cs, k_rows, s_rows = tiles(RR, RRN, ("u_t", [P, SC, T]), ("cs", [P, 2, T]), ("k_rows", [P, 2, 512]), ("s_rows", [P, 512]))
    ku = [tile(f"ku{k}", [P, NSLOT * HD], f32, RR + 2048 * k) for k in range(4)]
    vu = [tile(f"vu{k}", [P, NSLOT * HD], f32, RR + 2048 * k) for k in range(6)]
    xnew, xtmp, st_rows = tiles(RR, RRN, ("xnew", [P, 2, 256]), ("xtmp", [P, 3, 256]), ("st_rows", [P, 6, P]))
    em_tab, ctmp, b_in, c_in = tiles(RM, top[0] - RM, ("em_tab", [P, 3, NTILE, NB]),
                                           ("ctmp", [P, 2, NTILE, NB // 2]), ("b_in", [P, 2, NTILE, 16]),
                                           ("c_in", [P, 2, SC, 64]))
    prm, pw, npowi, wf, scr = tiles(RM + 40960, top[0] - RM - 40960, ("prm", [P, 4 * NTILE]), ("pw", [P, 2, NTILE, LAGS]),
                                   ("npowi", [P, NTILE, LAGS]), ("wf", [P, 2, NTILE, STEP]), ("scr", [P, 26, NTILE]))
    vec_rows, prm_rows, log_dt, x0_rows = tiles(RM, 4096, ("vec_rows", [P, P]), ("prm_rows", [P, P]), ("log_dt", [P, 2]),
                                                ("x0_rows", [P, 2, 2, P]))
    BASE2 = 4 * (2 * NTILE * NB + NTILE * NB + 2 * NTILE * NB // 2)
    pre, bb_t, ca5, kbig, ca_tmp, c_exp, c_t, b_tmp = tiles(
        RM, BASE2, ("pre", [P, 2, 4, STEP, 2, 16]), ("bb_t", [P, 1024]), ("ca5", [P, 4, 2, LAGS * 32]), ("kbig", [P, 4, P]),
        ("ca_tmp", [P, 2, 4, LAGS * 32]), ("c_exp", [P, 2, 2, 64]), ("c_t", [P, 2, 4, 32]), ("b_tmp", [P, 2, 4, STEP, 16]))
    x0_t = tile("x0_t", [P, 2, NS, NTILE])
    s_new = tile("s_new", [P, 2, NTILE, NS])
    x_fin = tile("x_fin", [P, 2, NTILE])
    sc_dec = tile("sc_dec", [P, NG, NS, NSLOT])
    kq = tile("kq", [P, NG, NS, NSLOT])
    v_new = tile("v_new", [P, NH, NS])
    pt_dec = tile("pt_dec", [P, NG, NS * NSLOT])
    att_new = tile("att_new", [P, NG, NS * NSLOT])
    stat = tile("stat", [P, 16])
    a_t = tile("a_t", [P, 2, NTILE])
    gm = tile("gm", [P, 2])

    pa = nc.alloc_psum_tensor("pa", [P, 4, 512], f32)
    pb = nc.alloc_psum_tensor("pb", [P, 4, 512], f32)

    ssm_tab = nc.dram_tensor("ssm_tab", [SC, P, TB], f32).ap()
    q_dram = nc.dram_tensor("q_dram", [NS, NH * HD], f32).ap()
    x_dram = nc.dram_tensor("x_dram", [P, KD * T], f32).ap()


    def sems(names):
        return [nc.alloc_semaphore(n) for n in names.split()]

    slab_loaded = [nc.alloc_semaphore(f"slab_loaded{k}") for k in range(RING)]
    hi_ready, lo_ready, slab_used, evacuated = sems("hi_ready lo_ready slab_used evacuated")
    const_ready, rows_loaded, vec_t, vec_ready, rows_t, x_ready = sems("const_ready rows_loaded vec_t vec_ready rows_t x_ready")
    sq_ready, ssq_ready, ssq_zero, xhi_ready, xlo_ready = sems("sq_ready ssq_ready ssq_zero xhi_ready xlo_ready")
    mean_ready, sd_ready, rstd_ready = sems("mean_ready sd_ready rstd_ready")
    gate_ready, silu_ready, hid_ready, acthi_ready, actlo_ready = sems("gate_ready silu_ready hid_ready acthi_ready actlo_ready")
    par_loaded, dt_loaded, dt_rows, prm_t, prm_ready, dt_ready = sems("par_loaded dt_loaded dt_rows prm_t prm_ready dt_ready")
    angles_ready, trig_ready, den_ready, inv_ready, step_done = sems("angles_ready trig_ready den_ready inv_ready step_done")
    tab_stored, pre_ready, bb_done, bbt_ready, ca_ready, k_done, kbig_ready = sems(
        "tab_stored pre_ready bb_done bbt_ready ca_ready k_done kbig_ready")
    ca_step, k_step = sems("ca_step k_step")
    u_ready, u4_zero, u4_loaded, spilled, const_loaded = sems("u_ready u4_zero u4_loaded spilled const_loaded")
    head_sq, stat_done, head_sd_ready, head_inv, t1_ready, rot_ready, cos_ready, qk_ready = sems(
        "head_sq stat_done head_sd_ready head_inv t1_ready rot_ready cos_ready qk_ready")
    heads_t, rows_ready, rows_stored, v_new_ready = sems("heads_t rows_ready rows_stored v_new_ready")
    ku_loaded = [nc.alloc_semaphore(f"ku_loaded{k}") for k in range(4)]
    qb_loaded = [nc.alloc_semaphore(f"qb_loaded{k}") for k in range(2)]
    vu_loaded = [nc.alloc_semaphore(f"vu_loaded{k}") for k in range(2)]
    prod_ready, sc_ready, kq_ready, ds_done, dmax_ready, dexp_ready, dec_step, diag_ready, dt_done, dec_ready = sems(
        "prod_ready sc_ready kq_ready ds_done dmax_ready dexp_ready dec_step diag_ready dt_done dec_ready")
    pv_done, pv_read = sems("pv_done pv_read")
    s_done, sm_ready, sm_step, nmax_ready, exp_ready, inv_sum, pn_ready, p_t, pt_ready, att_done, att_read = sems(
        "s_done sm_ready sm_step nmax_ready exp_ready inv_sum pn_ready p_t pt_ready att_done att_read")
    tab_loaded = [nc.alloc_semaphore(f"tab_loaded{k}") for k in range(2)]
    xs_zero, su_done, sv_ready, zr_ready, zi_step, zr_step, scan_ready, xi_ready, xr_ready, y_done, y_read = sems(
        "xs_zero su_done sv_ready zr_ready zi_step zr_step scan_ready xi_ready xr_ready y_done y_read")
    yt_loaded, yl_loaded, gelu_ready, zhi_ready, zlo_ready, sgl_ready, shi_ready, slo_ready = sems(
        "yt_loaded yl_loaded gelu_ready zhi_ready zlo_ready sgl_ready shi_ready slo_ready")
    xnew_step, st_t, st_rows_ready = sems("xnew_step st_t st_rows_ready")
    att_hi_ready, att_lo_ready, sig_ready, prod_s, m_ready, x_back = sems("att_hi_ready att_lo_ready sig_ready prod_s m_ready x_back")
    yt_ready, yrow_ready, stored = sems("yt_ready yrow_ready stored")

    def q_end(name):
        return PH[name].slab0 + PH[name].iters * PH[name].slabs

    XQ = {"q": 0, "k": 6, "v": 12, "gates_a": 18}

    def pair_group(x):
        return PH["q"].group0 + x

    def stored_rows(r):
        return 16 * (r + 1) if r < 3 else 48 + 32 * (r - 2)

    caches = [A["cache_kv_w128"][0], A["cache_kv_w512"][0], A["cache_kv_w2048"][0]]
    new_caches = [O["kv128_s"][0], O["kv512_s"][0], O["kv2048_s"][0]]
    prompt_kv = [O["kv128_p"][0, 0], O["kv512_p"][0, 0], O["kv2048_p"][0, 0]]
    UNIT_LOAD, UNIT_USE = 13, 9
    UNITS = [(g, b) for g in range(NG) for b in range(NS)]
    E0, M0 = TB_E, TB_M

    block = nc.Block()
    with block:
        @block.sync
        def _(sync):
            n_stored = [0]

            def put(ph, i, j, src, kt=KS, mt=256):
                slot, turn, n = ph.slab(i, j)
                if not below(n, RING):
                    sync.wait_ge(lo_ready, n - (RING - 1))
                dst = raw[:, slot, 0:kt, :]
                if mt == P:
                    dst = raw[:, slot, :, :].rearrange("p a (b m) -> p (a b) m", b=2)
                sync.dma_start(dst, src.rearrange("(k p) m -> p k m", p=P)).then_inc(slab_loaded[slot], 16)

            def cols(w, row, rows, col, width=256):
                return w[row:row + rows, bass.ds(col, width)]

            def shift(g, row, rows, times=1):
                src = caches[g][:, :, bass.ds(row + 1, rows)].rearrange("b t n h d -> (b t) n (h d)")
                dst = new_caches[g][:, :, bass.ds(row, rows)].rearrange("b t n h d -> (b t) n (h d)")
                sync.dma_start(dst, src).then_inc(stored, 16)
                n_stored[0] += 16 * times

            def peeled(ph, peel, body):
                before = n_stored[0]
                loop(sync, ph, body, peel)
                looped = ph.iters - peel if ph.iters - peel > 1 else 0
                if looped:
                    per = (n_stored[0] - before) // (peel + 1)
                    n_stored[0] += per * (looped - 1)

            def ffn(f):
                wg, wu, wd = (A[f"ffn{f + 1}_w_{x}"][0] for x in ("gate", "up", "down"))
                for b in range(3):
                    up0 = 48 * (8 * b + 21 * f)
                    down0 = 32 * (4 * b + 8 * f)
                    def up(i, ph=PH[f"up{f}{b}"], b=b, up0=up0):
                        for j in range(8):
                            put(ph, i, j, cols((wg, wu)[j // 4], 512 * (j % 4), 512, BLOCK_TILE0[b] * P + i * 256))
                            if j in (2, 4, 6):
                                shift(2, up0 + i * 48 + 16 * (j // 2 - 1), 16)
                    peeled(PH[f"up{f}{b}"], 2 if (f, b) == (0, 0) else 1 if b == 0 else 0, up)
                    if b == 2:
                        for j in range(4):
                            put(PH[f"single{f}"], 0, j, cols((wg, wu)[j // 2], 1024 * (j % 2), 1024, FF - P, P), mt=P)
                    kts = pair_slabs(f"down{f}{b}")
                    def down(i, ph=PH[f"down{f}{b}"], b=b, down0=down0, kts=kts):
                        for g in range(ph.groups):
                            for s, kt in enumerate(kts):
                                put(ph, i, g * len(kts) + s, cols(wd, BLOCK_TILE0[b] * P + 512 * s, kt * P, (i * ph.groups + g) * 256), kt)
                                if (f, b) in ((0, 0), (0, 1), (1, 0)) and s == 2:
                                    shift(1, down0 + i * 32 + 16 * g, 16)
                    peeled(PH[f"down{f}{b}"], 0, down)

            tails = [(1, r, min(16, 511 - r)) for r in range(384, 511, 16)] + [(0, r, min(16, 127 - r)) for r in range(0, 127, 16)] \
                + [(2, r, min(16, 2047 - r)) for r in range(2016, 2047, 16)]

            sync.dma_start(x_rows[:, 0:2, :], A["x_prompt"][0].rearrange("(b p) d -> p b d", p=P)).then_inc(rows_loaded, 16)
            sync.dma_start(x_rows[0:NS, 2, :], A["x_sample"][:, 0, :]).then_inc(rows_loaded, 16)
            for name, row, rows in VEC_LOADS:
                src = A[name][0]
                if len(src.shape) == 1:
                    src = src.rearrange("(r c) -> r c", c=P)
                sync.dma_start(vec_rows[row:row + rows, :], src).then_inc(rows_loaded, 16)
            ffn(0)

            w_in = A["w_in"][0]
            for name, col0 in (("u", UOFF), ("q", 0), ("k", NH * HD), ("v", 2 * NH * HD), ("gates_a", GOFF)):
                ph = PH[name]
                for i in range(ph.iters):
                    for j in range(4):
                        put(ph, i, j, cols(w_in, 512 * j, 512, col0 + 256 * i))
                        q_slab = ph.slab0 + 4 * i + j - PH["q"].slab0
                        v_slab = ph.slab0 + 4 * i + j - PH["v"].slab0
                        if name in ("q", "k") and j in (1, 3) and tails:
                            shift(*tails.pop(0))
                        if q_slab == 0:
                            sync.wait_ge(slab_used, q_end("down02"))
                            sync.dma_start(masks[:], A["consts"][:, C_MASK0:NC]).then_inc(const_loaded, 16)
                            sync.wait_ge(tab_stored, 16 * 4 * SC)
                            sync.dma_start(cs[:].rearrange("p a t -> p (a t)"), A["consts"][:, 0:2 * T]).then_inc(const_loaded, 16)
                        if 8 <= q_slab < 32:
                            n = q_slab - 8
                            if n == 0:
                                sync.wait_ge(u4_zero, 1)
                                sync.wait_ge(u_ready, 4)
                            if n < 16:
                                s, jj = n // 4, n % 4
                                dst = u4[32 * s:32 * s + 32, jj::4, NS:NS + NB]
                                src = u_t[32 * jj:32 * jj + 32, :, s * NB:(s + 1) * NB]
                            else:
                                jj, last = n % 4, n >= 20
                                dst = u4[96 * last:96 * last + 32, jj::4, (NS + NB) * last:(NS + NB) * last + NS]
                                src = u_t[32 * jj:32 * jj + 32, :, NT:T]
                            sync.dma_start(dst, src).then_inc(u4_loaded, 16)
                        if 0 <= v_slab - UNIT_LOAD < len(UNITS):
                            n = v_slab - UNIT_LOAD
                            g, b = UNITS[n]
                            if n == 0:
                                sync.wait_ge(u4_loaded, 16 * 24)
                                sync.wait_ge(rows_stored, stored_rows(2))
                                sync.wait_ge(qk_ready, NH)
                            if n >= 4:
                                sync.wait_ge(prod_ready, n - 3)
                            elif n >= 2:
                                sync.wait_ge(prod_ready, n - 1)
                            dil = GROUPS[g][1]
                            src = caches[g][b, 0].rearrange("(m r) h d -> m r (h d)", r=dil)[:, 0, :]
                            sync.dma_start(ku[n % 4][:], src).then_inc(ku_loaded[n % 4], 16)
                            if n >= 4:
                                sync.wait_ge(prod_ready, n - 1)
                            sync.dma_start(qb[n % 2][:], q_dram[b:b + 1, g * 512:(g + 1) * 512].to_broadcast([P, 512])).then_inc(qb_loaded[n % 2], 16)
            while tails:
                shift(*tails.pop(0))

            def gates_b(i, ph=PH["gates_b"]):
                for j in range(8):
                    put(ph, i, j, cols(w_in, 512 * (j % 4), 512, GOFF + D + i * 512 + 256 * (j // 4)))
                    if j in (1, 5):
                        h = j // 4
                        if below(i, 1):
                            if h == 0:
                                sync.wait_ge(prod_ready, len(UNITS))
                                sync.wait_ge(qk_ready, NH)
                                sync.wait_ge(rows_stored, stored_rows(8))
                        else:
                            sync.wait_ge(pv_done, 2 * i + h - 1)
                        for g, (_, dil) in enumerate(GROUPS):
                            src = caches[g].rearrange("b t (m r) h d -> b t m r (h d)", r=dil)[bass.ds(2 * i + h, 1), 1, :, 0, :]
                            sync.dma_start(vu[3 * h + g][:], src.rearrange("o m c -> (o m) c")).then_inc(vu_loaded[h], 16)
                    if j in (3, 7):
                        h = j // 4
                        if below(i, 1):
                            if h == 0:
                                sync.wait_ge(att_done, NSLOT)
                        else:
                            sync.wait_ge(y_done, 2 * i + h - 1)
                        src = ssm_tab[bass.ds(2 * i + h, 1)].rearrange("o p c -> (o p) c")
                        sync.dma_start(tab[h][:], src).then_inc(tab_loaded[h], 16)
            loop(sync, PH["gates_b"], gates_b, 1)

            def attn_branch(i, ph=PH["attn_branch"]):
                for g in range(4):
                    put(ph, i, g, cols(A["w_attn_branch"][0], 0, 512, (4 * i + g) * 256))
            loop(sync, PH["attn_branch"], attn_branch, 2)
            sync.wait_ge(y_read, SC)
            for s in range(3):
                for jj in range(4):
                    sync.dma_start(yt_v[32 * jj:32 * jj + 32, :, s * NB:(s + 1) * NB],
                                   u4[32 * s:32 * s + 32, jj::4, NS:NS + NB]).then_inc(yt_loaded, 16)

            def glu(i, ph=PH["glu"]):
                for j in range(4):
                    put(ph, i, j, cols(A["glu_w"][0], 512 * (j % 2), 512, (2 * i + j // 2) * 256))
            loop(sync, PH["glu"], glu, 2)

            def ssm_branch(i, ph=PH["ssm_branch"]):
                for j in range(4):
                    put(ph, i, j, cols(A["w_ssm_branch"][0], 512 * (j % 2), 512, (2 * i + j // 2) * 256))
            loop(sync, PH["ssm_branch"], ssm_branch)

            def w_out(i, ph=PH["w_out"]):
                for j in range(8):
                    put(ph, i, j, cols(A["w_out"][0], 512 * (j % 4), 512, (2 * i + j // 4) * 256))
            loop(sync, PH["w_out"], w_out)
            ffn(1)
            for t in range(3):
                n = P if t < 2 else NS
                dst = O["y_p"][0, t * P:(t + 1) * P, :] if t < 2 else O["y_s"][:, 0, :]
                sync.wait_ge(yrow_ready, KD // 2)
                sync.dma_start(dst, y_rows[0:n, t, :]).then_inc(stored, 16)
            n_stored[0] += 48
            sync.wait_ge(stored, n_stored[0])

        @block.scalar
        def _(act):
            def split_hi(ph, i, j):
                slot, turn, n = ph.slab(i, j)
                if isinstance(n, int) and n >= TOTAL:
                    return
                act.wait_ge(slab_loaded[slot], 16 * turn + 16)
                if not below(n, RING):
                    act.wait_ge(slab_used, n - (RING - 1))
                act.activation(w_hi[:, slot], raw[:, slot], ACT.Copy).then_inc(hi_ready, 1)

            def split_x(c, cnt, gain0, ready, count):
                act.wait_ge(ready, count)
                if not below(cnt, 1):
                    act.wait_ge(ssq_ready, cnt)
                act.activation(sq_v[:], x_t[:, bass.ds(2 * c, 2), :], ACT.Square).then_inc(sq_ready, 1)
                for u in range(2):
                    ins = act.activation(xg_hi[:, bass.ds(2 * c + u, 1), :], x_t[:, bass.ds(2 * c + u, 1), :],
                                         ACT.Copy, scale=vec[:, bass.ds(gain0 + 2 * c + u, 1)])
                ins.then_inc(xhi_ready, 1)

            def root(r):
                act.wait_ge(mean_ready, r + 1)
                act.activation(sd[:], pb[:, 0, 0:T], ACT.Sqrt, bias=eps_t).then_inc(sd_ready, 1)

            def ssm_params(i, j):
                if i == 0 and j == 5:
                    act.wait_ge(prm_t, 1)
                    act.activation(prm[:], pb[:, 1, 0:P], ACT.Copy).then_inc(prm_ready, 1)
                    act.activation(x0_t[:].rearrange("p a b t -> p (a b t)"), pb[:, 2, :], ACT.Copy).then_inc(prm_ready, 1)
                    act.wait_ge(prm_ready, 2)
                    act.activation(scr[:, 0], prm[:, 2 * NTILE:3 * NTILE], ACT.Exp).then_inc(dt_ready, 1)
                if i == 1 and j == 1:
                    act.wait_ge(angles_ready, 1)
                    act.activation(scr[:, 8], scr[:, 1], ACT.Exp).then_inc(trig_ready, 1)
                    act.activation(scr[:, 9:11], scr[:, 3:5], ACT.Sin).then_inc(trig_ready, 1)

            def ffn(f):
                names = [f"up{f}0", f"down{f}0", f"up{f}1", f"down{f}1", f"up{f}2", f"single{f}", f"down{f}2"]
                for nm in names:
                    ph = PH[nm]
                    if nm.startswith("down"):
                        kts = pair_slabs(nm)
                        def down(i):
                            for j in range(ph.slabs):
                                split_hi(ph, i, j + LEAD)
                                if nm in NORM_AFTER and j % len(kts) == len(kts) - 1:
                                    r, g = NORM_AFTER[nm], j // len(kts)
                                    c = i * ph.groups + g
                                    split_x(c, 8 * r + c, V_NORM[r], evacuated, ph.group(i, g) + 1)
                        loop(act, ph, down, ph.iters if nm == LAST else 0)
                        continue
                    w = 1 if nm.startswith("single") else 2
                    half = ph.slabs // 2
                    def up(i):
                        h, tile0 = HID0[nm] + i, 10 if w == 1 else 2 * i
                        for j in range(ph.slabs):
                            split_hi(ph, i, j + LEAD)
                            if j == 1 and below(i, 1) and nm in ("up00", "up10"):
                                root(2 * f)
                            if below(i, 2) and nm == "up00":
                                ssm_params(i, j)
                            if j == half - 1:
                                act.wait_ge(gate_ready, h + 1)
                                act.activation(silu_v[:, 0:w], gate_v[:, 0:w], ACT.Silu).then_inc(silu_ready, 1)
                            if nm == "up01" and j == 4:
                                act.wait_ge(bb_done, i + 1)
                                if not below(i, 1):
                                    act.wait_ge(tab_stored, 16 * SC + 48 * i)
                                    act.wait_ge(k_done, i)
                                act.activation(bb_t[:], pb[:, 0:2, :].rearrange("p a b -> p (a b)"), ACT.Copy)
                                act.activation(c_t[:].rearrange("p a b c -> p (a b c)"), pb[:, 2, 0:256], ACT.Copy).then_inc(bbt_ready, 1)
                            if j == ph.slabs - 1:
                                act.wait_ge(hid_ready, h + 1)
                                act.activation(act_hi[:, bass.ds(tile0, w), :], hid_v[:, 0:w], ACT.Copy).then_inc(acthi_ready, 1)
                    loop(act, ph, up, 2 if nm == "up00" else 1 if nm in ("up10", "up01") else 0)

            def head_sq_root(x, j):
                if j == 1 and 1 <= x <= NH:
                    act.wait_ge(stat_done, x)
                    if x >= 2:
                        act.wait_ge(t1_ready, 2 * (x - 1))
                    act.activation(head_sd[:], pb[:, 0:2, 0:T], ACT.Sqrt, bias=eps_t).then_inc(head_sd_ready, 1)
                if j == 3 and x < NH:
                    act.wait_ge(evacuated, pair_group(x) + 1)
                    if x:
                        act.wait_ge(stat_done, x)
                    act.activation(sq_v[:], gate_v[:], ACT.Square).then_inc(head_sq, 1)

            def head_rows(x, j):
                e = x - 2 if j == 0 else x - 1
                if not (j == 0 and 0 <= e < 12 or j == 2 and 12 <= e < 18):
                    return
                r, h = e // 2, e % 2
                act.wait_ge(heads_t, e + 1)
                if h == 0 and r:
                    act.wait_ge(rows_stored, stored_rows(r - 1))
                if e in range(6, 12):
                    act.activation(k_rows[:, :, 256 * h:256 * h + 256], pb[:, 2, :].rearrange("p (a b) -> p a b", a=2), ACT.Copy)
                if e >= 12:
                    act.activation(v_tok[:, :, 256 * (e - 12):256 * (e - 11)], pb[:, 2, :].rearrange("p (a b) -> p a b", a=2), ACT.Copy)
                act.activation(s_rows[0:NS, 256 * h:256 * h + 256], pb[0:NS, 3, 0:256], ACT.Copy).then_inc(rows_ready, 1)

            def attention(i, j):
                h = i // 2
                if i % 2 == 0 and j == 1:
                    act.wait_ge(nmax_ready, h + 1)
                    act.activation(probs[:, 0:NG * P], probs[:, 0:NG * P], ACT.Exp, bias=stat[:, 2:3], accum_out=stat[:, 4:5])
                    act.activation(probs[:, NG * P:], probs[:, NG * P:], ACT.Exp, bias=stat[:, 3:4], accum_out=stat[:, 5:6]).then_inc(exp_ready, 1)
                if i % 2 == 0 and j == 3:
                    act.wait_ge(inv_sum, h + 1)
                    act.activation(probs[:, 0:NG * P], probs[:, 0:NG * P], ACT.Copy, scale=stat[:, 6:7])
                    act.activation(probs[:, NG * P:], probs[:, NG * P:], ACT.Copy, scale=stat[:, 7:8]).then_inc(pn_ready, 1)
                if i % 2 == 1 and j == 1:
                    act.wait_ge(p_t, h + 1)
                    act.activation(probs_t[:, 0:8], pb[:, 0:2, :].rearrange("p a (b c) -> p (a b) c", b=4), ACT.Copy)
                    act.activation(probs_t[:, 8], pb[:, 2, 0:P], ACT.Copy).then_inc(pt_ready, 1)
                if i % 2 == 1 and j == 3:
                    act.wait_ge(att_done, h + 1)
                    act.activation(att_v[:, h, 0:NT], pb[:, 3, 0:NT], ACT.Copy).then_inc(att_read, 1)
                if i == 5 and j == 0:
                    act.wait_ge(dmax_ready, 1)
                    act.activation(dec_p[:], pb[0:32, 3, 0:NG * P + NG], ACT.Exp, bias=stat[0:32, 9:10], scale=SCALE,
                                   accum_out=stat[0:32, 10:11]).then_inc(dexp_ready, 1)

            def gates_b(i, ph=PH["gates_b"]):
                for j in range(8):
                    split_hi(ph, i, j + LEAD)
                    if j in (4, 7):
                        h = 0 if j == 4 else 1
                        k = 2 * i + h
                        act.wait_ge(y_done, k + 1)
                        act.activation(u4[:, bass.ds(4 * k, 4), 0:NS + NB], pb[:, 2, 0:288].rearrange("p (a b) -> p a b", a=4), ACT.Copy)
                        act.activation(x_fin[:, :, bass.ds(4 * k, 4)], xs[:, :, :, NS + NB], ACT.Copy).then_inc(y_read, 1)
                    if j in (1, 4):
                        h = j // 4
                        k = 2 * i + h
                        act.wait_ge(su_done, k + 1)
                        if below(i, 1) and h == 0:
                            act.wait_ge(xs_zero, 1)
                        else:
                            act.wait_ge(scan_ready, 2 * k)
                            act.wait_ge(y_done, k)
                        s_ps = pb[:, 0:2, 0:288].rearrange("p a (t c) -> p a t c", t=4)
                        act.activation(sv[:].rearrange("p a (t c) -> p a t c", t=4), s_ps[:, :, :, 0:NB], ACT.Copy)
                        act.activation(s_new[:, :, bass.ds(4 * k, 4), :], s_ps[:, :, :, NB:NB + NS], ACT.Copy)
                        for ri in range(2):
                            ins = act.activation(xs[:, ri, :, 0:NS], x0_t[:, ri, :, bass.ds(4 * k, 4)].rearrange("p b t -> p t b"), ACT.Copy)
                        ins.then_inc(sv_ready, 1)

            def sigmoid(c, count):
                act.activation(gates[:, bass.ds(c, 2), :], gates[:, bass.ds(c, 2), :], ACT.Sigmoid).then_inc(sig_ready, 1)

            act.wait_ge(const_ready, 1)
            act.wait_ge(vec_ready, 1)
            for c in range(KD // 2):
                split_x(c, c, V_NORM[0], x_ready, c + 1)
                if c < LEAD:
                    split_hi(PH["up00"], 0, c)
            ffn(0)
            for name in ("u", "q", "k", "v", "gates_a"):
                ph = PH[name]
                for i in range(ph.iters):
                    x = XQ.get(name, -99) + i
                    for j in range(4):
                        split_hi(ph, i, j + LEAD)
                        if name == "u" and i == 0 and j == 1:
                            root(1)
                        if name != "u":
                            head_sq_root(x, j)
                            head_rows(x, j)
                        if name == "gates_a":
                            attention(i, j)
            loop(act, PH["gates_b"], gates_b, 1)
            act.wait_ge(pv_read, NS)
            act.wait_ge(scan_ready, 2 * SC)
            act.activation(att_hi[:], att_v[:], ACT.Copy).then_inc(att_hi_ready, 1)
            act.wait_ge(evacuated, PH["attn_branch"].group0)
            for i in range(2):
                for g in range(4):
                    split_hi(PH["attn_branch"], i, g + LEAD)
                    sigmoid(2 * (4 * i + g), 1)
            act.wait_ge(yt_loaded, 16 * 12)
            act.wait_ge(yl_loaded, 16 * 8)
            act.wait_ge(slab_used, q_end("gates_b"))
            for k in range(2):
                act.activation(zs_v[:, 4 * k:4 * k + 4], yt_v[:, 4 * k:4 * k + 4], ACT.Gelu_apprx_tanh).then_inc(gelu_ready, 1)
                act.wait_ge(gelu_ready, k + 1)
                act.activation(zs_hi[:, 4 * k:4 * k + 4], zs_v[:, 4 * k:4 * k + 4], ACT.Copy).then_inc(zhi_ready, 1)

            def glu(i, ph=PH["glu"]):
                for j in range(4):
                    split_hi(ph, i, j + LEAD)
                    if j % 2 == 1:
                        g = j // 2
                        c = 2 * i + g
                        act.wait_ge(slab_used, ph.slab(i, j)[2] + 1)
                        act.wait_ge(evacuated, ph.group(i, g))
                        for u in range(2):
                            ins = act.activation(gate_v[:, u], pa[:, 2 * ph.banks(i, g) + u, 0:T], ACT.Sigmoid,
                                                 bias=vec[:, V_GLU + 2 * c + u:V_GLU + 2 * c + u + 1])
                        ins.then_inc(sgl_ready, 1)
                        act.wait_ge(evacuated, ph.group(i, g) + 1)
                        act.activation(s_hi[:, 2 * c:2 * c + 2], up_v[:], ACT.Copy).then_inc(shi_ready, 1)
                    if i == 1 and j == 0:
                        act.wait_ge(st_t, 1)
                        act.activation(st_rows[:, 0:4, :], pb[:, 0, :].rearrange("p (a b) -> p a b", a=4), ACT.Copy)
                        act.activation(st_rows[0:32, 4:6, :], pb[0:32, 1, 0:256].rearrange("p (a b) -> p a b", a=2), ACT.Copy).then_inc(st_rows_ready, 1)
            loop(act, PH["glu"], glu, 2)

            def ssm_branch(i, ph=PH["ssm_branch"]):
                for j in range(4):
                    split_hi(ph, i, j + LEAD)
                    if j % 2 == 0:
                        sigmoid(KD + 2 * (2 * i + j // 2), 1)
                    else:
                        c = 2 * i + j // 2
                        act.wait_ge(m_ready, c + 1)
                        act.activation(act_hi[:, bass.ds(2 * c, 2), :], hid_v[:], ACT.Copy).then_inc(acthi_ready, 1)
            loop(act, PH["ssm_branch"], ssm_branch)

            def w_out(i, ph=PH["w_out"]):
                for j in range(8):
                    split_hi(ph, i, j + LEAD)
                    if j % 4 == 3:
                        c = 2 * i + j // 4
                        split_x(c, 16 + c, V_NORM[2], evacuated, ph.group(i, j // 4) + 1)
            loop(act, PH["w_out"], w_out)
            ffn(1)

        @block.vector
        def _(dve):
            def split_lo(ph, i, j):
                slot, turn, n = ph.slab(i, j)
                if isinstance(n, int) and n >= TOTAL:
                    return
                dve.wait_ge(hi_ready, n + 1)
                dve.tensor_tensor(w_lo[:, slot], raw[:, slot], w_hi[:, slot].bitcast(f32), ALU.subtract).then_inc(lo_ready, 1)

            def split_x(c, cnt, gain0):
                dve.wait_ge(xhi_ready, cnt + 1)
                for u in range(2):
                    k = 2 * c + u
                    ins = dve.scalar_tensor_tensor(xg_lo[:, bass.ds(k, 1), :], x_t[:, bass.ds(k, 1), :],
                                                   vec[:, bass.ds(gain0 + k, 1)], xg_hi[:, bass.ds(k, 1), :].bitcast(f32),
                                                   ALU.mult, ALU.subtract)
                ins.then_inc(xlo_ready, 1)

            def times_rstd(out, ph, i, g, j, w=2):
                b = 2 * ph.banks(i, g)
                dve.wait_ge(slab_used, ph.slab(i, j)[2] + 1)
                return dve.tensor_tensor(out, pa[:, b:b + w, 0:T], rstd[:, None, :].to_broadcast([P, w, T]), ALU.mult)

            def root(r):
                dve.wait_ge(sd_ready, r + 1)
                dve.reciprocal(rstd[:], sd[:]).then_inc(rstd_ready, 1)
                dve.wait_ge(rstd_ready, r + 1)

            def residual(ph, i, g, j, scale):
                c = i * ph.groups + g
                b = 2 * ph.banks(i, g)
                dve.wait_ge(slab_used, ph.slab(i, j)[2] + 1)
                dve.scalar_tensor_tensor(x_t[:, bass.ds(2 * c, 2), :], pa[:, b:b + 2, 0:T], scale,
                                         x_t[:, bass.ds(2 * c, 2), :], ALU.mult, ALU.add).then_inc(evacuated, 1)
                return c

            def ssm_table(i, j):
                if j == 5:
                    dve.wait_ge(bbt_ready, i + 1)
                    if not below(i, 1):
                        dve.wait_ge(tab_stored, 16 * SC + 48 * i)
                        dve.wait_ge(k_done, i)
                    def lags(k):
                        return ca_tmp[:, k].rearrange("p t (n f) -> p t n f", n=LAGS)
                    def c_of(ri):
                        return c_t[:, ri, :, None, :].to_broadcast([P, 4, LAGS, 32])
                    def pow_of(t):
                        return t[:, bass.ds(4 * i, 4), :, None].to_broadcast([P, 4, LAGS, 32])
                    for ri, (p0, p1) in enumerate(((pw[:, 0], pw[:, 1]), (npowi, pw[:, 0]))):
                        if not (below(i, 1) and ri == 0):
                            dve.wait_ge(ca_ready, 2 * i + ri)
                        dve.tensor_tensor(lags(0), c_of(0), pow_of(p0), ALU.mult).then_inc(ca_step, 1)
                        dve.tensor_tensor(lags(1), c_of(1), pow_of(p1), ALU.mult).then_inc(ca_step, 1)
                        dve.wait_ge(ca_step, 4 * i + 2 * ri + 2)
                        dve.tensor_tensor(ca5[:, :, ri, :], ca_tmp[:, 0], ca_tmp[:, 1], ALU.subtract).then_inc(ca_ready, 1)
                if j == 7:
                    dve.wait_ge(k_done, i + 1)
                    for s in range(STEP):
                        dve.tensor_copy(kbig[32 * s:32 * s + 32, :, 32 * s:P],
                                        pb[0:32, 3, :].rearrange("p (t c) -> p t c", t=4)[:, :, 0:P - 32 * s]).then_inc(k_step, 1)
                    dve.wait_ge(k_step, 4 * i + 4)
                    for t in range(4):
                        ins = dve.scalar_tensor_tensor(kbig[:, t, :], ident[:], prm[:, bass.ds(3 * NTILE + 4 * i + t, 1)],
                                                       kbig[:, t, :], ALU.mult, ALU.add)
                    ins.then_inc(kbig_ready, 1)

            def ffn(f):
                for nm in [f"up{f}0", f"down{f}0", f"up{f}1", f"down{f}1", f"up{f}2", f"single{f}", f"down{f}2"]:
                    ph = PH[nm]
                    if nm.startswith("down"):
                        kts = pair_slabs(nm)
                        def down(i):
                            for j in range(ph.slabs):
                                split_lo(ph, i, j + LEAD)
                                if j % len(kts) == len(kts) - 1:
                                    c = residual(ph, i, j // len(kts), j, 0.5)
                                    if nm in NORM_AFTER:
                                        split_x(c, 8 * NORM_AFTER[nm] + c, V_NORM[NORM_AFTER[nm]])
                        loop(dve, ph, down, ph.iters if nm == LAST else 0)
                        continue
                    w = 1 if nm.startswith("single") else 2
                    half = ph.slabs // 2
                    def up(i):
                        h, a, tile0 = HID0[nm] + i, ACT0[nm] + i, 10 if w == 1 else 2 * i
                        for j in range(ph.slabs):
                            split_lo(ph, i, j + LEAD)
                            if j == 1 and below(i, 1) and nm in ("up00", "up10"):
                                root(2 * f)
                            if nm == "up00" and below(i, 1) and j == 7:
                                dve.wait_ge(den_ready, 1)
                                dve.reciprocal(scr[:, 12], scr[:, 11]).then_inc(inv_ready, 1)
                            if nm == "up01":
                                ssm_table(i, j)
                            if j == half - 1:
                                b = 2 * ph.banks(i, 0)
                                dve.wait_ge(slab_used, ph.slab(i, j)[2] + 1)
                                dve.tensor_tensor(gate_v[:, 0:w], pa[:, b:b + w, 0:T], rstd[:, None, :].to_broadcast([P, w, T]),
                                                  ALU.mult).then_inc(gate_ready, 1)
                                dve.wait_ge(gate_ready, h + 1)
                                dve.sem_inc(evacuated, 1)
                            if j == ph.slabs - 1:
                                times_rstd(up_v[:, 0:w], ph, i, 1, j, w).then_inc(evacuated, 1)
                                dve.wait_ge(evacuated, ph.group(i, 1) + 1)
                                dve.wait_ge(silu_ready, h + 1)
                                dve.tensor_tensor(hid_v[:, 0:w], silu_v[:, 0:w], up_v[:, 0:w], ALU.mult).then_inc(hid_ready, 1)
                                dve.wait_ge(acthi_ready, a + 1)
                                dve.tensor_tensor(act_lo[:, bass.ds(tile0, w), :], hid_v[:, 0:w],
                                                  act_hi[:, bass.ds(tile0, w), :].bitcast(f32), ALU.subtract).then_inc(actlo_ready, 1)
                    loop(dve, ph, up, 2 if nm == "up00" else 1 if nm in ("up10", "up01") else 0)

            def permuted(ap):
                return ap[:, :, 0:NT].rearrange("p u (c s) -> p u s c", s=STEP)

            def u_out(ph, i):
                b = 2 * ph.banks(i, 0)
                dve.wait_ge(slab_used, ph.slab(i, 3)[2] + 1)
                if i == 0:
                    dve.wait_ge(tab_stored, 16 * 4 * SC)
                dst = u_t[:, 2 * i:2 * i + 2, 0:NT].rearrange("p u (s c) -> p u s c", s=STEP)
                dve.tensor_tensor(dst, permuted(pa[:, b:b + 2, :]),
                                  rstd[:, None, 0:NT].to_broadcast([P, 2, NT]).rearrange("p u (c s) -> p u s c", s=STEP), ALU.mult)
                dve.tensor_tensor(u_t[:, 2 * i:2 * i + 2, NT:T], pa[:, b:b + 2, NT:T],
                                  rstd[:, None, NT:T].to_broadcast([P, 2, NS]), ALU.mult).then_inc(u_ready, 1)
                dve.wait_ge(u_ready, i + 1)
                dve.sem_inc(evacuated, 1)

            def head(x):
                dve.wait_ge(head_sd_ready, x + 1)
                dve.reciprocal(head_sd[:], head_sd[:]).then_inc(head_inv, 1)
                dve.wait_ge(head_inv, x + 1)
                if x:
                    dve.wait_ge(qk_ready, x)
                for u in range(2):
                    dve.scalar_tensor_tensor(up_v[:, u], gate_v[:, u], vec[:, V_HEAD + 2 * x + u:V_HEAD + 2 * x + u + 1],
                                             head_sd[:, u], ALU.mult, ALU.mult).then_inc(t1_ready, 1)
                dve.wait_ge(t1_ready, 2 * x + 2)
                if x == 0:
                    dve.wait_ge(const_loaded, 32)
                for to, frm in ((0, 64), (64, 0)):
                    dve.tensor_tensor(silu_v[to:to + 64], up_v[frm:frm + 64],
                                      cs[frm:frm + 64, 1, None, :].to_broadcast([64, 2, T]), ALU.mult).then_inc(rot_ready, 1)

            def attention(i, j):
                h = i // 2
                if i % 2 == 0 and j == 0:
                    dve.wait_ge(s_done, h + 1)
                    if h:
                        dve.wait_ge(p_t, h)
                    n0 = NG * P
                    dve.scalar_tensor_tensor(probs[:, 0:n0], pb[:, 0, 0:n0], SCALE, masks[:, 0:n0], ALU.mult, ALU.add)
                    dve.scalar_tensor_tensor(probs[:, n0:], pb[:, 1:3, :].rearrange("p a b -> p (a b)")[:, 0:NG * NT], SCALE,
                                             masks[:, n0:], ALU.mult, ALU.add).then_inc(sm_ready, 1)
                    dve.wait_ge(sm_ready, h + 1)
                    dve.tensor_reduce(stat[:, 0:1], probs[:, 0:n0], AX.X, ALU.max)
                    dve.tensor_reduce(stat[:, 1:2], probs[:, n0:], AX.X, ALU.max).then_inc(sm_step, 1)
                    dve.wait_ge(sm_step, h + 1)
                    dve.tensor_scalar(stat[:, 2:4], stat[:, 0:2], -1.0, None, ALU.mult).then_inc(nmax_ready, 1)
                if i % 2 == 0 and j == 2:
                    dve.wait_ge(exp_ready, h + 1)
                    dve.reciprocal(stat[:, 6:8], stat[:, 4:6]).then_inc(inv_sum, 1)

            dstep = Chain(dve, dec_step)

            def decode(i, j):
                n = NG * P
                if (i, j) == (4, 3):
                    dve.wait_ge(ds_done, 1)
                    dstep(dve.tensor_reduce(stat[0:32, 8:9], pb[0:32, 3, 0:n + NG], AX.X, ALU.max))
                    dve.tensor_scalar(stat[0:32, 9:10], stat[0:32, 8:9], -SCALE, None, ALU.mult).then_inc(dmax_ready, 1)
                if (i, j) == (5, 1):
                    dve.wait_ge(dexp_ready, 1)
                    dstep(dve.reciprocal(stat[0:32, 11:12], stat[0:32, 10:11]))
                    dstep(dve.tensor_scalar(dec_p[:], dec_p[:], stat[0:32, 11:12], None, ALU.mult))
                    for g in range(NG):
                        ins = dve.tensor_scalar(dec_diag[:, g, :], ident[0:32, 0:32], dec_p[:, n + g:n + g + 1], None, ALU.mult)
                    ins.then_inc(diag_ready, 1)
                if (i, j) == (6, 3):
                    dve.wait_ge(dt_done, 1)
                    dve.wait_ge(v_new_ready, 6)
                    dve.tensor_copy(pt_dec[:].rearrange("p a b -> p (a b)"), pb[:, 3, 0:96])
                    dstep(dve.tensor_tensor(att_new[:].rearrange("p g (b h) -> p g b h", b=NS),
                                            pb[:, 3, P:P + 96].rearrange("p (g b h) -> p g b h", g=NG, b=NS),
                                            v_new[:].rearrange("p (g h) b -> p g b h", g=NG), ALU.mult))
                    dstep(dve.tensor_tensor(att_new[:, 0], att_new[:, 0], att_new[:, 1], ALU.add))
                    dve.tensor_tensor(att_new[:, 0], att_new[:, 0], att_new[:, 2], ALU.add).then_inc(dec_ready, 1)

            def gates_b(i, ph=PH["gates_b"]):
                for j in range(8):
                    split_lo(ph, i, j + LEAD)
                    if j in (1, 4):
                        h = j // 4
                        k = 2 * i + h
                        E, M = tab[h][:, E0:M0].rearrange("p (a c) -> p a c", a=2), tab[h][:, M0:TB]
                        dve.wait_ge(sv_ready, k + 1)
                        if not (below(i, 1) and h == 0):
                            dve.wait_ge(xi_ready, k)
                        dve.tensor_tensor(d_tmp[:, 0], sv[:, 1], E[:, 0], ALU.mult).then_inc(zi_step, 1)
                        dve.tensor_tensor(d_tmp[:, 1], sv[:, 0], E[:, 1], ALU.mult).then_inc(zi_step, 1)
                        dve.wait_ge(zi_step, 5 * k + 2)
                        dve.tensor_tensor(z_in[:, 1], d_tmp[:, 0], d_tmp[:, 1], ALU.subtract).then_inc(zi_step, 1)
                        dve.wait_ge(zi_step, 5 * k + 3)
                        if not (below(i, 1) and h == 0):
                            dve.wait_ge(xr_ready, k)
                        dve.tensor_tensor_scan(z_out[:, 1], M, z_in[:, 1], 0.0, ALU.mult, ALU.add).then_inc(scan_ready, 1)
                        dve.wait_ge(zr_ready, k + 1)
                        dve.tensor_tensor_scan(z_out[:, 0], M, z_in[:, 0], 0.0, ALU.mult, ALU.add).then_inc(scan_ready, 1)
                    if j in (2, 5):
                        h = j // 4
                        k = 2 * i + h
                        E = tab[h][:, E0:M0].rearrange("p (a c) -> p a c", a=2)
                        dve.wait_ge(scan_ready, 2 * k + 2)
                        dve.tensor_tensor(d_tmp[:, 0], z_out[:, 0], E[:, 1], ALU.mult).then_inc(zi_step, 1)
                        dve.tensor_tensor(d_tmp[:, 1], z_out[:, 1], E[:, 0], ALU.mult).then_inc(zi_step, 1)
                        dve.wait_ge(zi_step, 5 * k + 5)
                        if below(i, 1) and h == 0:
                            dve.wait_ge(xs_zero, 1)
                        else:
                            dve.wait_ge(y_read, k)
                        dve.tensor_tensor(xs[:, 1, :, NS + 1:NS + 1 + NB], d_tmp[:, 0].rearrange("p (t c) -> p t c", t=4),
                                          d_tmp[:, 1].rearrange("p (t c) -> p t c", t=4), ALU.add).then_inc(xi_ready, 1)
                    if j in (2, 6):
                        h = j // 4
                        k = 2 * i + h
                        dve.wait_ge(pv_done, k + 1)
                        dve.tensor_tensor(att_v[:, :, bass.ds(NT + k, 1)], pb[:, 3, 0:NSLOT, None],
                                          att_new[:, 0, bass.ds(NSLOT * k, NSLOT), None], ALU.add).then_inc(pv_read, 1)
                    if j % 4 == 3:
                        g = j // 4
                        if below(i, 1) and g == 0:
                            dve.wait_ge(att_done, NSLOT)
                        times_rstd(gates[:, bass.ds(KD + 4 * i + 2 * g, 2), :], ph, i, g, j).then_inc(evacuated, 1)

            dve.memset(eps_t, EPS)
            dve.memset(head_w[:], 1.0 / HD)
            dve.memset(ones[:], 1.0)
            dve.memset(mean_w[:], 1.0 / D).then_inc(const_ready, 1)
            dve.wait_ge(vec_t, 1)
            dve.tensor_copy(vec[:, 0:NV], pb[:, 3, 0:NV]).then_inc(vec_ready, 1)
            dve.wait_ge(vec_ready, 1)
            for c in range(KD // 2):
                dve.wait_ge(rows_t, c + 1)
                dve.tensor_copy(x_t[:, 2 * c:2 * c + 2, :], pb[:, 2 * (c % 2):2 * (c % 2) + 2, 0:T]).then_inc(x_ready, 1)
                split_x(c, c, V_NORM[0])
                if c < LEAD:
                    split_lo(PH["up00"], 0, c)
                if c == 3:
                    dve.wait_ge(dt_loaded, 16)
                    dve.tensor_copy(prm_rows[64:96, :].rearrange("p (g s) -> p g s", g=2),
                                    log_dt[64:96, :, None].to_broadcast([32, 2, 64])).then_inc(dt_rows, 1)
            ffn(0)
            for name in ("u", "q", "k", "v", "gates_a"):
                ph = PH[name]
                for i in range(ph.iters):
                    x = XQ.get(name, -99) + i
                    for j in range(4):
                        split_lo(ph, i, j + LEAD)
                        if name == "u" and i == 0 and j == 1:
                            root(1)
                        if name == "gates_a":
                            attention(i, j)
                            decode(i, j)
                        if j == 2 and 1 <= x <= NH:
                            head(x - 1)
                        n = ph.slab0 + 4 * i + j - PH["v"].slab0 - UNIT_USE
                        if 0 <= n < len(UNITS):
                            g, b = UNITS[n]
                            dve.wait_ge(prod_ready, n + 1)
                            dve.tensor_reduce(sc_dec[:, g, b, :], prod[n % 2][:], AX.X, ALU.add).then_inc(sc_ready, 1)
                        if j == 3 and name == "u":
                            u_out(ph, i)
                        elif j == 3 and name == "gates_a":
                            times_rstd(gates[:, 2 * i:2 * i + 2, :], ph, i, 0, j).then_inc(evacuated, 1)
                        elif j == 3:
                            if 1 <= x <= NH:
                                dve.wait_ge(t1_ready, 2 * x)
                            elif x > NH:
                                dve.wait_ge(heads_t, x)
                            times_rstd(gate_v[:], ph, i, 0, j).then_inc(evacuated, 1)
                            if name == "v":
                                dve.wait_ge(evacuated, pair_group(x) + 1)
                                dve.tensor_copy(v_new[:, 2 * i:2 * i + 2, :], gate_v[:, :, NT:T]).then_inc(v_new_ready, 1)
            loop(dve, PH["gates_b"], gates_b, 1)
            dve.wait_ge(att_hi_ready, 1)
            dve.tensor_tensor(att_lo[:], att_v[:], att_hi[:].bitcast(f32), ALU.subtract).then_inc(att_lo_ready, 1)
            ph = PH["attn_branch"]
            for i in range(2):
                for g in range(4):
                    split_lo(ph, i, g + LEAD)
                    c, b = 4 * i + g, 2 * ph.banks(i, g)
                    dve.wait_ge(slab_used, ph.slab(i, g)[2] + 1)
                    dve.wait_ge(sig_ready, c + 1)
                    dve.tensor_tensor(gates[:, 2 * c:2 * c + 2, :], pa[:, b:b + 2, 0:T], gates[:, 2 * c:2 * c + 2, :],
                                      ALU.mult).then_inc(evacuated, 1)
            for k in range(2):
                dve.wait_ge(zhi_ready, k + 1)
                dve.tensor_tensor(zs_lo[:, 4 * k:4 * k + 4], zs_v[:, 4 * k:4 * k + 4], zs_hi[:, 4 * k:4 * k + 4].bitcast(f32),
                                  ALU.subtract).then_inc(zlo_ready, 1)
            ph = PH["glu"]
            for i in range(2):
                for j in range(4):
                    split_lo(ph, i, j + LEAD)
                    if j % 2 == 1:
                        c = 2 * i + j // 2
                        dve.wait_ge(sgl_ready, c + 1)
                        if c:
                            dve.wait_ge(slo_ready, c)
                        dve.tensor_tensor(up_v[:], zs_v[:, 2 * c:2 * c + 2], gate_v[:], ALU.mult).then_inc(evacuated, 1)
                        dve.wait_ge(shi_ready, c + 1)
                        dve.tensor_tensor(s_lo[:, 2 * c:2 * c + 2], up_v[:], s_hi[:, 2 * c:2 * c + 2].bitcast(f32),
                                          ALU.subtract).then_inc(slo_ready, 1)

            def ssm_branch(i, ph=PH["ssm_branch"]):
                for j in range(4):
                    split_lo(ph, i, j + LEAD)
                    if j % 2 == 1:
                        c, b = 2 * i + j // 2, 2 * ph.banks(i, j // 2)
                        sig = gates[:, bass.ds(KD + 2 * c, 2), :]
                        dve.wait_ge(slab_used, ph.slab(i, j)[2] + 1)
                        dve.wait_ge(sig_ready, 8 + c + 1)
                        if not below(c, 1):
                            dve.wait_ge(m_ready, c)
                        dve.tensor_tensor(up_v[:, :, 0:NT].rearrange("p u (c s) -> p u s c", s=STEP),
                                          pa[:, b:b + 2, 0:NT].rearrange("p u (s c) -> p u s c", s=STEP),
                                          sig[:, :, 0:NT].rearrange("p u (c s) -> p u s c", s=STEP), ALU.mult).then_inc(prod_s, 1)
                        dve.tensor_tensor(up_v[:, :, NT:T], pa[:, b:b + 2, NT:T], sig[:, :, NT:T], ALU.mult).then_inc(evacuated, 1)
                        dve.wait_ge(evacuated, ph.group(i, j // 2) + 1)
                        dve.wait_ge(prod_s, c + 1)
                        if not below(c, 1):
                            dve.wait_ge(acthi_ready, ACT0["ssm_branch"] + c)
                        dve.tensor_tensor(hid_v[:], up_v[:], gates[:, bass.ds(2 * c, 2), :], ALU.add).then_inc(m_ready, 1)
                        dve.wait_ge(acthi_ready, ACT0["ssm_branch"] + c + 1)
                        dve.tensor_tensor(act_lo[:, bass.ds(2 * c, 2), :], hid_v[:], act_hi[:, bass.ds(2 * c, 2), :].bitcast(f32),
                                          ALU.subtract).then_inc(actlo_ready, 1)
            loop(dve, PH["ssm_branch"], ssm_branch)
            dve.wait_ge(x_back, 16)

            def w_out(i, ph=PH["w_out"]):
                for j in range(8):
                    split_lo(ph, i, j + LEAD)
                    if j % 4 == 3:
                        c = residual(ph, i, j // 4, j, 1.0)
                        split_x(c, 16 + c, V_NORM[2])
            loop(dve, PH["w_out"], w_out)
            ffn(1)
            for c in range(KD // 2):
                dve.wait_ge(yt_ready, c + 1)
                for t in range(3):
                    n = P if t < 2 else NS
                    ins = dve.tensor_copy(y_rows[0:n, t, 256 * c:256 * c + 256], pb[0:n, t, 0:256])
                ins.then_inc(yrow_ready, 1)

        @block.tensor
        def _(pe):
            def tile_products(out, slot, kk, c, hi, lo, first, last, m0=None):
                if m0 is None:
                    m0 = P * c
                wh, wl = w_hi[:, slot, kk, m0:m0 + P], w_lo[:, slot, kk, m0:m0 + P]
                pe.matmul(out, wh, hi, start=first, stop=False)
                pe.matmul(out, wh, lo, start=False, stop=False)
                return pe.matmul(out, wl, hi, start=False, stop=last)

            def slab_products(ph, i, j, g, hi, lo, k0, kt, first, last, w=2):
                slot, turn, n = ph.slab(i, j)
                pe.wait_ge(lo_ready, n + 1)
                b = 2 * ph.banks(i, g)
                for c in range(2):
                    for kk in range(kt):
                        ins = tile_products(pa[:, b + c, 0:T], slot, kk, c, hi[:, k0 + kk, :], lo[:, k0 + kk, :],
                                            first and kk == 0, last and kk == kt - 1)
                ins.then_inc(slab_used, 1)

            def open_group(ph, i, g):
                q = ph.group(i, g)
                if not below(q, 2):
                    pe.wait_ge(evacuated, q - 1)

            def mean_square(r):
                pe.wait_ge(ssq_ready, 8 * (r + 1))
                pe.matmul(pb[:, 0, 0:T], mean_w[:], ssq[:, 0, :], start=True, stop=False)
                pe.matmul(pb[:, 0, 0:T], mean_w[:], ssq[:, 1, :], start=False, stop=True).then_inc(mean_ready, 1)

            def ssm_setup(i, j):
                if i == 0 and j == 4:
                    pe.wait_ge(par_loaded, 16 * 13)
                    pe.wait_ge(dt_rows, 1)
                    pe.transpose(pb[:, 1, 0:P], prm_rows[:], ident[:])
                    for ri in range(2):
                        for blk in range(2):
                            ins = pe.transpose(pb[:, 2, (2 * ri + blk) * P:(2 * ri + blk + 1) * P], x0_rows[:, ri, blk, :], ident[:])
                    ins.then_inc(prm_t, 1)

            def ssm_table(i, j):
                if j == 3:
                    pe.wait_ge(pre_ready, i + 1)
                    if not below(i, 1):
                        pe.wait_ge(bbt_ready, i)
                    for t in range(4):
                        for ri in range(2):
                            m = 2 * t + ri
                            pe.transpose(pb[:, m // 4, (m % 4) * P:(m % 4 + 1) * P], pre[:, ri, t].rearrange("p s g c -> p (s g c)"), ident[:])
                    for ri in range(2):
                        ins = pe.transpose(pb[:, 2, ri * P:(ri + 1) * P], c_exp[:, ri].rearrange("p g s -> p (g s)"), ident[:])
                    ins.then_inc(bb_done, 1)
                if j == 7:
                    pe.wait_ge(ca_ready, 2 * i + 2)
                    if not below(i, 1):
                        pe.wait_ge(kbig_ready, i)
                    for t in range(4):
                        for ri in range(2):
                            ins = pe.matmul(pb[0:32, 3, t * P:(t + 1) * P], pre[:, ri, t, STEP - 1].rearrange("p g c -> p (g c)"),
                                            ca5[:, t, ri, 0:P], start=ri == 0, stop=ri == 1)
                    ins.then_inc(k_done, 1)

            def ffn(f):
                xn = 2 * f
                for nm in [f"up{f}0", f"down{f}0", f"up{f}1", f"down{f}1", f"up{f}2", f"single{f}", f"down{f}2"]:
                    ph = PH[nm]
                    if nm.startswith("down"):
                        kts, up0 = pair_slabs(nm), ACT0["up" + nm[4:]]
                        def down(i):
                            for g in range(ph.groups):
                                open_group(ph, i, g)
                                for s, kt in enumerate(kts):
                                    if g == 0:
                                        pe.wait_ge(actlo_ready, up0 + 2 * s + 2)
                                    slab_products(ph, i, g * len(kts) + s, g, act_hi, act_lo, KS * s, kt, s == 0, s == len(kts) - 1)
                        loop(pe, ph, down)
                    elif nm.startswith("single"):
                        for j in range(4):
                            g, kh = j // 2, j % 2
                            if kh == 0:
                                open_group(ph, 0, g)
                            slot, turn, n = ph.slab(0, j)
                            pe.wait_ge(lo_ready, n + 1)
                            for kk in range(8):
                                k = kh * 8 + kk
                                ins = tile_products(pa[:, 2 * ph.banks(0, g), 0:T], slot, kk // 2, 0, xg_hi[:, k, :], xg_lo[:, k, :],
                                                    k == 0, k == KD - 1, m0=P * (kk % 2))
                            ins.then_inc(slab_used, 1)
                    else:
                        def up(i):
                            for j in range(8):
                                g, s = j // 4, j % 4
                                if s == 0:
                                    open_group(ph, i, g)
                                if g == 0:
                                    pe.wait_ge(xlo_ready, 8 * xn + 2 * s + 2)
                                slab_products(ph, i, j, g, xg_hi, xg_lo, KS * s, KS, s == 0, s == 3)
                                if j == 2 and below(i, 1) and nm in ("up00", "up10"):
                                    mean_square(xn)
                                if nm == "up00" and below(i, 1):
                                    ssm_setup(i, j)
                                if nm == "up01":
                                    ssm_table(i, j)
                        loop(pe, ph, up, 2 if nm == "up00" else 1 if nm in ("up10", "up01") else 0)

            def head_stats(x):
                pe.wait_ge(head_sq, x)
                pe.wait_ge(*((sd_ready, 2) if x == 1 else (head_sd_ready, x - 1)))
                for u in range(2):
                    ins = pe.matmul(pb[:, u, 0:T], head_w[:], sq_v[:, u, :], start=True, stop=True)
                ins.then_inc(stat_done, 1)

            def heads_to_rows(x, j):
                e = x - 2 if j == 0 else x - 1
                if not (j == 0 and 0 <= e < 12 or j == 2 and 12 <= e < 18):
                    return
                if e < 12:
                    pe.wait_ge(qk_ready, e + 1)
                else:
                    pe.wait_ge(evacuated, pair_group(e) + 1)
                if e:
                    pe.wait_ge(rows_ready, e)
                if e == 17:
                    pe.wait_ge(sm_ready, 1)
                for u in range(2):
                    src = qk[:, 2 * e + u, :] if e < 12 else gate_v[:, u, :]
                    if e >= 6:
                        for t in range(2):
                            pe.transpose(pb[:, 2, 256 * t + P * u:256 * t + P * (u + 1)], src[:, t * P:(t + 1) * P], ident[:])
                    ins = pe.transpose(pb[0:NS, 3, P * u:P * (u + 1)], src[:, NT:T], ident[:])
                ins.then_inc(heads_t, 1)

            def attention(i, j):
                h = i // 2
                if i % 2 == 0 and j == 0:
                    pe.wait_ge(qk_ready, 12)
                    pe.wait_ge(*((rows_ready, 17) if h == 0 else (pt_ready, h)))
                    for g in range(NG):
                        q, k = qk[:, NSLOT * g + h, :], qk[:, NH + NSLOT * g + h, :]
                        pe.matmul(pb[:, 0, g * P:(g + 1) * P], q[:, 0:P], k[:, 0:P], start=True, stop=True)
                        ins = pe.matmul(pb[:, 1 + g // 2, (g % 2) * NT:(g % 2 + 1) * NT], q[:, P:NT], k[:, 0:NT], start=True, stop=True)
                    ins.then_inc(s_done, 1)
                if i % 2 == 1 and j == 0:
                    pe.wait_ge(pn_ready, h + 1)
                    if h == 0:
                        pe.wait_ge(rows_ready, 18)
                    for m in range(9):
                        ins = pe.transpose(pb[:, m // 4, (m % 4) * P:(m % 4 + 1) * P], probs[:, m * P:(m + 1) * P], ident[:])
                    ins.then_inc(p_t, 1)
                if i % 2 == 1 and j == 2:
                    pe.wait_ge(pt_ready, h + 1)
                    if h:
                        pe.wait_ge(att_read, h)
                    if h == 3:
                        pe.wait_ge(dec_ready, 1)
                    if h == 2:
                        pe.wait_ge(dexp_ready, 1)
                    for g in range(NG):
                        v0 = (NSLOT * g + h) * HD
                        pe.matmul(pb[:, 3, 0:P], v_tok[:, 0, v0:v0 + HD], probs_t[:, g, :], start=g == 0, stop=g == NG - 1)
                    for g in range(NG):
                        v0 = (NSLOT * g + h) * HD
                        for t in range(2):
                            ins = pe.matmul(pb[:, 3, P:NT], v_tok[:, t, v0:v0 + HD], probs_t[:, NG + 2 * g + t, :],
                                            start=g == 0 and t == 0, stop=g == NG - 1 and t == 1)
                    ins.then_inc(att_done, 1)

            def decode(i, j):
                if (i, j) == (4, 2):
                    pe.wait_ge(sc_ready, len(UNITS))
                    pe.wait_ge(kq_ready, 1)
                    pe.wait_ge(att_read, 2)
                    for g in range(NG):
                        pe.transpose(pb[0:32, 3, g * P:(g + 1) * P], sc_dec[:, g].rearrange("p b h -> p (b h)"), ident[:])
                    for g in range(NG):
                        ins = pe.matmul(pb[0:32, 3, NG * P + g:NG * P + g + 1], kq[:, g].rearrange("p b h -> p (b h)"), ones[:, 0:1],
                                        start=True, stop=True)
                    ins.then_inc(ds_done, 1)
                if (i, j) == (6, 2):
                    pe.wait_ge(diag_ready, 1)
                    pe.wait_ge(att_read, 3)
                    for g in range(NG):
                        pe.transpose(pb[:, 3, g * 32:(g + 1) * 32], dec_p[:, g * P:(g + 1) * P], ident[0:32, 0:32])
                    pe.matmul(pb[:, 3, P:P + 96], ones[0:32, :], dec_diag[:].rearrange("p a b -> p (a b)"),
                              start=True, stop=True).then_inc(dt_done, 1)

            def gates_b(i, ph=PH["gates_b"]):
                for j in range(8):
                    if j % 4 == 0:
                        open_group(ph, i, j // 4)
                    slab_products(ph, i, j, j // 4, xg_hi, xg_lo, KS * (j % 4), KS, j % 4 == 0, j % 4 == 3)
                    if j in (4, 7):
                        h = 0 if j == 4 else 1
                        k = 2 * i + h
                        pe.wait_ge(xr_ready, k + 1)
                        pe.wait_ge(xi_ready, k + 1)
                        if not (below(i, 1) and h == 0):
                            pe.wait_ge(y_read, k)
                        for t in range(4):
                            out = pb[:, 2, t * (NS + NB):(t + 1) * (NS + NB)]
                            for ri in range(2):
                                c0 = TB_C + (2 * t + ri) * P
                                pe.matmul(out, tab[h][:, c0:c0 + P], xs[:, ri, t, 0:NS + NB], start=ri == 0, stop=False)
                            ins = pe.matmul(out, tab[h][:, TB_K + t * P:TB_K + (t + 1) * P], u4[:, bass.ds(4 * k + t, 1), 0:NS + NB],
                                            start=False, stop=True)
                        ins.then_inc(y_done, 1)
                    if j in (1, 4):
                        h = j // 4
                        k = 2 * i + h
                        pe.wait_ge(tab_loaded[h], 16 * i + 16)
                        if below(i, 1) and h == 0:
                            pe.wait_ge(u4_loaded, 16 * 24)
                        else:
                            pe.wait_ge(sv_ready, k)
                        for t in range(4):
                            for ri in range(2):
                                c0 = TB_B + (2 * t + ri) * P
                                ins = pe.matmul(pb[:, ri, t * (NS + NB):(t + 1) * (NS + NB)], tab[h][:, c0:c0 + P],
                                                u4[:, bass.ds(4 * k + t, 1), NS:2 * NS + NB], start=True, stop=True)
                        ins.then_inc(su_done, 1)
                    if j in (2, 6):
                        h = j // 4
                        k = 2 * i + h
                        pe.wait_ge(vu_loaded[h], 48 * i + 48)
                        if below(i, 1) and h == 0:
                            pe.wait_ge(att_read, NSLOT)
                        else:
                            pe.wait_ge(pv_read, k)
                        for hh in range(NSLOT):
                            for g in range(NG):
                                ins = pe.matmul(pb[:, 3, hh:hh + 1], vu[3 * h + g][:, hh * HD:(hh + 1) * HD],
                                                pt_dec[:, g, bass.ds(NSLOT * k + hh, 1)], start=g == 0, stop=g == NG - 1)
                        ins.then_inc(pv_done, 1)

            pe.wait_ge(const_ready, 2)
            pe.wait_ge(rows_loaded, 32 + 16 * len(VEC_LOADS))
            pe.transpose(pb[:, 3, 0:NV], vec_rows[0:NV, :], ident[0:NV, 0:NV]).then_inc(vec_t, 1)
            for c in range(KD // 2):
                if c == 1:
                    pe.wait_ge(vec_ready, 1)
                if c >= 2:
                    pe.wait_ge(x_ready, c - 1)
                for u in range(2):
                    k, bank = 2 * c + u, 2 * (c % 2) + u
                    for t in range(2):
                        pe.transpose(pb[:, bank, t * P:(t + 1) * P], x_rows[:, t, k * P:(k + 1) * P], ident[:])
                    ins = pe.transpose(pb[:, bank, 2 * P:T], x_rows[0:NS, 2, k * P:(k + 1) * P], ident[0:NS, 0:NS])
                ins.then_inc(rows_t, 1)
            pe.wait_ge(x_ready, KD // 2)
            ffn(0)
            for name in ("u", "q", "k", "v", "gates_a"):
                ph = PH[name]
                for i in range(ph.iters):
                    x = XQ.get(name, -99) + i
                    open_group(ph, i, 0)
                    for j in range(4):
                        if name == "u":
                            pe.wait_ge(xlo_ready, 8 + 2 * j + 2)
                        slab_products(ph, i, j, 0, xg_hi, xg_lo, KS * j, KS, j == 0, j == 3)
                        if name == "u" and i == 0 and j == 2:
                            mean_square(1)
                        if j == 1 and 1 <= x <= NH:
                            head_stats(x)
                        heads_to_rows(x, j)
                        if name == "gates_a":
                            attention(i, j)
                            decode(i, j)
            loop(pe, PH["gates_b"], gates_b, 1)
            ph = PH["attn_branch"]
            pe.wait_ge(att_lo_ready, 1)
            for i in range(2):
                for g in range(4):
                    open_group(ph, i, g)
                    slab_products(ph, i, g, g, att_hi, att_lo, 0, KS, True, True)
            ph = PH["glu"]
            for i in range(2):
                for j in range(4):
                    if j % 2 == 0:
                        open_group(ph, i, j // 2)
                    pe.wait_ge(zlo_ready, j % 2 + 1)
                    slab_products(ph, i, j, j // 2, zs_hi, zs_lo, KS * (j % 2), KS, j % 2 == 0, j % 2 == 1)
                    if (i, j) == (0, 2):
                        pe.wait_ge(xnew_step, 8)
                        for ri in range(2):
                            for blk in range(2):
                                m = 2 * ri + blk
                                pe.transpose(pb[:, 0, m * P:(m + 1) * P], xnew[:, ri, blk * P:(blk + 1) * P], ident[:])
                        for ri in range(2):
                            ins = pe.transpose(pb[0:32, 1, ri * P:(ri + 1) * P], x_fin[:, ri, :], ident[:])
                        ins.then_inc(st_t, 1)

            def ssm_branch(i, ph=PH["ssm_branch"]):
                for j in range(4):
                    if j % 2 == 0:
                        open_group(ph, i, j // 2)
                    if below(i, 1):
                        pe.wait_ge(slo_ready, 2 * (j % 2) + 2)
                    slab_products(ph, i, j, j // 2, s_hi, s_lo, KS * (j % 2), KS, j % 2 == 0, j % 2 == 1)
            loop(pe, PH["ssm_branch"], ssm_branch, 1)

            def w_out(i, ph=PH["w_out"]):
                for j in range(8):
                    if j % 4 == 0:
                        open_group(ph, i, j // 4)
                    if below(i, 1) and j < 4:
                        pe.wait_ge(actlo_ready, ACT0["ssm_branch"] + 2 * j + 2)
                    slab_products(ph, i, j, j // 4, act_hi, act_lo, KS * (j % 4), KS, j % 4 == 0, j % 4 == 3)
            loop(pe, PH["w_out"], w_out, 1)
            ffn(1)
            ph = PH[LAST]
            for c in range(KD // 2):
                pe.wait_ge(evacuated, ph.group0 + c + 1)
                if c:
                    pe.wait_ge(yrow_ready, c)
                for u in range(2):
                    for t in range(3):
                        n = P if t < 2 else NS
                        ins = pe.transpose(pb[0:n, t, u * P:(u + 1) * P], x_t[:, 2 * c + u, t * P:t * P + n], ident[:])
                ins.then_inc(yt_ready, 1)

        @block.gpsimd
        def _(pool):
            def squares(r, after):
                if r:
                    pool.wait_ge(mean_ready, r)
                pool.memset(ssq[:], 0.0).then_inc(ssq_zero, 1)
                pool.wait_ge(ssq_zero, r + 2)
                for c in range(8):
                    pool.wait_ge(sq_ready, 8 * r + c + 1)
                    if c:
                        pool.wait_ge(ssq_ready, 8 * r + c)
                    pool.tensor_tensor(ssq[:], ssq[:], sq_v[:], ALU.add).then_inc(ssq_ready, 1)
                    after(c)

            def parameters():
                step = Chain(pool, step_done)
                tt, ts = pool.tensor_tensor, pool.tensor_scalar
                lr, li = prm[:, 0:NTILE], prm[:, NTILE:2 * NTILE]
                S = lambda k: scr[:, k]
                pool.wait_ge(prm_ready, 2)
                pool.wait_ge(dt_ready, 1)
                step(tt(S(1), lr, S(0), ALU.mult))
                step(tt(S(2), li, S(0), ALU.mult))
                step(ts(S(5), S(2), 1 / (2 * np.pi), None, ALU.mult))
                step(ts(S(6), S(5), 0.25, None, ALU.add))
                step(ts(scr[:, 5:7], scr[:, 5:7], MAGIC, None, ALU.add))
                step(ts(scr[:, 5:7], scr[:, 5:7], -MAGIC, None, ALU.add))
                for m, part in enumerate(TWO_PI):
                    step(ts(scr[:, 14:16], scr[:, 5:7], part, None, ALU.mult))
                    for k in range(2):
                        step(tt(S(3 + k), S(2) if m == 0 else S(3 + k), S(14 + k), ALU.subtract))
                step(ts(S(4), S(4), float(np.pi / 2), None, ALU.add))
                step(ts(scr[:, 3:5], scr[:, 3:5], 3.1415925, None, ALU.min))
                pool.tensor_scalar(scr[:, 3:5], scr[:, 3:5], -3.1415925, None, ALU.max).then_inc(angles_ready, 1)
                step(tt(S(14), lr, lr, ALU.mult))
                step(tt(S(15), li, li, ALU.mult))
                tt(S(11), S(14), S(15), ALU.add).then_inc(den_ready, 1)
                pool.wait_ge(trig_ready, 2)
                mag, sn, cn, ar, ai = S(8), S(9), S(10), a_t[:, 0], a_t[:, 1]
                step(tt(ar, mag, cn, ALU.mult))
                step(tt(ai, mag, sn, ALU.mult))
                step(ts(S(13), ar, -1.0, None, ALU.add))
                pool.wait_ge(inv_ready, 1)
                for out, p, q, op in ((16, (S(13), lr), (ai, li), ALU.add), (17, (ai, lr), (S(13), li), ALU.subtract)):
                    step(tt(S(14), *p, ALU.mult))
                    step(tt(S(15), *q, ALU.mult))
                    step(tt(S(out), S(14), S(15), op))
                    step(tt(S(out), S(out), S(12), ALU.mult))

                def cmul(outr, outi, xr, xi, yr, yi, t0, t1):
                    step(tt(t0, xr, yr, ALU.mult))
                    step(tt(t1, xi, yi, ALU.mult))
                    step(tt(outr, t0, t1, ALU.subtract))
                    step(tt(t0, xr, yi, ALU.mult))
                    step(tt(t1, xi, yr, ALU.mult))
                    step(tt(outi, t0, t1, ALU.add))

                step(pool.memset(pw[:, 0, :, 0:1], 1.0))
                step(pool.memset(pw[:, 1, :, 0:1], 0.0))
                for n in range(1, LAGS):
                    cmul(pw[:, 0, :, n], pw[:, 1, :, n], pw[:, 0, :, n - 1], pw[:, 1, :, n - 1], ar, ai, S(14), S(15))
                step(ts(npowi[:], pw[:, 1], -1.0, None, ALU.mult))
                for s in range(STEP):
                    n = STEP - 1 - s
                    cmul(wf[:, 0, :, s], wf[:, 1, :, s], pw[:, 0, :, n], pw[:, 1, :, n], S(16), S(17), S(14), S(15))
                step(tt(S(18), mag, mag, ALU.mult))
                step(tt(S(19), S(18), S(18), ALU.mult))
                step(pool.tensor_copy(em_tab[:, 2], scr[:, 19, :, None].to_broadcast([P, NTILE, NB])))
                step(pool.memset(em_tab[:, 2, :, 0:1], 0.0))
                cmul(S(20), S(21), cn, sn, cn, sn, S(14), S(15))
                cmul(S(22), S(23), S(20), S(21), S(20), S(21), S(14), S(15))
                step(pool.memset(em_tab[:, 0, :, 0:1], 1.0))
                step(pool.memset(em_tab[:, 1, :, 0:1], 0.0))
                n, u, w = 1, (22, 23), (24, 25)
                while n < NB:
                    ur, ui = (scr[:, k, :, None].to_broadcast([P, NTILE, n]) for k in u)
                    cmul(em_tab[:, 0, :, n:2 * n], em_tab[:, 1, :, n:2 * n], em_tab[:, 0, :, 0:n], em_tab[:, 1, :, 0:n], ur, ui,
                         ctmp[:, 0, :, 0:n], ctmp[:, 1, :, 0:n])
                    cmul(S(w[0]), S(w[1]), S(u[0]), S(u[1]), S(u[0]), S(u[1]), S(14), S(15))
                    n, u, w = 2 * n, w, u
                for k in range(SC):
                    pool.dma_start(ssm_tab[k, :, TB_E:TB].rearrange("p (a t c) -> p a t c", a=3, t=4),
                                   em_tab[:, :, 4 * k:4 * k + 4, :]).then_inc(tab_stored, 16)
                pool.wait_ge(tab_stored, 16 * SC)
                step(pool.memset(pre[:], 0.0))
                step(pool.memset(kbig[:], 0.0))
                return step

            def half_b(i, step):
                def w_of(ri):
                    return wf[:, ri, 4 * i:4 * i + 4, :, None].to_broadcast([P, 4, STEP, 16])
                def b_of(ri):
                    return b_in[:, ri, 4 * i:4 * i + 4, None, :].to_broadcast([P, 4, STEP, 16])
                for ri, (x, y, op) in enumerate((((0, 0), (1, 1), ALU.subtract), ((0, 1), (1, 0), ALU.add))):
                    step(pool.tensor_tensor(b_tmp[:, 0], w_of(x[0]), b_of(x[1]), ALU.mult))
                    step(pool.tensor_tensor(b_tmp[:, 1], w_of(y[0]), b_of(y[1]), ALU.mult))
                    for g in range(2):
                        step(pool.tensor_tensor(pre[64 * g:64 * g + 64, ri, :, :, g, :], b_tmp[64 * g:64 * g + 64, 0],
                                                b_tmp[64 * g:64 * g + 64, 1], op))
                for ri in range(2):
                    for g in range(2):
                        ins = pool.tensor_scalar(c_exp[:, ri, g, :], c_in[:, ri, i, :],
                                                 gm[:, g:g + 1], None, ALU.mult)
                ins.then_inc(pre_ready, 1)

            def store_table(i):
                pool.wait_ge(kbig_ready, i + 1)
                row = ssm_tab[i]
                pool.dma_start(row[:, TB_B:TB_C], bb_t[:]).then_inc(tab_stored, 16)
                pool.dma_start(row[:, TB_C:TB_K].rearrange("p (a c) -> p a c", a=8),
                               ca5[:].rearrange("p t a c -> p (t a) c")[:, :, 32:]).then_inc(tab_stored, 16)
                pool.dma_start(row[:, TB_K:TB_E], kbig[:].rearrange("p t c -> p (t c)")).then_inc(tab_stored, 16)

            pool.memset(ident[:], 0.0).then_inc(ssq_zero, 1)
            pool.wait_ge(ssq_zero, 1)
            pool.affine_select(out=ident[:], in_=ident[:], compare_op=ALU.not_equal, fill=1.0,
                               base=0, pattern=[[-1, P]], channel_multiplier=1).then_inc(const_ready, 1)
            pool.dma_start(log_dt[64:96, :], A["ssm_log_dt"][0].rearrange("(t g) -> t g", g=2)).then_inc(dt_loaded, 16)
            for row, name in ((0, "ssm_lambda_re"), (32, "ssm_lambda_im")):
                pool.dma_start(prm_rows[row:row + 32, :], A[name][0].rearrange("(t g) s -> t (g s)", g=2)).then_inc(par_loaded, 16)
            for s in range(STEP):
                pool.dma_start(prm_rows[96:128, 32 * s:32 * s + 32], A["ssm_d"][0].rearrange("(t f) -> t f", f=32)).then_inc(par_loaded, 16)
            for ri, name in enumerate(("state_ssm_re", "state_ssm_im")):
                pool.dma_start(x0_rows[:, ri], A[name][0].rearrange("(k b) (t g) s -> (b t) k (g s)", k=2, g=2)).then_inc(par_loaded, 16)
            pool.dma_start(gm[:], A["consts"][:, C_GM:C_GM + 2]).then_inc(par_loaded, 16)
            for ri, name in enumerate(("ssm_b_re", "ssm_b_im")):
                pool.dma_start(b_in[:, ri], A[name][0].rearrange("(t g) p c -> (g p) t c", g=2)).then_inc(par_loaded, 16)
            for ri, name in enumerate(("ssm_c_re", "ssm_c_im")):
                pool.dma_start(c_in[:, ri], A[name][0].rearrange("(k q) c p -> (q c) k p", k=SC)).then_inc(par_loaded, 16)

            squares(0, lambda c: None)
            pool.wait_ge(par_loaded, 16 * 13)
            step = parameters()
            for i in range(SC):
                if i:
                    pool.wait_ge(k_done, i)
                half_b(i, step)
                if i:
                    store_table(i - 1)
            store_table(SC - 1)
            pool.wait_ge(tab_stored, 16 * 4 * SC)

            def spill(c):
                pool.wait_ge(evacuated, PH["down02"].group0 + c + 1)
                pool.dma_start(x_dram[:, 2 * c * T:(2 * c + 2) * T], x_t[:, 2 * c:2 * c + 2, :].rearrange("p a t -> p (a t)")).then_inc(spilled, 16)
            squares(1, spill)
            pool.wait_ge(spilled, 16 * KD // 2)
            pool.wait_ge(xlo_ready, KD)
            for lo in (0, NS + NB):
                ins = pool.memset(u4[:, :, lo:lo + NS], 0.0)
            ins.then_inc(u4_zero, 1)

            pool.wait_ge(const_loaded, 32)

            def heads(x):
                pool.wait_ge(t1_ready, 2 * x + 2)
                pool.tensor_tensor(qk[:, 2 * x:2 * x + 2, :], up_v[:], cs[:, 0, None, :].to_broadcast([P, 2, T]), ALU.mult).then_inc(cos_ready, 1)
                pool.wait_ge(cos_ready, x + 1)
                pool.wait_ge(rot_ready, 2 * x + 2)
                pool.tensor_tensor(qk[:, 2 * x:2 * x + 2, :], qk[:, 2 * x:2 * x + 2, :], silu_v[:], ALU.add).then_inc(qk_ready, 1)

            def store_rows(r):
                pool.wait_ge(rows_ready, 2 * r + 2)
                g, kv = r % 3, r // 3 - 1
                if kv < 0:
                    pool.dma_start(q_dram[:, g * 512:(g + 1) * 512], s_rows[0:NS, :]).then_inc(rows_stored, 16)
                    return
                n = GROUPS[g][0]
                pool.dma_start(new_caches[g][:, kv, n - 1].rearrange("b h d -> b (h d)"), s_rows[0:NS, :]).then_inc(rows_stored, 16)
                src = k_rows if kv == 0 else v_tok[:, :, g * 512:(g + 1) * 512]
                dst = prompt_kv[g][kv].rearrange("n h d -> n (h d)")
                if g == 0:
                    pool.dma_start(dst, src[:, 1]).then_inc(rows_stored, 16)
                else:
                    pool.dma_start(dst.rearrange("(t p) c -> p t c", p=P), src if kv else src[:]).then_inc(rows_stored, 16)

            def unit(n):
                pool.wait_ge(ku_loaded[n % 4], 16 * (n // 4 + 1))
                pool.wait_ge(qb_loaded[n % 2], 16 * (n // 2 + 1))
                if n >= 2:
                    pool.wait_ge(sc_ready, n - 1)
                pool.tensor_tensor(prod[n % 2][:].rearrange("p h d -> p (h d)"), ku[n % 4][:], qb[n % 2][:], ALU.mult).then_inc(prod_ready, 1)

            for x in range(NH):
                heads(x)
                if x >= 2 and x % 2 == 0:
                    store_rows((x - 2) // 2)
            store_rows(5)
            for n in range(len(UNITS)):
                unit(n)
                if n in (3, 11, 19):
                    store_rows(6 + n // 8)
            q_s = qk[:, 0:NH, NT:T].rearrange("p (g h) b -> p g b h", g=NG)
            k_s = qk[:, NH:2 * NH, NT:T].rearrange("p (g h) b -> p g b h", g=NG)
            pool.tensor_tensor(kq[:], q_s, k_s, ALU.mult).then_inc(kq_ready, 1)

            pool.wait_ge(att_done, NSLOT)
            pool.memset(xs[:, :, :, NS:NS + 1], 0.0).then_inc(xs_zero, 1)

            def gates_b(i):
                for h in range(2):
                    k = 2 * i + h
                    E = tab[h][:, E0:M0].rearrange("p (a c) -> p a c", a=2)
                    pool.wait_ge(sv_ready, k + 1)
                    if not (below(i, 1) and h == 0):
                        pool.wait_ge(xr_ready, k)
                    pool.tensor_tensor(p_tmp[:, 0], sv[:, 0], E[:, 0], ALU.mult).then_inc(zr_step, 1)
                    pool.wait_ge(zr_step, 4 * k + 1)
                    pool.tensor_tensor(p_tmp[:, 1], sv[:, 1], E[:, 1], ALU.mult).then_inc(zr_step, 1)
                    pool.wait_ge(zr_step, 4 * k + 2)
                    pool.tensor_tensor(z_in[:, 0], p_tmp[:, 0], p_tmp[:, 1], ALU.add).then_inc(zr_ready, 1)
                    pool.wait_ge(scan_ready, 2 * k + 2)
                    pool.tensor_tensor(p_tmp[:, 0], z_out[:, 0], E[:, 0], ALU.mult).then_inc(zr_step, 1)
                    pool.wait_ge(zr_step, 4 * k + 3)
                    pool.tensor_tensor(p_tmp[:, 1], z_out[:, 1], E[:, 1], ALU.mult).then_inc(zr_step, 1)
                    pool.wait_ge(zr_step, 4 * k + 4)
                    if not (below(i, 1) and h == 0):
                        pool.wait_ge(y_read, k)
                    pool.tensor_tensor(xs[:, 0, :, NS + 1:NS + 1 + NB], p_tmp[:, 0].rearrange("p (t c) -> p t c", t=4),
                                       p_tmp[:, 1].rearrange("p (t c) -> p t c", t=4), ALU.subtract).then_inc(xr_ready, 1)
            loop(pool, PH["gates_b"], gates_b, 1)
            pool.wait_ge(y_read, SC)
            for jj in range(4):
                pool.dma_start(yt_v[32 * jj:32 * jj + 32, :, 3 * NB:4 * NB], u4[96:128, jj::4, NS:NS + NB]).then_inc(yl_loaded, 16)
                pool.dma_start(yt_v[32 * jj:32 * jj + 32, :, NT:T], u4[0:32, jj::4, 0:NS]).then_inc(yl_loaded, 16)
            pool.wait_ge(pv_done, NS)
            step = Chain(pool, xnew_step)
            ar, ai = (a_t[:, ri, None, :].to_broadcast([P, NS, NTILE]) for ri in range(2))
            tmp = [xtmp[:, k].rearrange("p (b t) -> p b t", b=NS) for k in range(2)]
            for ri, (x, y, op) in enumerate(((0, 1, ALU.subtract), (1, 0, ALU.add))):
                step(pool.tensor_tensor(tmp[0], ar, x0_t[:, x], ALU.mult))
                step(pool.tensor_tensor(tmp[1], ai, x0_t[:, y], ALU.mult))
                step(pool.tensor_tensor(tmp[0], tmp[0], tmp[1], op))
                step(pool.tensor_tensor(xnew[:, ri].rearrange("p (b t) -> p b t", b=NS), tmp[0],
                                        s_new[:, ri].rearrange("p t b -> p b t"), ALU.add))
            pool.wait_ge(yt_loaded, 16 * 12)
            pool.wait_ge(yl_loaded, 16 * 8)
            pool.wait_ge(att_lo_ready, 1)
            pool.dma_start(x_t[:].rearrange("p a t -> p (a t)"), x_dram).then_inc(x_back, 16)
            pool.wait_ge(st_rows_ready, 1)
            for ri, (sample, prompt) in enumerate((("ssm_re_s", "ssm_re_p"), ("ssm_im_s", "ssm_im_p"))):
                pool.dma_start(O[sample][0].rearrange("(k b) (t g) s -> (b t) k (g s)", k=2, g=2),
                               st_rows[:, 2 * ri:2 * ri + 2, :]).then_inc(rows_stored, 16)
                pool.dma_start(O[prompt][0, 0].rearrange("(t g) s -> t (g s)", g=2), st_rows[0:32, 4 + ri, :]).then_inc(rows_stored, 16)
            squares(2, lambda c: None)
            pool.wait_ge(rows_stored, stored_rows(8) + 64)


_OUTS = [("y_p", (1, 256, 2048)), ("y_s", (8, 1, 2048)),
         ("kv128_p", (1, 1, 2, 128, 4, 128)), ("kv512_p", (1, 1, 2, 256, 4, 128)), ("kv2048_p", (1, 1, 2, 256, 4, 128)),
         ("ssm_re_p", (1, 1, 64, 64)), ("ssm_im_p", (1, 1, 64, 64)),
         ("kv128_s", (1, 8, 2, 128, 4, 128)), ("kv512_s", (1, 8, 2, 512, 4, 128)), ("kv2048_s", (1, 8, 2, 2048, 4, 128)),
         ("ssm_re_s", (1, 8, 64, 64)), ("ssm_im_s", (1, 8, 64, 64))]


def kernel(**inputs):
    import concourse.bacc as _bacc
    from concourse.bass_utils import run_bass_kernel_spmd as _run

    nc = _bacc.Bacc("TRN2", target_bir_lowering=False, num_devices=1)
    arrays, args, outs = {}, {}, {}
    for name, a in {**inputs, "consts": shape_constants()}.items():
        a = np.ascontiguousarray(a)
        arrays[f"in_{name}"] = a
        args[name] = nc.dram_tensor(f"in_{name}", a.shape, mybir.dt.from_np(a.dtype), kind="ExternalInput").ap()
    for name, shape in _OUTS:
        outs[name] = nc.dram_tensor(f"out_{name}", shape, mybir.dt.float32, kind="ExternalOutput").ap()
    build_layer(nc, args, outs)
    r = _run(nc, [arrays], core_ids=[0])
    return tuple(r.results[0][f"out_{name}"] for name, _ in _OUTS)
```

```python
import numpy as np
import concourse.bass as bass
from concourse import mybir

D = 2048
P = 128
KD = D // P
NT = 256
NS = 8
T = NT + NS
FF = 5504
HD = 128
NSLOT = 4
GROUPS = ((128, 1), (512, 4), (2048, 16))
NG = len(GROUPS)
NH = NG * NSLOT
BACK = 128
SW = 1024
SC = SW // P
NTILE = 32
STEP = 4
NB = NT // STEP
LAGS = STEP + 1
UOFF = 3 * NH * HD
GOFF = UOFF + SW
EPS = 1e-6
SCALE = float(HD) ** -0.5
NEG = -1e30

RING = 4
LEAD = 3
KS = 4

BLOCK_TILE0 = (0, 16, 32)


def ffn_phases(f):
    return [(f"up{f}0", 8, 8, 2), (f"down{f}0", 4, 8, 2), (f"up{f}1", 8, 8, 2), (f"down{f}1", 4, 8, 2),
            (f"up{f}2", 5, 8, 2), (f"single{f}", 1, 4, 2), (f"down{f}2", 2, 12, 4)]


MIX_PHASES = [("u", 4, 4, 1), ("q", 6, 4, 1), ("k", 6, 4, 1), ("v", 6, 4, 1), ("gates_a", 8, 4, 1),
              ("gates_b", 4, 8, 2), ("attn_branch", 2, 4, 4), ("glu", 2, 4, 2), ("ssm_branch", 4, 4, 2),
              ("w_out", 4, 8, 2)]
ORDER = ffn_phases(0) + MIX_PHASES + ffn_phases(1)

ACT0 = {"up00": 0, "up01": 8, "up02": 16, "single0": 21, "ssm_branch": 22,
        "up10": 30, "up11": 38, "up12": 46, "single1": 51}
HID0 = {"up00": 0, "up01": 8, "up02": 16, "single0": 21, "up10": 22, "up11": 30, "up12": 38, "single1": 43}
NORM_AFTER = {"down02": 1, "w_out": 2}
LAST = ORDER[-1][0]

VEC_LOADS = (("ffn1_norm", 0, 16), ("mix_norm", 16, 16), ("ffn2_norm", 32, 16), ("q_norm", 48, 12),
             ("k_norm", 60, 12), ("glu_b", 72, 8))
V_NORM, V_HEAD, V_GLU, NV = (0, 16, 32), 48, 72, 80

C_COS, C_SIN, C_GM, C_MASK0 = 0, T, 2 * T, 2 * T + 2
C_MASK1 = C_MASK0 + NG * P
NC = C_MASK1 + NG * NT

TB_B, TB_C, TB_K, TB_E, TB_M, TB = 0, 1024, 2048, 2560, 3072, 3328
MAGIC = 1.5 * 2.0 ** 23
TWO_PI = (6.28125, 0.0019350051879882812, 3.0199157663e-07)


def shape_constants():
    past = 2048
    pos = np.concatenate([np.arange(NT), np.full(NS, past)]).astype(np.float32)
    inv = np.power(np.float32(10000.0), -np.arange(HD // 2, dtype=np.float32) * np.float32(2.0 / HD))
    ang = (pos[None, :] * inv[:, None]).astype(np.float32)
    c = np.zeros((P, NC), np.float32)
    c[:, C_COS:C_COS + T] = np.concatenate([np.cos(ang), np.cos(ang)], 0)
    c[:, C_SIN:C_SIN + T] = np.concatenate([np.sin(ang), -np.sin(ang)], 0)
    c[:, C_GM + 1] = (np.arange(P) // 16) % 2
    c[:, C_GM] = 1 - c[:, C_GM + 1]
    for first, width, base in ((0, P, C_MASK0), (P, NT, C_MASK1)):
        q, k = np.arange(first, first + P)[:, None], np.arange(width)[None, :]
        for g, (_, dil) in enumerate(GROUPS):
            ok = (k <= q) & (q - k <= BACK * dil) & ((q - k) % dil == 0)
            c[:, base + g * width:base + (g + 1) * width] = np.where(ok, 0.0, NEG)
    return c


class Phase:

    def __init__(self, name, iters, slabs, groups, slab0, group0):
        self.name, self.iters, self.slabs, self.groups = name, iters, slabs, groups
        self.slab0, self.group0 = slab0, group0

    def slab(self, i, j):
        return (self.slab0 + j) % RING, (self.slab0 + j) // RING + i * (self.slabs // RING), self.slab0 + j + i * self.slabs

    def banks(self, i, g):
        return (self.group0 + g + (i * self.groups if self.groups % 2 else 0)) % 2

    def group(self, i, g):
        return self.group0 + g + i * self.groups


def plan():
    phases, slab, group = {}, 0, 0
    for name, iters, slabs, groups in ORDER:
        phases[name] = Phase(name, iters, slabs, groups, slab, group)
        slab, group = slab + iters * slabs, group + iters * groups
    return phases, slab


def pair_slabs(name):
    if name in ("down02", "down12"):
        return (4, 4, 3)
    return {"attn_branch": (4,), "glu": (4, 4), "ssm_branch": (4, 4)}.get(name, (4, 4, 4, 4))


def below(n, limit):
    return isinstance(n, int) and n < limit


def loop(eng, ph, body, peel=0, tail=0):
    if ph.iters - peel - tail == 1:
        peel = ph.iters - tail
    for i in range(peel):
        body(i)
    if ph.iters - tail > peel:
        with eng.Fori(peel, ph.iters - tail) as i:
            body(i)
    for i in range(ph.iters - tail, ph.iters):
        body(i)


class Chain:

    def __init__(self, eng, sem):
        self.eng, self.sem, self.n = eng, sem, 0

    def __call__(self, ins):
        self.n += 1
        ins.then_inc(self.sem, 1)
        self.eng.wait_ge(self.sem, self.n)


def build_layer(nc, A, O):
    f32, f32r = mybir.dt.float32, mybir.dt.float32r
    ALU, ACT, AX = mybir.AluOpType, mybir.ActivationFunctionType, mybir.AxisListType
    PH, TOTAL = plan()

    END = 229344
    top = [16512]

    def region(nbytes):
        at = top[0]
        top[0] += (nbytes + 31) // 32 * 32
        assert top[0] <= END, top[0]
        return at

    def tile(name, shape, dt=f32, at=None):
        if at is None:
            at = region(4 * int(np.prod(shape[1:])))
        return nc.alloc_sbuf_tensor_at(name, shape, dt, offset=at)

    def tiles(at, limit, *specs):
        out, start = [], at
        for name, shape, *dt in specs:
            out.append(tile(name, shape, dt[0] if dt else f32, at))
            at += (4 * int(np.prod(shape[1:])) + 31) // 32 * 32
        assert at - start <= limit, (specs[0][0], at - start, limit)
        return out

    CH = 4 * KD * T
    raw = tile("raw", [P, RING, KS, 256])
    w_hi = tile("w_hi", [P, RING, KS, 256], f32r)
    w_lo = tile("w_lo", [P, RING, KS, 256], f32r)
    rstd = tile("rstd", [P, T])
    sd = tile("sd", [P, T])
    ident, mean_w, head_w, ones = (tile(n, [P, P]) for n in ("ident", "mean_w", "head_w", "ones"))
    vec = tile("vec", [P, NV])
    small = tile("small", [P, 4])
    eps_t, halfpi_t = small[:, 0:1], small[:, 1:2]

    RX = region(CH)
    x_t = tile("x_t", [P, KD, T], f32, RX)
    u4, att_v, qb1 = tiles(RX, CH, ("u4", [P, NTILE, NS + NB + NS]),
                           ("att_v", [P, NSLOT, T]),
                           ("qb1", [P, NSLOT * HD]))
    RG = region(2 * CH)
    xg_hi, xg_lo = tiles(RG, 2 * CH, ("xg_hi", [P, KD, T], f32r), ("xg_lo", [P, KD, T], f32r))
    s_hi, s_lo, zs_v = tiles(RG, 2 * CH, ("s_hi", [P, SC, T], f32r), ("s_lo", [P, SC, T], f32r), ("zs_v", [P, SC, T]))
    y_rows = tile("y_rows", [P, 3, D], f32, RG)
    RA = region(2 * CH)
    act_hi, act_lo = tiles(RA, 2 * CH, ("act_hi", [P, KD, T], f32r), ("act_lo", [P, KD, T], f32r))
    x_rows = tile("x_rows", [P, 3, D], f32, RA)
    gates = tile("gates", [P, 2 * KD, T], f32, RA)
    masks, probs, probs_t, dec_p, dec_diag = tiles(
        RA + CH, CH, ("masks", [P, NG * (P + NT)]), ("probs", [P, NG * (P + NT)]),
        ("probs_t", [P, 9, P]), ("dec_p", [NS * NSLOT, NG * P + NG]), ("dec_diag", [NS * NSLOT, NG, NS * NSLOT]))
    RT = region(5 * 8 * T)
    gate_v, up_v, silu_v, hid_v, sq_v = tiles(RT, 40 * T, *((n, [P, 2, T]) for n in ("gate_v", "up_v", "silu_v", "hid_v", "sq_v")))
    prod = [tile(f"prod{k}", [P, NSLOT, HD], f32, RT + 8 * T * (k + 1)) for k in range(2)]
    sv = tile("sv", [P, 2, 4 * NB], f32, RT + 24 * T)
    squares_v = [sq_v, hid_v]
    att_hi, att_lo = tiles(RT + 8 * T, 32 * T, ("att_hi", [P, NSLOT, T], f32r), ("att_lo", [P, NSLOT, T], f32r))
    RQ = region(8 * T)
    ssq = tile("ssq", [P, 2, T], f32, RQ)
    qb0 = tile("qb0", [P, NSLOT * HD], f32, RT + 32 * T)
    qb = [qb0, qb1]
    head_sd = tile("head_sd", [P, 2, T], f32, RQ)
    QKV = 4 * (2 * NH * T + 2 * NH * HD)
    RM = region(QKV)
    qk, v_tok = tiles(RM, QKV, ("qk", [P, 2 * NH, T]),
                      ("v_tok", [P, 2, NH * HD]))
    tab0, tab1, z_out, d_tmp, z_in, xs, p_tmp = tiles(
        RM, QKV, ("tab0", [P, TB]), ("tab1", [P, TB]), ("z_out", [P, 2, 4 * NB]), ("d_tmp", [P, 2, 4 * NB]), ("z_in", [P, 2, 4 * NB]),
        ("xs", [P, 2, 4, NS + 1 + NB]), ("p_tmp", [P, 2, 4 * NB]))
    tab = [tab0, tab1]
    zs_hi, zs_lo, yt_v = tiles(RM, QKV, ("zs_hi", [P, SC, T], f32r), ("zs_lo", [P, SC, T], f32r), ("yt_v", [P, SC, T]))
    RR = region(4 * (SC * T + 2 * T + 2 * 512 + 512))
    RRN = top[0] - RR
    u_t, cs, k_rows, s_rows = tiles(RR, RRN, ("u_t", [P, SC, T]), ("cs", [P, 2, T]), ("k_rows", [P, 2, 512]), ("s_rows", [P, 512]))
    ku = [tile(f"ku{k}", [P, NSLOT * HD], f32, RR + 2048 * k) for k in range(4)]
    vu = [tile(f"vu{k}", [P, NSLOT * HD], f32, RR + 2048 * k) for k in range(6)]
    xnew, xtmp, st_rows = tiles(RR, RRN, ("xnew", [P, 2, 256]), ("xtmp", [P, 3, 256]), ("st_rows", [P, 6, P]))
    em_tab, ctmp, b_in, c_in = tiles(RM, top[0] - RM, ("em_tab", [P, 3, NTILE, NB]),
                                           ("ctmp", [P, 2, NTILE, NB // 2]), ("b_in", [P, 2, NTILE, 16]),
                                           ("c_in", [P, 2, SC, 64]))
    prm, pw, npowi, wf, scr = tiles(RM + 40960, top[0] - RM - 40960, ("prm", [P, 4 * NTILE]), ("pw", [P, 2, NTILE, LAGS]),
                                   ("npowi", [P, NTILE, LAGS]), ("wf", [P, 2, NTILE, STEP]), ("scr", [P, 26, NTILE]))
    vec_rows, prm_rows, log_dt, x0_rows = tiles(RM, 4096, ("vec_rows", [P, P]), ("prm_rows", [P, P]), ("log_dt", [P, 2]),
                                                ("x0_rows", [P, 2, 2, P]))
    BASE2 = 4 * (2 * NTILE * NB + NTILE * NB + 2 * NTILE * NB // 2)
    pre, bb_t, ca5, kbig, ca_tmp, im_tmp, c_exp, c_t, b_tmp = tiles(
        RM, BASE2, ("pre", [P, 2, 4, STEP, 2, 16]), ("bb_t", [P, 1024]), ("ca5", [P, 4, 2, LAGS * 32]), ("kbig", [P, 4, P]),
        ("ca_tmp", [P, 2, 4, LAGS * 32]), ("im_tmp", [P, 2, 4, LAGS * 32]),
        ("c_exp", [P, 2, 2, 64]), ("c_t", [P, 2, 4, 32]), ("b_tmp", [P, 2, 4, STEP, 16]))
    x0_t = tile("x0_t", [P, 2, NS, NTILE])
    s_new = tile("s_new", [P, 2, NTILE, NS])
    x_fin = tile("x_fin", [P, 2, NTILE])
    sc_dec = tile("sc_dec", [P, NG, NS, NSLOT])
    kq = tile("kq", [P, NG, NS, NSLOT])
    v_new = tile("v_new", [P, NH, NS])
    pt_dec = tile("pt_dec", [P, NG, NS * NSLOT])
    att_new = tile("att_new", [P, NG, NS * NSLOT])
    stat = tile("stat", [P, 16])
    a_t = tile("a_t", [P, 2, NTILE])
    gm = tile("gm", [P, 2])

    pa = nc.alloc_psum_tensor("pa", [P, 4, 512], f32)
    pb = nc.alloc_psum_tensor("pb", [P, 4, 512], f32)

    ssm_tab = nc.dram_tensor("ssm_tab", [SC, P, TB], f32).ap()
    q_dram = nc.dram_tensor("q_dram", [NS, NH * HD], f32).ap()
    x_dram = nc.dram_tensor("x_dram", [P, KD * T], f32).ap()


    def sems(names):
        return [nc.alloc_semaphore(n) for n in names.split()]

    slab_loaded = [nc.alloc_semaphore(f"slab_loaded{k}") for k in range(RING)]
    hi_ready, lo_ready, slab_used, evacuated = sems("hi_ready lo_ready slab_used evacuated")
    const_ready, rows_loaded, right_loaded, vec_loaded, vec_t, vec_ready, rows_t, x_ready = sems(
        "const_ready rows_loaded right_loaded vec_loaded vec_t vec_ready rows_t x_ready")
    sq_ready, ssq_ready, ssq_zero, xhi_ready, xlo_ready = sems("sq_ready ssq_ready ssq_zero xhi_ready xlo_ready")
    mean_ready, sd_ready, rstd_ready = sems("mean_ready sd_ready rstd_ready")
    gate_ready, silu_ready, hid_ready, acthi_ready, actlo_ready = sems("gate_ready silu_ready hid_ready acthi_ready actlo_ready")
    par_loaded, dt_loaded, dt_rows, prm_t, prm_ready, dt_ready = sems("par_loaded dt_loaded dt_rows prm_t prm_ready dt_ready")
    angles_ready, trig_ready, den_ready, inv_ready, step_done = sems("angles_ready trig_ready den_ready inv_ready step_done")
    tab_stored, e_stored, b_loaded, pre_ready, bb_done, bbt_ready, ca_ready, ca_im_ready, k_done, kbig_ready = sems(
        "tab_stored e_stored b_loaded pre_ready bb_done bbt_ready ca_ready ca_im_ready k_done kbig_ready")
    ca_step, k_step = sems("ca_step k_step")
    u_ready, u4_zero, u4_loaded, spilled, const_loaded = sems("u_ready u4_zero u4_loaded spilled const_loaded")
    head_sq, stat_done, head_sd_ready, head_inv, t1_ready, rot_ready, cos_ready, qk_ready = sems(
        "head_sq stat_done head_sd_ready head_inv t1_ready rot_ready cos_ready qk_ready")
    heads_t, rows_ready, rows_stored, v_new_ready = sems("heads_t rows_ready rows_stored v_new_ready")
    ku_loaded = [nc.alloc_semaphore(f"ku_loaded{k}") for k in range(4)]
    qb_loaded = [nc.alloc_semaphore(f"qb_loaded{k}") for k in range(2)]
    vu_loaded = [nc.alloc_semaphore(f"vu_loaded{k}") for k in range(2)]
    prod_ready, sc_ready, kq_ready, ds_done, dmax_ready, dexp_ready, dec_step, diag_ready, dt_done, dec_ready = sems(
        "prod_ready sc_ready kq_ready ds_done dmax_ready dexp_ready dec_step diag_ready dt_done dec_ready")
    vs_ready, v_step, v_sum_ready, pv_done, pv_read = sems("vs_ready v_step v_sum_ready pv_done pv_read")
    s_done, sm_ready, sm_step, nmax_ready, exp_ready, inv_sum, pn_ready, p_t, pt_ready, att_done, att_read = sems(
        "s_done sm_ready sm_step nmax_ready exp_ready inv_sum pn_ready p_t pt_ready att_done att_read")
    tab_loaded = [nc.alloc_semaphore(f"tab_loaded{k}") for k in range(2)]
    xs_zero, su_done, sv_ready, zr_ready, zi_step, zr_step, scan_ready, xi_ready, xr_ready, y_done, y_read = sems(
        "xs_zero su_done sv_ready zr_ready zi_step zr_step scan_ready xi_ready xr_ready y_done y_read")
    yt_loaded, yl_loaded, gelu_ready, zhi_ready, zlo_ready, sgl_ready, shi_ready, slo_ready = sems(
        "yt_loaded yl_loaded gelu_ready zhi_ready zlo_ready sgl_ready shi_ready slo_ready")
    xnew_step, st_t, st_rows_ready = sems("xnew_step st_t st_rows_ready")
    att_hi_ready, att_lo_ready, sig_ready, prod_s, m_ready, x_back = sems("att_hi_ready att_lo_ready sig_ready prod_s m_ready x_back")
    yt_ready, yrow_ready, stored = sems("yt_ready yrow_ready stored")

    def q_end(name):
        return PH[name].slab0 + PH[name].iters * PH[name].slabs

    XQ = {"q": 0, "k": 6, "v": 12, "gates_a": 18}

    def pair_group(x):
        return PH["q"].group0 + x

    def stored_rows(r):
        return 16 * (r + 1) if r < 3 else 48 + 32 * (r - 2)

    caches = [A["cache_kv_w128"][0], A["cache_kv_w512"][0], A["cache_kv_w2048"][0]]
    new_caches = [O["kv128_s"][0], O["kv512_s"][0], O["kv2048_s"][0]]
    prompt_kv = [O["kv128_p"][0, 0], O["kv512_p"][0, 0], O["kv2048_p"][0, 0]]
    UNIT_LOAD, UNIT_USE = 13, 9
    UNITS = [(g, b) for g in range(NG) for b in range(NS)]
    E0, M0 = TB_E, TB_M

    block = nc.Block()
    with block:
        @block.sync
        def _(sync):
            n_stored = [0]

            def put(ph, i, j, src, kt=KS, mt=256):
                slot, turn, n = ph.slab(i, j)
                if not below(n, RING):
                    sync.wait_ge(lo_ready, n - (RING - 1))
                dst = raw[:, slot, 0:kt, :]
                if mt == P:
                    dst = raw[:, slot, :, :].rearrange("p a (b m) -> p (a b) m", b=2)
                sync.dma_start(dst, src.rearrange("(k p) m -> p k m", p=P)).then_inc(slab_loaded[slot], 16)

            def cols(w, row, rows, col, width=256):
                return w[row:row + rows, bass.ds(col, width)]

            def shift(g, row, rows, times=1):
                src = caches[g][:, :, bass.ds(row + 1, rows)].rearrange("b t n h d -> (b t) n (h d)")
                dst = new_caches[g][:, :, bass.ds(row, rows)].rearrange("b t n h d -> (b t) n (h d)")
                sync.dma_start(dst, src).then_inc(stored, 16)
                n_stored[0] += 16 * times

            def peeled(ph, peel, body):
                before = n_stored[0]
                loop(sync, ph, body, peel)
                looped = ph.iters - peel if ph.iters - peel > 1 else 0
                if looped:
                    per = (n_stored[0] - before) // (peel + 1)
                    n_stored[0] += per * (looped - 1)

            def ffn(f):
                wg, wu, wd = (A[f"ffn{f + 1}_w_{x}"][0] for x in ("gate", "up", "down"))
                for b in range(3):
                    up0 = 48 * (8 * b + 21 * f)
                    down0 = 32 * (4 * b + 8 * f)
                    def up(i, ph=PH[f"up{f}{b}"], b=b, up0=up0):
                        for j in range(8):
                            put(ph, i, j, cols((wg, wu)[j // 4], 512 * (j % 4), 512, BLOCK_TILE0[b] * P + i * 256))
                            if j in (2, 4, 6):
                                shift(2, up0 + i * 48 + 16 * (j // 2 - 1), 16)
                    peeled(PH[f"up{f}{b}"], 2 if (f, b) == (0, 0) else 1 if b == 0 else 0, up)
                    if b == 2:
                        for j in range(4):
                            put(PH[f"single{f}"], 0, j, cols((wg, wu)[j // 2], 1024 * (j % 2), 1024, FF - P, P), mt=P)
                    kts = pair_slabs(f"down{f}{b}")
                    def down(i, ph=PH[f"down{f}{b}"], b=b, down0=down0, kts=kts):
                        for g in range(ph.groups):
                            for s, kt in enumerate(kts):
                                put(ph, i, g * len(kts) + s, cols(wd, BLOCK_TILE0[b] * P + 512 * s, kt * P, (i * ph.groups + g) * 256), kt)
                                if (f, b) in ((0, 0), (0, 1), (1, 0)) and s == 2:
                                    shift(1, down0 + i * 32 + 16 * g, 16)
                    peeled(PH[f"down{f}{b}"], 0, down)

            tails = [(1, r, min(16, 511 - r)) for r in range(384, 511, 16)] + [(0, r, min(16, 127 - r)) for r in range(0, 127, 16)] \
                + [(2, r, min(16, 2047 - r)) for r in range(2016, 2047, 16)]

            for k, loaded in ((0, rows_loaded), (1, right_loaded)):
                half = slice(k * D // 2, (k + 1) * D // 2)
                sync.dma_start(x_rows[:, 0:2, half], A["x_prompt"][0].rearrange("(b p) d -> p b d", p=P)[:, :, half]).then_inc(loaded, 16)
                if k == 0:
                    sync.dma_start(x_rows[0:NS, 2, :], A["x_sample"][:, 0, :]).then_inc(loaded, 16)
            ffn(0)

            w_in = A["w_in"][0]
            for name, col0 in (("u", UOFF), ("q", 0), ("k", NH * HD), ("v", 2 * NH * HD), ("gates_a", GOFF)):
                ph = PH[name]
                for i in range(ph.iters):
                    for j in range(4):
                        put(ph, i, j, cols(w_in, 512 * j, 512, col0 + 256 * i))
                        q_slab = ph.slab0 + 4 * i + j - PH["q"].slab0
                        v_slab = ph.slab0 + 4 * i + j - PH["v"].slab0
                        if name in ("q", "k") and j in (1, 3) and tails:
                            shift(*tails.pop(0))
                        if q_slab == 0:
                            sync.wait_ge(slab_used, q_end("down02"))
                            sync.dma_start(masks[:], A["consts"][:, C_MASK0:NC]).then_inc(const_loaded, 16)
                            sync.wait_ge(tab_stored, 16 * 3 * SC)
                            sync.wait_ge(e_stored, 16 * SC)
                            sync.dma_start(cs[:].rearrange("p a t -> p (a t)"), A["consts"][:, 0:2 * T]).then_inc(const_loaded, 16)
                        if 8 <= q_slab < 32:
                            n = q_slab - 8
                            if n == 0:
                                sync.wait_ge(u4_zero, 1)
                                sync.wait_ge(u_ready, 4)
                            if n < 16:
                                s, jj = n // 4, n % 4
                                dst = u4[32 * s:32 * s + 32, jj::4, NS:NS + NB]
                                src = u_t[32 * jj:32 * jj + 32, :, s * NB:(s + 1) * NB]
                            else:
                                jj, last = n % 4, n >= 20
                                dst = u4[96 * last:96 * last + 32, jj::4, (NS + NB) * last:(NS + NB) * last + NS]
                                src = u_t[32 * jj:32 * jj + 32, :, NT:T]
                            sync.dma_start(dst, src).then_inc(u4_loaded, 16)
                        if 0 <= v_slab - UNIT_LOAD < len(UNITS):
                            n = v_slab - UNIT_LOAD
                            g, b = UNITS[n]
                            if n == 0:
                                sync.wait_ge(u4_loaded, 16 * 24)
                                sync.wait_ge(rows_stored, stored_rows(2))
                                sync.wait_ge(qk_ready, 2 * NH)
                            if n >= 4:
                                sync.wait_ge(prod_ready, n - 3)
                            elif n >= 2:
                                sync.wait_ge(prod_ready, n - 1)
                            dil = GROUPS[g][1]
                            src = caches[g][b, 0].rearrange("(m r) h d -> m r (h d)", r=dil)[:, 0, :]
                            sync.dma_start(ku[n % 4][:], src).then_inc(ku_loaded[n % 4], 16)
                            if n >= 4:
                                sync.wait_ge(prod_ready, n - 1)
                            sync.dma_start(qb[n % 2][:], q_dram[b:b + 1, g * 512:(g + 1) * 512].to_broadcast([P, 512])).then_inc(qb_loaded[n % 2], 16)
            while tails:
                shift(*tails.pop(0))

            def gates_b(i, ph=PH["gates_b"]):
                for j in range(8):
                    put(ph, i, j, cols(w_in, 512 * (j % 4), 512, GOFF + D + i * 512 + 256 * (j // 4)))
                    if j in (1, 5):
                        h = j // 4
                        if below(i, 1):
                            if h == 0:
                                sync.wait_ge(prod_ready, len(UNITS))
                                sync.wait_ge(qk_ready, 2 * NH)
                                sync.wait_ge(rows_stored, stored_rows(8))
                        else:
                            sync.wait_ge(pv_done, 2 * i + h - 1)
                        for g, (_, dil) in enumerate(GROUPS):
                            src = caches[g].rearrange("b t (m r) h d -> b t m r (h d)", r=dil)[bass.ds(2 * i + h, 1), 1, :, 0, :]
                            sync.dma_start(vu[3 * h + g][:], src.rearrange("o m c -> (o m) c")).then_inc(vu_loaded[h], 16)
                    if j in (3, 7):
                        h = j // 4
                        if below(i, 1):
                            if h == 0:
                                sync.wait_ge(att_done, NSLOT)
                        else:
                            sync.wait_ge(y_done, 2 * i + h - 1)
                        src = ssm_tab[bass.ds(2 * i + h, 1)].rearrange("o p c -> (o p) c")
                        sync.dma_start(tab[h][:], src).then_inc(tab_loaded[h], 16)
            loop(sync, PH["gates_b"], gates_b, 1, 1)

            def attn_branch(i, ph=PH["attn_branch"]):
                for g in range(4):
                    put(ph, i, g, cols(A["w_attn_branch"][0], 0, 512, (4 * i + g) * 256))
            loop(sync, PH["attn_branch"], attn_branch, 2)
            sync.wait_ge(y_read, SC)
            moves = [(s, jj) for s in range(STEP) for jj in range(4 if s < STEP - 1 else 2)]

            def move(n):
                for s, jj in moves[:n]:
                    sync.dma_start(yt_v[32 * jj:32 * jj + 32, :, s * NB:(s + 1) * NB],
                                   u4[32 * s:32 * s + 32, jj::4, NS:NS + NB]).then_inc(yt_loaded, 16)
                del moves[:n]

            def glu(i, ph=PH["glu"]):
                for j in range(4):
                    move(8 if (i, j) == (0, 0) else 3)
                    put(ph, i, j, cols(A["glu_w"][0], 512 * (j % 2), 512, (2 * i + j // 2) * 256))
            loop(sync, PH["glu"], glu, 2)

            def ssm_branch(i, ph=PH["ssm_branch"]):
                for j in range(4):
                    put(ph, i, j, cols(A["w_ssm_branch"][0], 512 * (j % 2), 512, (2 * i + j // 2) * 256))
            loop(sync, PH["ssm_branch"], ssm_branch)

            def w_out(i, ph=PH["w_out"]):
                for j in range(8):
                    put(ph, i, j, cols(A["w_out"][0], 512 * (j % 4), 512, (2 * i + j // 4) * 256))
            loop(sync, PH["w_out"], w_out)
            ffn(1)
            for lo, hi in ((0, 4), (4, 7), (7, 8)):
                c0, c1 = 2 * P * lo, 2 * P * hi
                sync.wait_ge(yrow_ready, hi)
                sync.dma_start(O["y_p"][0].rearrange("(b p) d -> p b d", p=P)[:, :, c0:c1], y_rows[:, 0:2, c0:c1]).then_inc(stored, 16)
                sync.dma_start(O["y_s"][:, 0, c0:c1], y_rows[0:NS, 2, c0:c1]).then_inc(stored, 16)
                n_stored[0] += 32
            sync.wait_ge(stored, n_stored[0])

        @block.scalar
        def _(act):
            def split_hi(ph, i, j):
                slot, turn, n = ph.slab(i, j)
                if isinstance(n, int) and n >= TOTAL:
                    return
                act.wait_ge(slab_loaded[slot], 16 * turn + 16)
                if not below(n, RING):
                    act.wait_ge(slab_used, n - (RING - 1))
                act.activation(w_hi[:, slot], raw[:, slot], ACT.Copy).then_inc(hi_ready, 1)

            def split_x(c, odd, cnt, gain0, ready, count):
                act.wait_ge(ready, count)
                if not below(cnt, 2):
                    act.wait_ge(ssq_ready, cnt - 1)
                for u in range(2):
                    ins = act.activation(xg_hi[:, bass.ds(2 * c + u, 1), :], x_t[:, bass.ds(2 * c + u, 1), :],
                                         ACT.Copy, scale=vec[:, bass.ds(gain0 + 2 * c + u, 1)])
                ins.then_inc(xhi_ready, 1)
                act.activation(squares_v[odd][:], x_t[:, bass.ds(2 * c, 2), :], ACT.Square).then_inc(sq_ready, 1)

            def root(r):
                act.wait_ge(mean_ready, r + 1)
                act.activation(sd[:], pb[:, 0, 0:T], ACT.Sqrt, bias=eps_t).then_inc(sd_ready, 1)

            def ssm_params(i, j):
                if i == 0 and j == 5:
                    act.wait_ge(prm_t, 1)
                    act.activation(vec[:, KD:NV], pb[:, 1, P + KD:P + NV], ACT.Copy).then_inc(prm_ready, 1)
                    act.activation(prm[:], pb[:, 1, 0:P], ACT.Copy).then_inc(prm_ready, 1)
                    act.activation(x0_t[:].rearrange("p a b t -> p (a b t)"), pb[:, 2, :], ACT.Copy).then_inc(prm_ready, 1)
                    act.wait_ge(prm_ready, 3)
                    act.activation(scr[:, 0], prm[:, 2 * NTILE:3 * NTILE], ACT.Exp).then_inc(dt_ready, 1)
                if i == 1 and j == 1:
                    act.wait_ge(angles_ready, 1)
                    act.activation(scr[:, 8], scr[:, 1], ACT.Exp).then_inc(trig_ready, 1)
                    act.activation(scr[:, 9:11], scr[:, 3:5], ACT.Sin).then_inc(trig_ready, 1)

            def store_table(i, j):
                def row(i, c0, c1):
                    return ssm_tab[bass.ds(i, 1), :, c0:c1].rearrange("o p c -> (o p) c")
                if j == 1 and not below(i, 1):
                    act.wait_ge(kbig_ready, i)
                    act.dma_start(row(i - 1, TB_K, TB_E), kbig[:].rearrange("p t c -> p (t c)")).then_inc(tab_stored, 16)
                if j == 5:
                    act.wait_ge(bbt_ready, i + 1)
                    act.dma_start(row(i, TB_B, TB_C), bb_t[:]).then_inc(tab_stored, 16)
                if j == 7:
                    act.wait_ge(ca_ready, i + 1)
                    act.wait_ge(ca_im_ready, i + 1)
                    act.dma_start(row(i, TB_C, TB_K).rearrange("p (a c) -> p a c", a=8),
                                  ca5[:].rearrange("p t a c -> p (t a) c")[:, :, 32:]).then_inc(tab_stored, 16)

            def ffn(f):
                names = [f"up{f}0", f"down{f}0", f"up{f}1", f"down{f}1", f"up{f}2", f"single{f}", f"down{f}2"]
                for nm in names:
                    ph = PH[nm]
                    if nm.startswith("down"):
                        kts = pair_slabs(nm)
                        def down(i):
                            for j in range(ph.slabs):
                                split_hi(ph, i, j + LEAD)
                                if nm in NORM_AFTER and j % len(kts) == len(kts) - 1:
                                    r, g = NORM_AFTER[nm], j // len(kts)
                                    c = i * ph.groups + g
                                    split_x(c, g % 2, 8 * r + c, V_NORM[r], evacuated, ph.group(i, g) + 1)
                        loop(act, ph, down, ph.iters if nm == LAST else 0)
                        continue
                    w = 1 if nm.startswith("single") else 2
                    half = ph.slabs // 2
                    def up(i):
                        h, tile0 = HID0[nm] + i, 10 if w == 1 else 2 * i
                        for j in range(ph.slabs):
                            split_hi(ph, i, j + LEAD)
                            if j == 1 and below(i, 1) and nm in ("up00", "up10"):
                                root(2 * f)
                            if below(i, 2) and nm == "up00":
                                ssm_params(i, j)
                            if j == half - 1:
                                act.wait_ge(gate_ready, h + 1)
                                act.activation(silu_v[:, 0:w], gate_v[:, 0:w], ACT.Silu).then_inc(silu_ready, 1)
                            if nm == "up01":
                                store_table(i, j)
                            if nm == "up01" and j == 4:
                                act.wait_ge(bb_done, i + 1)
                                if not below(i, 1):
                                    act.wait_ge(tab_stored, 48 * i)
                                    act.wait_ge(k_done, i)
                                act.activation(bb_t[:], pb[:, 0:2, :].rearrange("p a b -> p (a b)"), ACT.Copy)
                                act.activation(c_t[:].rearrange("p a b c -> p (a b c)"), pb[:, 2, 0:256], ACT.Copy).then_inc(bbt_ready, 1)
                            if j == ph.slabs - 1:
                                act.wait_ge(hid_ready, h + 1)
                                act.activation(act_hi[:, bass.ds(tile0, w), :], hid_v[:, 0:w], ACT.Copy).then_inc(acthi_ready, 1)
                    loop(act, ph, up, 2 if nm == "up00" else 1 if nm in ("up10", "up01") else 0)
                    if nm == "up01":
                        store_table(SC, 1)

            def head_sq_root(x, j):
                if j == 1 and 1 <= x <= NH:
                    act.wait_ge(stat_done, x)
                    if x >= 2:
                        act.wait_ge(t1_ready, 2 * (x - 1))
                    act.activation(head_sd[:], pb[:, 0:2, 0:T], ACT.Sqrt, bias=eps_t).then_inc(head_sd_ready, 1)
                if j == 3 and x < NH:
                    act.wait_ge(evacuated, pair_group(x) + 1)
                    if x:
                        act.wait_ge(stat_done, x)
                    act.activation(sq_v[:], gate_v[:], ACT.Square).then_inc(head_sq, 1)

            def head_rows(x, j):
                e = x - 2 if j == 1 else x - 1
                if not (j == 1 and 0 <= e < 12 or j == 2 and 12 <= e < 18):
                    return
                r, h = e // 2, e % 2
                act.wait_ge(heads_t, e + 1)
                if h == 0 and r:
                    act.wait_ge(rows_stored, stored_rows(r - 1))
                if e in range(6, 12):
                    act.activation(k_rows[:, :, 256 * h:256 * h + 256], pb[:, 2, :].rearrange("p (a b) -> p a b", a=2), ACT.Copy)
                if e >= 12:
                    act.activation(v_tok[:, :, 256 * (e - 12):256 * (e - 11)], pb[:, 2, :].rearrange("p (a b) -> p a b", a=2), ACT.Copy)
                act.activation(s_rows[0:NS, 256 * h:256 * h + 256], pb[0:NS, 3, 0:256], ACT.Copy).then_inc(rows_ready, 1)

            def attention(i, j):
                h = i // 2
                if i % 2 == 0 and j == 1:
                    act.wait_ge(nmax_ready, h + 1)
                    act.activation(probs[:, 0:NG * P], probs[:, 0:NG * P], ACT.Exp, bias=stat[:, 2:3], accum_out=stat[:, 4:5])
                    act.activation(probs[:, NG * P:], probs[:, NG * P:], ACT.Exp, bias=stat[:, 3:4], accum_out=stat[:, 5:6]).then_inc(exp_ready, 1)
                if i % 2 == 0 and j == 3:
                    act.wait_ge(inv_sum, h + 1)
                    act.activation(probs[:, 0:NG * P], probs[:, 0:NG * P], ACT.Copy, scale=stat[:, 6:7])
                    act.activation(probs[:, NG * P:], probs[:, NG * P:], ACT.Copy, scale=stat[:, 7:8]).then_inc(pn_ready, 1)
                if i % 2 == 1 and j == 1:
                    act.wait_ge(p_t, h + 1)
                    act.activation(probs_t[:, 0:8], pb[:, 0:2, :].rearrange("p a (b c) -> p (a b) c", b=4), ACT.Copy)
                    act.activation(probs_t[:, 8], pb[:, 2, 0:P], ACT.Copy).then_inc(pt_ready, 1)
                if i % 2 == 1 and j == 3:
                    act.wait_ge(att_done, h + 1)
                    act.activation(att_v[:, h, 0:NT], pb[:, 3, 0:NT], ACT.Copy).then_inc(att_read, 1)
                if i == 5 and j == 0:
                    act.wait_ge(dmax_ready, 1)
                    act.activation(dec_p[:], pb[0:32, 3, 0:NG * P + NG], ACT.Exp, bias=stat[0:32, 9:10], scale=SCALE,
                                   accum_out=stat[0:32, 10:11]).then_inc(dexp_ready, 1)

            def gates_b(i, ph=PH["gates_b"]):
                for j in range(8):
                    split_hi(ph, i, j + LEAD)
                    if j in (0, 3):
                        h = j // 3
                        k = 2 * i + h
                        act.wait_ge(vu_loaded[h], 48 * i + 48)
                        if below(i, 1) and h == 0:
                            act.wait_ge(dec_ready, 1)
                        for g in range(NG):
                            for hh in range(NSLOT):
                                v = vu[3 * h + g][:, hh * HD:(hh + 1) * HD]
                                ins = act.activation(v, v, ACT.Copy, scale=pt_dec[:, g, bass.ds(NSLOT * k + hh, 1)])
                        ins.then_inc(vs_ready, 1)
                    if j in (4, 7):
                        h = 0 if j == 4 else 1
                        k = 2 * i + h
                        act.wait_ge(y_done, k + 1)
                        act.activation(u4[:, bass.ds(4 * k, 4), 0:NS + NB], pb[:, 2, 0:288].rearrange("p (a b) -> p a b", a=4), ACT.Copy)
                        act.activation(x_fin[:, :, bass.ds(4 * k, 4)], xs[:, :, :, NS + NB], ACT.Copy).then_inc(y_read, 1)
                    if j in (1, 4):
                        h = j // 4
                        k = 2 * i + h
                        act.wait_ge(su_done, k + 1)
                        if below(i, 1) and h == 0:
                            act.wait_ge(xs_zero, 1)
                        else:
                            act.wait_ge(scan_ready, 2 * k)
                            act.wait_ge(y_done, k)
                        s_ps = pb[:, 0:2, 0:288].rearrange("p a (t c) -> p a t c", t=4)
                        act.activation(sv[:].rearrange("p a (t c) -> p a t c", t=4), s_ps[:, :, :, 0:NB], ACT.Copy)
                        act.activation(s_new[:, :, bass.ds(4 * k, 4), :], s_ps[:, :, :, NB:NB + NS], ACT.Copy)
                        for ri in range(2):
                            ins = act.activation(xs[:, ri, :, 0:NS], x0_t[:, ri, :, bass.ds(4 * k, 4)].rearrange("p b t -> p t b"), ACT.Copy)
                        ins.then_inc(sv_ready, 1)
                    if isinstance(i, int) and i == ph.iters - 1 and j == 6:
                        act.wait_ge(pv_read, NS)
                        act.activation(att_hi[:], att_v[:], ACT.Copy).then_inc(att_hi_ready, 1)

            def sigmoid(c):
                act.activation(gates[:, bass.ds(c, 2), :], gates[:, bass.ds(c, 2), :], ACT.Sigmoid).then_inc(sig_ready, 1)

            def vec_load(k, sem):
                name, row, rows = VEC_LOADS[k]
                src = A[name][0]
                if len(src.shape) == 1:
                    src = src.rearrange("(r c) -> r c", c=P)
                act.dma_start(vec_rows[row:row + rows, :], src).then_inc(sem, 16)

            def more_loads(c):
                if c == 2:
                    act.dma_start(log_dt[64:96, :], A["ssm_log_dt"][0].rearrange("(t g) -> t g", g=2)).then_inc(dt_loaded, 16)
                    for row, name in ((0, "ssm_lambda_re"), (32, "ssm_lambda_im")):
                        act.dma_start(prm_rows[row:row + 32, :], A[name][0].rearrange("(t g) s -> t (g s)", g=2)).then_inc(par_loaded, 16)
                if c in (3, 4):
                    for s in (2 * c - 6, 2 * c - 5):
                        act.dma_start(prm_rows[96:128, 32 * s:32 * s + 32], A["ssm_d"][0].rearrange("(t f) -> t f", f=32)).then_inc(par_loaded, 16)
                if c in (5, 6):
                    ri, name = c - 5, ("state_ssm_re", "state_ssm_im")[c - 5]
                    act.dma_start(x0_rows[:, ri], A[name][0].rearrange("(k b) (t g) s -> (b t) k (g s)", k=2, g=2)).then_inc(par_loaded, 16)
                if 3 <= c < 8:
                    vec_load(c - 2, par_loaded)

            vec_load(0, vec_loaded)
            act.wait_ge(const_ready, 1)
            act.wait_ge(vec_ready, 1)
            for c in range(KD // 2):
                split_x(c, c % 2, c, V_NORM[0], x_ready, c + 1)
                if c < LEAD:
                    split_hi(PH["up00"], 0, c)
                more_loads(c)
            ffn(0)
            for name in ("u", "q", "k", "v", "gates_a"):
                ph = PH[name]
                for i in range(ph.iters):
                    x = XQ.get(name, -99) + i
                    for j in range(4):
                        split_hi(ph, i, j + LEAD)
                        if name == "u" and i == 0 and j == 1:
                            root(1)
                        if name != "u":
                            head_sq_root(x, j)
                            head_rows(x, j)
                        if name == "gates_a":
                            attention(i, j)
            loop(act, PH["gates_b"], gates_b, 1, 1)
            act.wait_ge(evacuated, PH["attn_branch"].group0)
            for i in range(2):
                for g in range(4):
                    split_hi(PH["attn_branch"], i, g + LEAD)
                    if i == 0:
                        sigmoid(4 * g)
                        sigmoid(4 * g + 2)
                    elif g in (1, 2):
                        if g == 1:
                            act.wait_ge(yt_loaded, 16 * 14)
                            act.wait_ge(yl_loaded, 16 * 6)
                            act.wait_ge(slab_used, q_end("gates_b"))
                        half = slice(4 * g - 4, 4 * g)
                        act.activation(zs_v[:, half], yt_v[:, half], ACT.Gelu_apprx_tanh).then_inc(gelu_ready, 1)
                        act.wait_ge(gelu_ready, g)
                        act.activation(zs_hi[:, half], zs_v[:, half], ACT.Copy).then_inc(zhi_ready, 1)

            def glu(i, ph=PH["glu"]):
                for j in range(4):
                    split_hi(ph, i, j + LEAD)
                    if j % 2 == 1:
                        g = j // 2
                        c = 2 * i + g
                        act.wait_ge(slab_used, ph.slab(i, j)[2] + 1)
                        act.wait_ge(evacuated, ph.group(i, g))
                        for u in range(2):
                            ins = act.activation(gate_v[:, u], pa[:, 2 * ph.banks(i, g) + u, 0:T], ACT.Sigmoid,
                                                 bias=vec[:, V_GLU + 2 * c + u:V_GLU + 2 * c + u + 1])
                        ins.then_inc(sgl_ready, 1)
                        act.wait_ge(evacuated, ph.group(i, g) + 1)
                        act.activation(s_hi[:, 2 * c:2 * c + 2], up_v[:], ACT.Copy).then_inc(shi_ready, 1)
                    if i == 1 and j == 0:
                        act.wait_ge(st_t, 1)
                        act.activation(st_rows[:, 0:4, :], pb[:, 0, :].rearrange("p (a b) -> p a b", a=4), ACT.Copy)
                        act.activation(st_rows[0:32, 4:6, :], pb[0:32, 1, 0:256].rearrange("p (a b) -> p a b", a=2),
                                       ACT.Copy).then_inc(st_rows_ready, 1)
            loop(act, PH["glu"], glu, 2)

            def merged_hi(c):
                act.wait_ge(m_ready, c + 1)
                act.activation(act_hi[:, bass.ds(2 * c, 2), :], hid_v[:], ACT.Copy).then_inc(acthi_ready, 1)

            def ssm_branch(i, ph=PH["ssm_branch"]):
                for j in range(4):
                    split_hi(ph, i, j + LEAD)
                    if j % 2 == 0:
                        sigmoid(KD + 2 * (2 * i + j // 2))
                        if not (below(i, 1) and j == 0):
                            merged_hi(2 * i + j // 2 - 1)
            loop(act, PH["ssm_branch"], ssm_branch, 1)
            merged_hi(KD // 2 - 1)

            def w_out(i, ph=PH["w_out"]):
                for j in range(8):
                    split_hi(ph, i, j + LEAD)
                    if j % 4 == 3:
                        c = 2 * i + j // 4
                        split_x(c, j // 4, 16 + c, V_NORM[2], evacuated, ph.group(i, j // 4) + 1)
            loop(act, PH["w_out"], w_out)
            ffn(1)

        @block.vector
        def _(dve):
            def split_lo(ph, i, j):
                slot, turn, n = ph.slab(i, j)
                if isinstance(n, int) and n >= TOTAL:
                    return
                dve.wait_ge(hi_ready, n + 1)
                dve.tensor_tensor(w_lo[:, slot], raw[:, slot], w_hi[:, slot].bitcast(f32), ALU.subtract).then_inc(lo_ready, 1)

            def split_x(c, cnt, gain0):
                dve.wait_ge(xhi_ready, cnt + 1)
                for u in range(2):
                    k = 2 * c + u
                    ins = dve.scalar_tensor_tensor(xg_lo[:, bass.ds(k, 1), :], x_t[:, bass.ds(k, 1), :],
                                                   vec[:, bass.ds(gain0 + k, 1)], xg_hi[:, bass.ds(k, 1), :].bitcast(f32),
                                                   ALU.mult, ALU.subtract)
                ins.then_inc(xlo_ready, 1)

            def times_rstd(out, ph, i, g, j, w=2):
                b = 2 * ph.banks(i, g)
                dve.wait_ge(slab_used, ph.slab(i, j)[2] + 1)
                return dve.tensor_tensor(out, pa[:, b:b + w, 0:T], rstd[:, None, :].to_broadcast([P, w, T]), ALU.mult)

            def root(r):
                dve.wait_ge(sd_ready, r + 1)
                dve.reciprocal(rstd[:], sd[:]).then_inc(rstd_ready, 1)
                dve.wait_ge(rstd_ready, r + 1)

            def residual(ph, i, g, j, scale):
                c = i * ph.groups + g
                b = 2 * ph.banks(i, g)
                dve.wait_ge(slab_used, ph.slab(i, j)[2] + 1)
                dve.scalar_tensor_tensor(x_t[:, bass.ds(2 * c, 2), :], pa[:, b:b + 2, 0:T], scale,
                                         x_t[:, bass.ds(2 * c, 2), :], ALU.mult, ALU.add).then_inc(evacuated, 1)
                return c

            def ssm_table(i, j):
                if j == 5:
                    dve.wait_ge(bbt_ready, i + 1)
                    if not below(i, 1):
                        dve.wait_ge(tab_stored, 48 * i)
                        dve.wait_ge(k_done, i)
                    def lags(k):
                        return ca_tmp[:, k].rearrange("p t (n f) -> p t n f", n=LAGS)
                    def c_of(ri):
                        return c_t[:, ri, :, None, :].to_broadcast([P, 4, LAGS, 32])
                    def pow_of(t):
                        return t[:, bass.ds(4 * i, 4), :, None].to_broadcast([P, 4, LAGS, 32])
                    if not below(i, 1):
                        dve.wait_ge(ca_ready, i)
                    dve.tensor_tensor(lags(0), c_of(0), pow_of(pw[:, 0]), ALU.mult).then_inc(ca_step, 1)
                    dve.tensor_tensor(lags(1), c_of(1), pow_of(pw[:, 1]), ALU.mult).then_inc(ca_step, 1)
                    dve.wait_ge(ca_step, 2 * i + 2)
                    dve.tensor_tensor(ca5[:, :, 0, :], ca_tmp[:, 0], ca_tmp[:, 1], ALU.subtract).then_inc(ca_ready, 1)
                if j == 7:
                    dve.wait_ge(k_done, i + 1)
                    for s in range(STEP):
                        dve.tensor_copy(kbig[32 * s:32 * s + 32, :, 32 * s:P],
                                        pb[0:32, 3, :].rearrange("p (t c) -> p t c", t=4)[:, :, 0:P - 32 * s]).then_inc(k_step, 1)
                    dve.wait_ge(k_step, 4 * i + 4)
                    for t in range(4):
                        ins = dve.scalar_tensor_tensor(kbig[:, t, :], ident[:], prm[:, bass.ds(3 * NTILE + 4 * i + t, 1)],
                                                       kbig[:, t, :], ALU.mult, ALU.add)
                    ins.then_inc(kbig_ready, 1)

            def rows_back(c):
                dve.wait_ge(yt_ready, c + 1)
                dve.tensor_copy(y_rows[:, 0:2, 256 * c:256 * c + 256], pb[:, 0:2, 0:256])
                dve.tensor_copy(y_rows[0:NS, 2, 256 * c:256 * c + 256], pb[0:NS, 2, 0:256]).then_inc(yrow_ready, 1)

            def ffn(f):
                for nm in [f"up{f}0", f"down{f}0", f"up{f}1", f"down{f}1", f"up{f}2", f"single{f}", f"down{f}2"]:
                    ph = PH[nm]
                    if nm.startswith("down"):
                        kts = pair_slabs(nm)
                        def down(i):
                            for j in range(ph.slabs):
                                split_lo(ph, i, j + LEAD)
                                if nm == LAST and j % len(kts) == 1 and j > 1:
                                    rows_back(i * ph.groups + j // len(kts) - 1)
                                if nm == LAST and j == 1 and i:
                                    rows_back(i * ph.groups - 1)
                                if j % len(kts) == len(kts) - 1:
                                    c = residual(ph, i, j // len(kts), j, 0.5)
                                    if nm in NORM_AFTER:
                                        split_x(c, 8 * NORM_AFTER[nm] + c, V_NORM[NORM_AFTER[nm]])
                        loop(dve, ph, down, ph.iters if nm == LAST else 0)
                        continue
                    w = 1 if nm.startswith("single") else 2
                    half = ph.slabs // 2
                    def up(i):
                        h, a, tile0 = HID0[nm] + i, ACT0[nm] + i, 10 if w == 1 else 2 * i
                        for j in range(ph.slabs):
                            split_lo(ph, i, j + LEAD)
                            if j == 1 and below(i, 1) and nm in ("up00", "up10"):
                                root(2 * f)
                            if nm == "up00" and below(i, 1) and j == 7:
                                dve.wait_ge(den_ready, 1)
                                dve.reciprocal(scr[:, 12], scr[:, 11]).then_inc(inv_ready, 1)
                            if nm == "up01":
                                ssm_table(i, j)
                            if j == half - 1:
                                b = 2 * ph.banks(i, 0)
                                dve.wait_ge(slab_used, ph.slab(i, j)[2] + 1)
                                dve.tensor_tensor(gate_v[:, 0:w], pa[:, b:b + w, 0:T], rstd[:, None, :].to_broadcast([P, w, T]),
                                                  ALU.mult).then_inc(gate_ready, 1)
                                dve.wait_ge(gate_ready, h + 1)
                                dve.sem_inc(evacuated, 1)
                            if j == ph.slabs - 1:
                                times_rstd(up_v[:, 0:w], ph, i, 1, j, w).then_inc(evacuated, 1)
                                dve.wait_ge(evacuated, ph.group(i, 1) + 1)
                                dve.wait_ge(silu_ready, h + 1)
                                dve.tensor_tensor(hid_v[:, 0:w], silu_v[:, 0:w], up_v[:, 0:w], ALU.mult).then_inc(hid_ready, 1)
                                dve.wait_ge(acthi_ready, a + 1)
                                dve.tensor_tensor(act_lo[:, bass.ds(tile0, w), :], hid_v[:, 0:w],
                                                  act_hi[:, bass.ds(tile0, w), :].bitcast(f32), ALU.subtract).then_inc(actlo_ready, 1)
                    loop(dve, ph, up, 2 if nm == "up00" else 1 if nm in ("up10", "up01") else 0)

            def permuted(ap):
                return ap[:, :, 0:NT].rearrange("p u (c s) -> p u s c", s=STEP)

            def u_out(ph, i):
                b = 2 * ph.banks(i, 0)
                dve.wait_ge(slab_used, ph.slab(i, 3)[2] + 1)
                if i == 0:
                    dve.wait_ge(tab_stored, 16 * 3 * SC)
                    dve.wait_ge(e_stored, 16 * SC)
                dst = u_t[:, 2 * i:2 * i + 2, 0:NT].rearrange("p u (s c) -> p u s c", s=STEP)
                dve.tensor_tensor(dst, permuted(pa[:, b:b + 2, :]),
                                  rstd[:, None, 0:NT].to_broadcast([P, 2, NT]).rearrange("p u (c s) -> p u s c", s=STEP), ALU.mult)
                dve.tensor_tensor(u_t[:, 2 * i:2 * i + 2, NT:T], pa[:, b:b + 2, NT:T],
                                  rstd[:, None, NT:T].to_broadcast([P, 2, NS]), ALU.mult).then_inc(u_ready, 1)
                dve.wait_ge(u_ready, i + 1)
                dve.sem_inc(evacuated, 1)

            def head(x, u):
                dve.wait_ge(head_sd_ready, x + 1)
                dve.reciprocal(head_sd[:, u], head_sd[:, u]).then_inc(head_inv, 1)
                dve.wait_ge(head_inv, 2 * x + u + 1)
                if x and u == 0:
                    dve.wait_ge(qk_ready, 2 * x)
                dve.scalar_tensor_tensor(up_v[:, u], gate_v[:, u], vec[:, V_HEAD + 2 * x + u:V_HEAD + 2 * x + u + 1],
                                         head_sd[:, u], ALU.mult, ALU.mult).then_inc(t1_ready, 1)

            def attention(i, j):
                h = i // 2
                if i % 2 == 0 and j == 0:
                    dve.wait_ge(s_done, h + 1)
                    if h:
                        dve.wait_ge(p_t, h)
                    n0 = NG * P
                    dve.scalar_tensor_tensor(probs[:, 0:n0], pb[:, 0, 0:n0], SCALE, masks[:, 0:n0], ALU.mult, ALU.add)
                    dve.scalar_tensor_tensor(probs[:, n0:], pb[:, 1:3, :].rearrange("p a b -> p (a b)")[:, 0:NG * NT], SCALE,
                                             masks[:, n0:], ALU.mult, ALU.add).then_inc(sm_ready, 1)
                    dve.wait_ge(sm_ready, h + 1)
                    dve.tensor_reduce(stat[:, 0:1], probs[:, 0:n0], AX.X, ALU.max)
                    dve.tensor_reduce(stat[:, 1:2], probs[:, n0:], AX.X, ALU.max).then_inc(sm_step, 1)
                    dve.wait_ge(sm_step, h + 1)
                    dve.tensor_scalar(stat[:, 2:4], stat[:, 0:2], -1.0, None, ALU.mult).then_inc(nmax_ready, 1)
                if i % 2 == 0 and j == 2:
                    dve.wait_ge(exp_ready, h + 1)
                    dve.reciprocal(stat[:, 6:8], stat[:, 4:6]).then_inc(inv_sum, 1)

            dstep = Chain(dve, dec_step)

            def decode(i, j):
                n = NG * P
                if (i, j) == (4, 3):
                    dve.wait_ge(ds_done, 1)
                    dstep(dve.tensor_reduce(stat[0:32, 8:9], pb[0:32, 3, 0:n + NG], AX.X, ALU.max))
                    dve.tensor_scalar(stat[0:32, 9:10], stat[0:32, 8:9], -SCALE, None, ALU.mult).then_inc(dmax_ready, 1)
                if (i, j) == (5, 1):
                    dve.wait_ge(dexp_ready, 1)
                    dstep(dve.reciprocal(stat[0:32, 11:12], stat[0:32, 10:11]))
                    dstep(dve.tensor_scalar(dec_p[:], dec_p[:], stat[0:32, 11:12], None, ALU.mult))
                    for g in range(NG):
                        ins = dve.tensor_scalar(dec_diag[:, g, :], ident[0:32, 0:32], dec_p[:, n + g:n + g + 1], None, ALU.mult)
                    ins.then_inc(diag_ready, 1)
                if (i, j) == (6, 3):
                    dve.wait_ge(dt_done, 1)
                    dve.wait_ge(v_new_ready, 6)
                    dve.tensor_copy(pt_dec[:].rearrange("p a b -> p (a b)"), pb[:, 3, 0:96])
                    dstep(dve.tensor_tensor(att_new[:].rearrange("p g (b h) -> p g b h", b=NS),
                                            pb[:, 3, P:P + 96].rearrange("p (g b h) -> p g b h", g=NG, b=NS),
                                            v_new[:].rearrange("p (g h) b -> p g b h", g=NG), ALU.mult))
                    dstep(dve.tensor_tensor(att_new[:, 0], att_new[:, 0], att_new[:, 1], ALU.add))
                    dve.tensor_tensor(att_new[:, 0], att_new[:, 0], att_new[:, 2], ALU.add).then_inc(dec_ready, 1)

            def gates_b(i, ph=PH["gates_b"]):
                for j in range(8):
                    split_lo(ph, i, j + LEAD)
                    if j in (1, 4):
                        h = j // 4
                        k = 2 * i + h
                        E, M = tab[h][:, E0:M0].rearrange("p (a c) -> p a c", a=2), tab[h][:, M0:TB]
                        dve.wait_ge(sv_ready, k + 1)
                        if not (below(i, 1) and h == 0):
                            dve.wait_ge(xi_ready, k)
                        dve.tensor_tensor(d_tmp[:, 0], sv[:, 1], E[:, 0], ALU.mult).then_inc(zi_step, 1)
                        dve.tensor_tensor(d_tmp[:, 1], sv[:, 0], E[:, 1], ALU.mult).then_inc(zi_step, 1)
                        dve.wait_ge(zi_step, 5 * k + 2)
                        dve.tensor_tensor(z_in[:, 1], d_tmp[:, 0], d_tmp[:, 1], ALU.subtract).then_inc(zi_step, 1)
                        dve.wait_ge(zi_step, 5 * k + 3)
                        if not (below(i, 1) and h == 0):
                            dve.wait_ge(xr_ready, k)
                        dve.tensor_tensor_scan(z_out[:, 1], M, z_in[:, 1], 0.0, ALU.mult, ALU.add).then_inc(scan_ready, 1)
                        dve.wait_ge(zr_ready, k + 1)
                        dve.tensor_tensor_scan(z_out[:, 0], M, z_in[:, 0], 0.0, ALU.mult, ALU.add).then_inc(scan_ready, 1)
                    if j in (2, 5):
                        h = j // 4
                        k = 2 * i + h
                        E = tab[h][:, E0:M0].rearrange("p (a c) -> p a c", a=2)
                        dve.wait_ge(scan_ready, 2 * k + 2)
                        dve.tensor_tensor(d_tmp[:, 0], z_out[:, 0], E[:, 1], ALU.mult).then_inc(zi_step, 1)
                        dve.tensor_tensor(d_tmp[:, 1], z_out[:, 1], E[:, 0], ALU.mult).then_inc(zi_step, 1)
                        dve.wait_ge(zi_step, 5 * k + 5)
                        if below(i, 1) and h == 0:
                            dve.wait_ge(xs_zero, 1)
                        else:
                            dve.wait_ge(y_read, k)
                        dve.tensor_tensor(xs[:, 1, :, NS + 1:NS + 1 + NB], d_tmp[:, 0].rearrange("p (t c) -> p t c", t=4),
                                          d_tmp[:, 1].rearrange("p (t c) -> p t c", t=4), ALU.add).then_inc(xi_ready, 1)
                    if j in (2, 6):
                        h = j // 4
                        k = 2 * i + h
                        dve.wait_ge(pv_done, k + 1)
                        dve.tensor_tensor(att_v[:, :, bass.ds(NT + k, 1)], pb[:, 3, 0:NSLOT, None],
                                          att_new[:, 0, bass.ds(NSLOT * k, NSLOT), None], ALU.add).then_inc(pv_read, 1)
                    if isinstance(i, int) and i == ph.iters - 1 and j == 7:
                        dve.wait_ge(att_hi_ready, 1)
                        dve.wait_ge(scan_ready, 2 * SC)
                        dve.tensor_tensor(att_lo[:], att_v[:], att_hi[:].bitcast(f32), ALU.subtract).then_inc(att_lo_ready, 1)
                    if j % 4 == 3:
                        g = j // 4
                        if below(i, 1) and g == 0:
                            dve.wait_ge(att_done, NSLOT)
                        times_rstd(gates[:, bass.ds(KD + 4 * i + 2 * g, 2), :], ph, i, g, j).then_inc(evacuated, 1)

            dve.memset(eps_t, EPS)
            dve.memset(head_w[:], 1.0 / HD)
            dve.memset(ones[:], 1.0)
            dve.memset(mean_w[:], 1.0 / D).then_inc(const_ready, 1)
            dve.wait_ge(vec_t, 1)
            dve.tensor_copy(vec[:, 0:KD], pb[:, 3, 0:KD]).then_inc(vec_ready, 1)
            dve.wait_ge(vec_ready, 1)
            def x_out(c):
                dve.wait_ge(rows_t, c + 1)
                dve.tensor_copy(x_t[:, 2 * c:2 * c + 2, :], pb[:, 2 * (c % 2):2 * (c % 2) + 2, 0:T]).then_inc(x_ready, 1)

            x_out(0)
            for c in range(KD // 2):
                if c + 1 < KD // 2:
                    x_out(c + 1)
                split_x(c, c, V_NORM[0])
                if c < LEAD:
                    split_lo(PH["up00"], 0, c)
            dve.wait_ge(dt_loaded, 16)
            dve.tensor_copy(prm_rows[64:96, :].rearrange("p (g s) -> p g s", g=2),
                            log_dt[64:96, :, None].to_broadcast([32, 2, 64])).then_inc(dt_rows, 1)
            ffn(0)
            for name in ("u", "q", "k", "v", "gates_a"):
                ph = PH[name]
                for i in range(ph.iters):
                    x = XQ.get(name, -99) + i
                    for j in range(4):
                        split_lo(ph, i, j + LEAD)
                        if name == "u" and i == 0 and j == 1:
                            root(1)
                        if name == "gates_a":
                            attention(i, j)
                            decode(i, j)
                        if j >= 2 and 1 <= x <= NH:
                            head(x - 1, j - 2)
                        n = ph.slab0 + 4 * i + j - PH["v"].slab0 - UNIT_USE
                        if 0 <= n < len(UNITS):
                            g, b = UNITS[n]
                            dve.wait_ge(prod_ready, n + 1)
                            dve.tensor_reduce(sc_dec[:, g, b, :], prod[n % 2][:], AX.X, ALU.add).then_inc(sc_ready, 1)
                        if j == 3 and name == "u":
                            u_out(ph, i)
                        elif j == 3 and name == "gates_a":
                            times_rstd(gates[:, 2 * i:2 * i + 2, :], ph, i, 0, j).then_inc(evacuated, 1)
                        elif j == 3:
                            if 1 <= x <= NH:
                                dve.wait_ge(t1_ready, 2 * x)
                            elif x > NH:
                                dve.wait_ge(heads_t, x)
                            times_rstd(gate_v[:], ph, i, 0, j).then_inc(evacuated, 1)
                            if name == "v":
                                dve.wait_ge(evacuated, pair_group(x) + 1)
                                dve.tensor_copy(v_new[:, 2 * i:2 * i + 2, :], gate_v[:, :, NT:T]).then_inc(v_new_ready, 1)
            loop(dve, PH["gates_b"], gates_b, 1, 1)
            ph = PH["attn_branch"]
            for i in range(2):
                for g in range(4):
                    split_lo(ph, i, g + LEAD)
                    c, b = 4 * i + g, 2 * ph.banks(i, g)
                    dve.wait_ge(slab_used, ph.slab(i, g)[2] + 1)
                    dve.wait_ge(sig_ready, c + 1)
                    dve.tensor_tensor(gates[:, 2 * c:2 * c + 2, :], pa[:, b:b + 2, 0:T], gates[:, 2 * c:2 * c + 2, :],
                                      ALU.mult).then_inc(evacuated, 1)
                    if i == 1 and g >= 2:
                        half = slice(4 * g - 8, 4 * g - 4)
                        dve.wait_ge(zhi_ready, g - 1)
                        dve.tensor_tensor(zs_lo[:, half], zs_v[:, half], zs_hi[:, half].bitcast(f32), ALU.subtract).then_inc(zlo_ready, 1)
            ph = PH["glu"]
            for i in range(2):
                for j in range(4):
                    split_lo(ph, i, j + LEAD)
                    if j % 2 == 1:
                        c = 2 * i + j // 2
                        dve.wait_ge(sgl_ready, c + 1)
                        if c:
                            dve.wait_ge(slo_ready, c)
                        dve.tensor_tensor(up_v[:], zs_v[:, 2 * c:2 * c + 2], gate_v[:], ALU.mult).then_inc(evacuated, 1)
                        dve.wait_ge(shi_ready, c + 1)
                        dve.tensor_tensor(s_lo[:, 2 * c:2 * c + 2], up_v[:], s_hi[:, 2 * c:2 * c + 2].bitcast(f32),
                                          ALU.subtract).then_inc(slo_ready, 1)

            def merged_lo(c):
                dve.wait_ge(acthi_ready, ACT0["ssm_branch"] + c + 1)
                dve.tensor_tensor(act_lo[:, bass.ds(2 * c, 2), :], hid_v[:], act_hi[:, bass.ds(2 * c, 2), :].bitcast(f32),
                                  ALU.subtract).then_inc(actlo_ready, 1)

            def ssm_branch(i, ph=PH["ssm_branch"]):
                for j in range(4):
                    split_lo(ph, i, j + LEAD)
                    if j % 2 == 0 and not (below(i, 1) and j == 0):
                        merged_lo(2 * i + j // 2 - 1)
                    if j % 2 == 1:
                        c, b = 2 * i + j // 2, 2 * ph.banks(i, j // 2)
                        sig = gates[:, bass.ds(KD + 2 * c, 2), :]
                        dve.wait_ge(slab_used, ph.slab(i, j)[2] + 1)
                        dve.wait_ge(sig_ready, 8 + c + 1)
                        if not below(c, 1):
                            dve.wait_ge(m_ready, c)
                        dve.tensor_tensor(up_v[:, :, 0:NT].rearrange("p u (c s) -> p u s c", s=STEP),
                                          pa[:, b:b + 2, 0:NT].rearrange("p u (s c) -> p u s c", s=STEP),
                                          sig[:, :, 0:NT].rearrange("p u (c s) -> p u s c", s=STEP), ALU.mult).then_inc(prod_s, 1)
                        dve.tensor_tensor(up_v[:, :, NT:T], pa[:, b:b + 2, NT:T], sig[:, :, NT:T], ALU.mult).then_inc(evacuated, 1)
                        dve.wait_ge(evacuated, ph.group(i, j // 2) + 1)
                        dve.wait_ge(prod_s, c + 1)
                        if not below(c, 1):
                            dve.wait_ge(actlo_ready, ACT0["ssm_branch"] + c)
                        dve.tensor_tensor(hid_v[:], up_v[:], gates[:, bass.ds(2 * c, 2), :], ALU.add).then_inc(m_ready, 1)
            loop(dve, PH["ssm_branch"], ssm_branch, 1)
            merged_lo(KD // 2 - 1)
            dve.wait_ge(x_back, 16)

            def w_out(i, ph=PH["w_out"]):
                for j in range(8):
                    split_lo(ph, i, j + LEAD)
                    if j % 4 == 3:
                        c = residual(ph, i, j // 4, j, 1.0)
                        split_x(c, 16 + c, V_NORM[2])
            loop(dve, PH["w_out"], w_out)
            ffn(1)
            rows_back(KD // 2 - 1)

        @block.tensor
        def _(pe):
            def tile_products(out, slot, kk, c, hi, lo, first, last, m0=None):
                if m0 is None:
                    m0 = P * c
                wh, wl = w_hi[:, slot, kk, m0:m0 + P], w_lo[:, slot, kk, m0:m0 + P]
                pe.matmul(out, wh, hi, start=first, stop=False)
                pe.matmul(out, wh, lo, start=False, stop=False)
                return pe.matmul(out, wl, hi, start=False, stop=last)

            def slab_products(ph, i, j, g, hi, lo, k0, kt, first, last):
                slot, turn, n = ph.slab(i, j)
                pe.wait_ge(lo_ready, n + 1)
                b = 2 * ph.banks(i, g)
                for c in range(2):
                    for kk in range(kt):
                        ins = tile_products(pa[:, b + c, 0:T], slot, kk, c, hi[:, k0 + kk, :], lo[:, k0 + kk, :],
                                            first and kk == 0, last and kk == kt - 1)
                ins.then_inc(slab_used, 1)

            def open_group(ph, i, g):
                q = ph.group(i, g)
                if not below(q, 2):
                    pe.wait_ge(evacuated, q - 1)

            def mean_square(r):
                if r == 0:
                    pe.wait_ge(x_ready, KD // 2)
                pe.wait_ge(ssq_ready, 8 * (r + 1))
                pe.matmul(pb[:, 0, 0:T], mean_w[:], ssq[:, 0, :], start=True, stop=False)
                pe.matmul(pb[:, 0, 0:T], mean_w[:], ssq[:, 1, :], start=False, stop=True).then_inc(mean_ready, 1)

            def turn_in(c):
                if c == 0:
                    pe.wait_ge(rows_loaded, 32)
                if c == 1:
                    pe.wait_ge(vec_ready, 1)
                if c == 4:
                    pe.wait_ge(right_loaded, 16)
                if c >= 2:
                    pe.wait_ge(x_ready, c - 1)
                for u in range(2):
                    k, bank = 2 * c + u, 2 * (c % 2) + u
                    for t in range(2):
                        pe.transpose(pb[:, bank, t * P:(t + 1) * P], x_rows[:, t, k * P:(k + 1) * P], ident[:])
                    ins = pe.transpose(pb[:, bank, 2 * P:T], x_rows[0:NS, 2, k * P:(k + 1) * P], ident[0:NS, 0:NS])
                ins.then_inc(rows_t, 1)

            def turn_back(c):
                pe.wait_ge(evacuated, PH[LAST].group0 + c + 1)
                if c:
                    pe.wait_ge(yrow_ready, c)
                for u in range(2):
                    for t in range(3):
                        n = P if t < 2 else NS
                        ins = pe.transpose(pb[0:n, t, u * P:(u + 1) * P], x_t[:, 2 * c + u, t * P:t * P + n], ident[:])
                ins.then_inc(yt_ready, 1)

            def ssm_setup(i, j):
                if i == 0 and j == 4:
                    pe.wait_ge(par_loaded, 16 * (8 + len(VEC_LOADS) - 1))
                    pe.wait_ge(dt_rows, 1)
                    pe.transpose(pb[:, 1, 0:P], prm_rows[:], ident[:])
                    pe.transpose(pb[:, 1, P:P + NV], vec_rows[0:NV, :], ident[0:NV, 0:NV])
                    for ri in range(2):
                        for blk in range(2):
                            ins = pe.transpose(pb[:, 2, (2 * ri + blk) * P:(2 * ri + blk + 1) * P], x0_rows[:, ri, blk, :], ident[:])
                    ins.then_inc(prm_t, 1)

            def ssm_table(i, j):
                if j == 3:
                    pe.wait_ge(pre_ready, i + 1)
                    if not below(i, 1):
                        pe.wait_ge(bbt_ready, i)
                    for t in range(4):
                        for ri in range(2):
                            m = 2 * t + ri
                            pe.transpose(pb[:, m // 4, (m % 4) * P:(m % 4 + 1) * P], pre[:, ri, t].rearrange("p s g c -> p (s g c)"), ident[:])
                    for ri in range(2):
                        ins = pe.transpose(pb[:, 2, ri * P:(ri + 1) * P], c_exp[:, ri].rearrange("p g s -> p (g s)"), ident[:])
                    ins.then_inc(bb_done, 1)
                if j == 7:
                    pe.wait_ge(ca_ready, i + 1)
                    pe.wait_ge(ca_im_ready, i + 1)
                    if not below(i, 1):
                        pe.wait_ge(kbig_ready, i)
                    for t in range(4):
                        for ri in range(2):
                            ins = pe.matmul(pb[0:32, 3, t * P:(t + 1) * P], pre[:, ri, t, STEP - 1].rearrange("p g c -> p (g c)"),
                                            ca5[:, t, ri, 0:P], start=ri == 0, stop=ri == 1)
                    ins.then_inc(k_done, 1)

            def ffn(f):
                xn = 2 * f
                for nm in [f"up{f}0", f"down{f}0", f"up{f}1", f"down{f}1", f"up{f}2", f"single{f}", f"down{f}2"]:
                    ph = PH[nm]
                    if nm.startswith("down"):
                        kts, up0 = pair_slabs(nm), ACT0["up" + nm[4:]]
                        def down(i):
                            for g in range(ph.groups):
                                open_group(ph, i, g)
                                for s, kt in enumerate(kts):
                                    if g == 0:
                                        pe.wait_ge(actlo_ready, up0 + 2 * s + 2)
                                    slab_products(ph, i, g * len(kts) + s, g, act_hi, act_lo, KS * s, kt, s == 0, s == len(kts) - 1)
                                    if nm == LAST and s == 0 and i + g:
                                        turn_back(i * ph.groups + g - 1)
                        loop(pe, ph, down, ph.iters if nm == LAST else 0)
                    elif nm.startswith("single"):
                        for j in range(4):
                            g, kh = j // 2, j % 2
                            if kh == 0:
                                open_group(ph, 0, g)
                            slot, turn, n = ph.slab(0, j)
                            pe.wait_ge(lo_ready, n + 1)
                            for kk in range(8):
                                k = kh * 8 + kk
                                ins = tile_products(pa[:, 2 * ph.banks(0, g), 0:T], slot, kk // 2, 0, xg_hi[:, k, :], xg_lo[:, k, :],
                                                    k == 0, k == KD - 1, m0=P * (kk % 2))
                            ins.then_inc(slab_used, 1)
                    else:
                        def up(i):
                            for j in range(8):
                                g, s = j // 4, j % 4
                                if nm == "up00" and below(i, 1):
                                    for c in ((), (5, 6), (7,))[j] if j < 3 else ():
                                        turn_in(c)
                                if s == 0:
                                    open_group(ph, i, g)
                                if g == 0:
                                    pe.wait_ge(xlo_ready, 8 * xn + 2 * s + 2)
                                slab_products(ph, i, j, g, xg_hi, xg_lo, KS * s, KS, s == 0, s == 3)
                                if j == 2 and below(i, 1) and nm in ("up00", "up10"):
                                    mean_square(xn)
                                if nm == "up00" and below(i, 1):
                                    ssm_setup(i, j)
                                if nm == "up01":
                                    ssm_table(i, j)
                        loop(pe, ph, up, 2 if nm == "up00" else 1 if nm in ("up10", "up01") else 0)

            def head_stats(x):
                pe.wait_ge(head_sq, x)
                pe.wait_ge(*((sd_ready, 2) if x == 1 else (head_sd_ready, x - 1)))
                for u in range(2):
                    ins = pe.matmul(pb[:, u, 0:T], head_w[:], sq_v[:, u, :], start=True, stop=True)
                ins.then_inc(stat_done, 1)

            def heads_to_rows(x, j):
                e = x - 2 if j == 1 else x - 1
                if not (j == 1 and 0 <= e < 12 or j == 2 and 12 <= e < 18):
                    return
                if e < 12:
                    pe.wait_ge(qk_ready, 2 * e + 2)
                else:
                    pe.wait_ge(evacuated, pair_group(e) + 1)
                if e:
                    pe.wait_ge(rows_ready, e)
                if e == 17:
                    pe.wait_ge(sm_ready, 1)
                for u in range(2):
                    src = qk[:, 2 * e + u, :] if e < 12 else gate_v[:, u, :]
                    if e >= 6:
                        for t in range(2):
                            pe.transpose(pb[:, 2, 256 * t + P * u:256 * t + P * (u + 1)], src[:, t * P:(t + 1) * P], ident[:])
                    ins = pe.transpose(pb[0:NS, 3, P * u:P * (u + 1)], src[:, NT:T], ident[:])
                ins.then_inc(heads_t, 1)

            def attention(i, j):
                h = i // 2
                if i % 2 == 0 and j == 0:
                    pe.wait_ge(qk_ready, 2 * NH)
                    pe.wait_ge(*((rows_ready, 17) if h == 0 else (pt_ready, h)))
                    for g in range(NG):
                        q, k = qk[:, NSLOT * g + h, :], qk[:, NH + NSLOT * g + h, :]
                        pe.matmul(pb[:, 0, g * P:(g + 1) * P], q[:, 0:P], k[:, 0:P], start=True, stop=True)
                        ins = pe.matmul(pb[:, 1 + g // 2, (g % 2) * NT:(g % 2 + 1) * NT], q[:, P:NT], k[:, 0:NT], start=True, stop=True)
                    ins.then_inc(s_done, 1)
                if i % 2 == 1 and j == 0:
                    pe.wait_ge(pn_ready, h + 1)
                    if h == 0:
                        pe.wait_ge(rows_ready, 18)
                    for m in range(9):
                        ins = pe.transpose(pb[:, m // 4, (m % 4) * P:(m % 4 + 1) * P], probs[:, m * P:(m + 1) * P], ident[:])
                    ins.then_inc(p_t, 1)
                if i % 2 == 1 and j == 2:
                    pe.wait_ge(pt_ready, h + 1)
                    if h:
                        pe.wait_ge(att_read, h)
                    if h == 3:
                        pe.wait_ge(dec_ready, 1)
                    if h == 2:
                        pe.wait_ge(dexp_ready, 1)
                    for g in range(NG):
                        v0 = (NSLOT * g + h) * HD
                        pe.matmul(pb[:, 3, 0:P], v_tok[:, 0, v0:v0 + HD], probs_t[:, g, :], start=g == 0, stop=g == NG - 1)
                    for g in range(NG):
                        v0 = (NSLOT * g + h) * HD
                        for t in range(2):
                            ins = pe.matmul(pb[:, 3, P:NT], v_tok[:, t, v0:v0 + HD], probs_t[:, NG + 2 * g + t, :],
                                            start=g == 0 and t == 0, stop=g == NG - 1 and t == 1)
                    ins.then_inc(att_done, 1)

            def decode(i, j):
                if (i, j) == (4, 2):
                    pe.wait_ge(sc_ready, len(UNITS))
                    pe.wait_ge(kq_ready, 1)
                    pe.wait_ge(att_read, 2)
                    for g in range(NG):
                        pe.transpose(pb[0:32, 3, g * P:(g + 1) * P], sc_dec[:, g].rearrange("p b h -> p (b h)"), ident[:])
                    for g in range(NG):
                        ins = pe.matmul(pb[0:32, 3, NG * P + g:NG * P + g + 1], kq[:, g].rearrange("p b h -> p (b h)"), ones[:, 0:1],
                                        start=True, stop=True)
                    ins.then_inc(ds_done, 1)
                if (i, j) == (6, 2):
                    pe.wait_ge(diag_ready, 1)
                    pe.wait_ge(att_read, 3)
                    for g in range(NG):
                        pe.transpose(pb[:, 3, g * 32:(g + 1) * 32], dec_p[:, g * P:(g + 1) * P], ident[0:32, 0:32])
                    pe.matmul(pb[:, 3, P:P + 96], ones[0:32, :], dec_diag[:].rearrange("p a b -> p (a b)"),
                              start=True, stop=True).then_inc(dt_done, 1)

            def gates_b(i, ph=PH["gates_b"]):
                for j in range(8):
                    if j % 4 == 0:
                        open_group(ph, i, j // 4)
                    slab_products(ph, i, j, j // 4, xg_hi, xg_lo, KS * (j % 4), KS, j % 4 == 0, j % 4 == 3)
                    if j in (4, 7):
                        h = 0 if j == 4 else 1
                        k = 2 * i + h
                        pe.wait_ge(xr_ready, k + 1)
                        pe.wait_ge(xi_ready, k + 1)
                        if not (below(i, 1) and h == 0):
                            pe.wait_ge(y_read, k)
                        for t in range(4):
                            out = pb[:, 2, t * (NS + NB):(t + 1) * (NS + NB)]
                            for ri in range(2):
                                c0 = TB_C + (2 * t + ri) * P
                                pe.matmul(out, tab[h][:, c0:c0 + P], xs[:, ri, t, 0:NS + NB], start=ri == 0, stop=False)
                            ins = pe.matmul(out, tab[h][:, TB_K + t * P:TB_K + (t + 1) * P], u4[:, bass.ds(4 * k + t, 1), 0:NS + NB],
                                            start=False, stop=True)
                        ins.then_inc(y_done, 1)
                    if j in (1, 4):
                        h = j // 4
                        k = 2 * i + h
                        pe.wait_ge(tab_loaded[h], 16 * i + 16)
                        if below(i, 1) and h == 0:
                            pe.wait_ge(u4_loaded, 16 * 24)
                        else:
                            pe.wait_ge(sv_ready, k)
                        for t in range(4):
                            for ri in range(2):
                                c0 = TB_B + (2 * t + ri) * P
                                ins = pe.matmul(pb[:, ri, t * (NS + NB):(t + 1) * (NS + NB)], tab[h][:, c0:c0 + P],
                                                u4[:, bass.ds(4 * k + t, 1), NS:2 * NS + NB], start=True, stop=True)
                        ins.then_inc(su_done, 1)
                    if j in (2, 6):
                        h = j // 4
                        k = 2 * i + h
                        pe.wait_ge(v_sum_ready, k + 1)
                        if below(i, 1) and h == 0:
                            pe.wait_ge(att_read, NSLOT)
                        else:
                            pe.wait_ge(pv_read, k)
                        for hh in range(NSLOT):
                            ins = pe.matmul(pb[:, 3, hh:hh + 1], vu[3 * h][:, hh * HD:(hh + 1) * HD], ones[:, 0:1],
                                            start=True, stop=True)
                        ins.then_inc(pv_done, 1)

            pe.wait_ge(const_ready, 2)
            pe.wait_ge(vec_loaded, 16)
            pe.transpose(pb[:, 3, 0:KD], vec_rows[0:KD, :], ident[0:KD, 0:KD]).then_inc(vec_t, 1)
            for c in range(5):
                turn_in(c)
            ffn(0)
            for name in ("u", "q", "k", "v", "gates_a"):
                ph = PH[name]
                for i in range(ph.iters):
                    x = XQ.get(name, -99) + i
                    open_group(ph, i, 0)
                    for j in range(4):
                        if name == "u":
                            pe.wait_ge(xlo_ready, 8 + 2 * j + 2)
                        slab_products(ph, i, j, 0, xg_hi, xg_lo, KS * j, KS, j == 0, j == 3)
                        if name == "u" and i == 0 and j == 2:
                            mean_square(1)
                        if j == 1 and 1 <= x <= NH:
                            head_stats(x)
                        heads_to_rows(x, j)
                        if name == "gates_a":
                            attention(i, j)
                            decode(i, j)
            loop(pe, PH["gates_b"], gates_b, 1, 1)
            ph = PH["attn_branch"]
            pe.wait_ge(att_lo_ready, 1)
            for i in range(2):
                for g in range(4):
                    open_group(ph, i, g)
                    slab_products(ph, i, g, g, att_hi, att_lo, 0, KS, True, True)
            ph = PH["glu"]
            for i in range(2):
                for j in range(4):
                    if j % 2 == 0:
                        open_group(ph, i, j // 2)
                    pe.wait_ge(zlo_ready, j % 2 + 1)
                    slab_products(ph, i, j, j // 2, zs_hi, zs_lo, KS * (j % 2), KS, j % 2 == 0, j % 2 == 1)
                    if (i, j) == (0, 2):
                        pe.wait_ge(xnew_step, 8)
                        for ri in range(2):
                            for blk in range(2):
                                m = 2 * ri + blk
                                pe.transpose(pb[:, 0, m * P:(m + 1) * P], xnew[:, ri, blk * P:(blk + 1) * P], ident[:])
                        for ri in range(2):
                            ins = pe.transpose(pb[0:32, 1, ri * P:(ri + 1) * P], x_fin[:, ri, :], ident[:])
                        ins.then_inc(st_t, 1)

            def ssm_branch(i, ph=PH["ssm_branch"]):
                for j in range(4):
                    if j % 2 == 0:
                        open_group(ph, i, j // 2)
                    if below(i, 1):
                        pe.wait_ge(slo_ready, 2 * (j % 2) + 2)
                    slab_products(ph, i, j, j // 2, s_hi, s_lo, KS * (j % 2), KS, j % 2 == 0, j % 2 == 1)
            loop(pe, PH["ssm_branch"], ssm_branch, 1)

            def w_out(i, ph=PH["w_out"]):
                for j in range(8):
                    if j % 4 == 0:
                        open_group(ph, i, j // 4)
                    if below(i, 1) and j < 4:
                        pe.wait_ge(actlo_ready, ACT0["ssm_branch"] + 2 * j + 2)
                    slab_products(ph, i, j, j // 4, act_hi, act_lo, KS * (j % 4), KS, j % 4 == 0, j % 4 == 3)
            loop(pe, PH["w_out"], w_out, 1)
            ffn(1)
            turn_back(KD // 2 - 1)

        @block.gpsimd
        def _(pool):
            def squares(r, after):
                if r:
                    pool.wait_ge(mean_ready, r)
                pool.memset(ssq[:], 0.0).then_inc(ssq_zero, 1)
                pool.wait_ge(ssq_zero, r + 2)
                for c in range(8):
                    pool.wait_ge(sq_ready, 8 * r + c + 1)
                    if c:
                        pool.wait_ge(ssq_ready, 8 * r + c)
                    pool.tensor_tensor(ssq[:], ssq[:], squares_v[c % 2][:], ALU.add).then_inc(ssq_ready, 1)
                    after(c)

            def parameters():
                step = Chain(pool, step_done)
                tt, ts = pool.tensor_tensor, pool.tensor_scalar
                lr, li = prm[:, 0:NTILE], prm[:, NTILE:2 * NTILE]
                S = lambda k: scr[:, k]
                pool.wait_ge(prm_ready, 3)
                pool.wait_ge(dt_ready, 1)
                step(tt(S(1), lr, S(0), ALU.mult))
                step(tt(S(2), li, S(0), ALU.mult))
                step(ts(S(5), S(2), 1 / (2 * np.pi), None, ALU.mult))
                step(ts(S(6), S(5), 0.25, None, ALU.add))
                step(ts(scr[:, 5:7], scr[:, 5:7], MAGIC, None, ALU.add))
                step(ts(scr[:, 5:7], scr[:, 5:7], -MAGIC, None, ALU.add))
                for m, part in enumerate(TWO_PI):
                    step(ts(scr[:, 14:16], scr[:, 5:7], part, None, ALU.mult))
                    for k in range(2):
                        step(tt(S(3 + k), S(2) if m == 0 else S(3 + k), S(14 + k), ALU.subtract))
                step(ts(S(4), S(4), float(np.pi / 2), None, ALU.add))
                step(ts(scr[:, 3:5], scr[:, 3:5], 3.1415925, None, ALU.min))
                pool.tensor_scalar(scr[:, 3:5], scr[:, 3:5], -3.1415925, None, ALU.max).then_inc(angles_ready, 1)
                step(tt(S(14), lr, lr, ALU.mult))
                step(tt(S(15), li, li, ALU.mult))
                tt(S(11), S(14), S(15), ALU.add).then_inc(den_ready, 1)
                pool.wait_ge(trig_ready, 2)
                mag, sn, cn, ar, ai = S(8), S(9), S(10), a_t[:, 0], a_t[:, 1]
                step(tt(ar, mag, cn, ALU.mult))
                step(tt(ai, mag, sn, ALU.mult))
                step(ts(S(13), ar, -1.0, None, ALU.add))
                pool.wait_ge(inv_ready, 1)
                for out, p, q, op in ((16, (S(13), lr), (ai, li), ALU.add), (17, (ai, lr), (S(13), li), ALU.subtract)):
                    step(tt(S(14), *p, ALU.mult))
                    step(tt(S(15), *q, ALU.mult))
                    step(tt(S(out), S(14), S(15), op))
                    step(tt(S(out), S(out), S(12), ALU.mult))

                def cmul(outr, outi, xr, xi, yr, yi, t0, t1):
                    step(tt(t0, xr, yr, ALU.mult))
                    step(tt(t1, xi, yi, ALU.mult))
                    step(tt(outr, t0, t1, ALU.subtract))
                    step(tt(t0, xr, yi, ALU.mult))
                    step(tt(t1, xi, yr, ALU.mult))
                    step(tt(outi, t0, t1, ALU.add))

                step(pool.memset(pw[:, 0, :, 0:1], 1.0))
                step(pool.memset(pw[:, 1, :, 0:1], 0.0))
                for n in range(1, LAGS):
                    cmul(pw[:, 0, :, n], pw[:, 1, :, n], pw[:, 0, :, n - 1], pw[:, 1, :, n - 1], ar, ai, S(14), S(15))
                step(ts(npowi[:], pw[:, 1], -1.0, None, ALU.mult))
                for s in range(STEP):
                    n = STEP - 1 - s
                    cmul(wf[:, 0, :, s], wf[:, 1, :, s], pw[:, 0, :, n], pw[:, 1, :, n], S(16), S(17), S(14), S(15))
                step(tt(S(18), mag, mag, ALU.mult))
                step(tt(S(19), S(18), S(18), ALU.mult))
                step(pool.tensor_copy(em_tab[:, 2], scr[:, 19, :, None].to_broadcast([P, NTILE, NB])))
                step(pool.memset(em_tab[:, 2, :, 0:1], 0.0))
                cmul(S(20), S(21), cn, sn, cn, sn, S(14), S(15))
                cmul(S(22), S(23), S(20), S(21), S(20), S(21), S(14), S(15))
                step(pool.memset(em_tab[:, 0, :, 0:1], 1.0))
                step(pool.memset(em_tab[:, 1, :, 0:1], 0.0))
                n, u, w = 1, (22, 23), (24, 25)
                while n < NB:
                    ur, ui = (scr[:, k, :, None].to_broadcast([P, NTILE, n]) for k in u)
                    cmul(em_tab[:, 0, :, n:2 * n], em_tab[:, 1, :, n:2 * n], em_tab[:, 0, :, 0:n], em_tab[:, 1, :, 0:n], ur, ui,
                         ctmp[:, 0, :, 0:n], ctmp[:, 1, :, 0:n])
                    cmul(S(w[0]), S(w[1]), S(u[0]), S(u[1]), S(u[0]), S(u[1]), S(14), S(15))
                    n, u, w = 2 * n, w, u
                for k in range(SC):
                    pool.dma_start(ssm_tab[k, :, TB_E:TB].rearrange("p (a t c) -> p a t c", a=3, t=4),
                                   em_tab[:, :, 4 * k:4 * k + 4, :]).then_inc(e_stored, 16)
                pool.wait_ge(e_stored, 16 * SC)
                step(pool.memset(pre[:], 0.0))
                step(pool.memset(kbig[:], 0.0))
                return step

            def half_b(i, step):
                def w_of(ri):
                    return wf[:, ri, 4 * i:4 * i + 4, :, None].to_broadcast([P, 4, STEP, 16])
                def b_of(ri):
                    return b_in[:, ri, 4 * i:4 * i + 4, None, :].to_broadcast([P, 4, STEP, 16])
                for ri, (x, y, op) in enumerate((((0, 0), (1, 1), ALU.subtract), ((0, 1), (1, 0), ALU.add))):
                    step(pool.tensor_tensor(b_tmp[:, 0], w_of(x[0]), b_of(x[1]), ALU.mult))
                    step(pool.tensor_tensor(b_tmp[:, 1], w_of(y[0]), b_of(y[1]), ALU.mult))
                    for g in range(2):
                        step(pool.tensor_tensor(pre[64 * g:64 * g + 64, ri, :, :, g, :], b_tmp[64 * g:64 * g + 64, 0],
                                                b_tmp[64 * g:64 * g + 64, 1], op))
                for ri in range(2):
                    for g in range(2):
                        ins = pool.tensor_scalar(c_exp[:, ri, g, :], c_in[:, ri, i, :],
                                                 gm[:, g:g + 1], None, ALU.mult)
                ins.then_inc(pre_ready, 1)

            def c_im(i, step):
                pool.wait_ge(bbt_ready, i + 1)
                if i:
                    pool.wait_ge(tab_stored, 48 * i)
                for k, p in ((0, npowi), (1, pw[:, 0])):
                    step(pool.tensor_tensor(im_tmp[:, k].rearrange("p t (n f) -> p t n f", n=LAGS),
                                            c_t[:, k, :, None, :].to_broadcast([P, 4, LAGS, 32]),
                                            p[:, 4 * i:4 * i + 4, :, None].to_broadcast([P, 4, LAGS, 32]), ALU.mult))
                pool.tensor_tensor(ca5[:, :, 1, :], im_tmp[:, 0], im_tmp[:, 1], ALU.subtract).then_inc(ca_im_ready, 1)

            pool.memset(ident[:], 0.0).then_inc(ssq_zero, 1)
            pool.wait_ge(ssq_zero, 1)
            pool.affine_select(out=ident[:], in_=ident[:], compare_op=ALU.not_equal, fill=1.0,
                               base=0, pattern=[[-1, P]], channel_multiplier=1).then_inc(const_ready, 1)
            pool.dma_start(gm[:], A["consts"][:, C_GM:C_GM + 2]).then_inc(b_loaded, 16)
            squares(0, lambda c: None)
            for ri, name in enumerate(("ssm_b_re", "ssm_b_im")):
                pool.dma_start(b_in[:, ri], A[name][0].rearrange("(t g) p c -> (g p) t c", g=2)).then_inc(b_loaded, 16)
            for ri, name in enumerate(("ssm_c_re", "ssm_c_im")):
                pool.dma_start(c_in[:, ri], A[name][0].rearrange("(k q) c p -> (q c) k p", k=SC)).then_inc(b_loaded, 16)
            step = parameters()
            pool.wait_ge(b_loaded, 16 * 5)
            for i in range(SC):
                if i:
                    pool.wait_ge(k_done, i)
                half_b(i, step)
                c_im(i, step)

            def spill(c):
                pool.wait_ge(evacuated, PH["down02"].group0 + c + 1)
                pool.dma_start(x_dram[:, 2 * c * T:(2 * c + 2) * T], x_t[:, 2 * c:2 * c + 2, :].rearrange("p a t -> p (a t)")).then_inc(spilled, 16)
            squares(1, spill)
            pool.wait_ge(spilled, 16 * KD // 2)
            pool.wait_ge(xlo_ready, KD)
            for lo in (0, NS + NB):
                ins = pool.memset(u4[:, :, lo:lo + NS], 0.0)
            ins.then_inc(u4_zero, 1)

            pool.wait_ge(tab_stored, 16 * 3 * SC)
            pool.wait_ge(const_loaded, 32)

            def heads(x):
                for u in range(2):
                    n = 2 * x + u
                    pool.wait_ge(t1_ready, n + 1)
                    if n:
                        pool.wait_ge(qk_ready, n)
                    for k, (to, frm) in enumerate(((0, 64), (64, 0))):
                        pool.tensor_tensor(silu_v[to:to + 64, u], up_v[frm:frm + 64, u], cs[frm:frm + 64, 1], ALU.mult).then_inc(rot_ready, 1)
                        pool.wait_ge(rot_ready, 2 * n + k + 1)
                    pool.tensor_tensor(qk[:, n], up_v[:, u], cs[:, 0], ALU.mult).then_inc(cos_ready, 1)
                    pool.wait_ge(cos_ready, n + 1)
                    pool.tensor_tensor(qk[:, n], qk[:, n], silu_v[:, u], ALU.add).then_inc(qk_ready, 1)

            def store_rows(r):
                pool.wait_ge(rows_ready, 2 * r + 2)
                g, kv = r % 3, r // 3 - 1
                if kv < 0:
                    pool.dma_start(q_dram[:, g * 512:(g + 1) * 512], s_rows[0:NS, :]).then_inc(rows_stored, 16)
                    return
                n = GROUPS[g][0]
                pool.dma_start(new_caches[g][:, kv, n - 1].rearrange("b h d -> b (h d)"), s_rows[0:NS, :]).then_inc(rows_stored, 16)
                src = k_rows if kv == 0 else v_tok[:, :, g * 512:(g + 1) * 512]
                dst = prompt_kv[g][kv].rearrange("n h d -> n (h d)")
                if g == 0:
                    pool.dma_start(dst, src[:, 1]).then_inc(rows_stored, 16)
                else:
                    pool.dma_start(dst.rearrange("(t p) c -> p t c", p=P), src if kv else src[:]).then_inc(rows_stored, 16)

            def unit(n):
                pool.wait_ge(ku_loaded[n % 4], 16 * (n // 4 + 1))
                pool.wait_ge(qb_loaded[n % 2], 16 * (n // 2 + 1))
                if n >= 2:
                    pool.wait_ge(sc_ready, n - 1)
                pool.tensor_tensor(prod[n % 2][:].rearrange("p h d -> p (h d)"), ku[n % 4][:], qb[n % 2][:], ALU.mult).then_inc(prod_ready, 1)

            for x in range(NH):
                if x >= 2 and x % 2 == 0:
                    store_rows((x - 2) // 2)
                heads(x)
            store_rows(5)
            for n in range(len(UNITS)):
                unit(n)
                if n in (3, 11, 19):
                    store_rows(6 + n // 8)
            q_s = qk[:, 0:NH, NT:T].rearrange("p (g h) b -> p g b h", g=NG)
            k_s = qk[:, NH:2 * NH, NT:T].rearrange("p (g h) b -> p g b h", g=NG)
            pool.tensor_tensor(kq[:], q_s, k_s, ALU.mult).then_inc(kq_ready, 1)

            pool.wait_ge(att_done, NSLOT)
            pool.memset(xs[:, :, :, NS:NS + 1], 0.0).then_inc(xs_zero, 1)

            def gates_b(i):
                for h in range(2):
                    k = 2 * i + h
                    pool.wait_ge(vs_ready, k + 1)
                    pool.tensor_tensor(vu[3 * h][:], vu[3 * h][:], vu[3 * h + 1][:], ALU.add).then_inc(v_step, 1)
                    pool.wait_ge(v_step, k + 1)
                    pool.tensor_tensor(vu[3 * h][:], vu[3 * h][:], vu[3 * h + 2][:], ALU.add).then_inc(v_sum_ready, 1)
                    E = tab[h][:, E0:M0].rearrange("p (a c) -> p a c", a=2)
                    pool.wait_ge(sv_ready, k + 1)
                    if not (below(i, 1) and h == 0):
                        pool.wait_ge(xr_ready, k)
                    pool.tensor_tensor(p_tmp[:, 0], sv[:, 0], E[:, 0], ALU.mult).then_inc(zr_step, 1)
                    pool.wait_ge(zr_step, 4 * k + 1)
                    pool.tensor_tensor(p_tmp[:, 1], sv[:, 1], E[:, 1], ALU.mult).then_inc(zr_step, 1)
                    pool.wait_ge(zr_step, 4 * k + 2)
                    pool.tensor_tensor(z_in[:, 0], p_tmp[:, 0], p_tmp[:, 1], ALU.add).then_inc(zr_ready, 1)
                    pool.wait_ge(scan_ready, 2 * k + 2)
                    pool.tensor_tensor(p_tmp[:, 0], z_out[:, 0], E[:, 0], ALU.mult).then_inc(zr_step, 1)
                    pool.wait_ge(zr_step, 4 * k + 3)
                    pool.tensor_tensor(p_tmp[:, 1], z_out[:, 1], E[:, 1], ALU.mult).then_inc(zr_step, 1)
                    pool.wait_ge(zr_step, 4 * k + 4)
                    if not (below(i, 1) and h == 0):
                        pool.wait_ge(y_read, k)
                    pool.tensor_tensor(xs[:, 0, :, NS + 1:NS + 1 + NB], p_tmp[:, 0].rearrange("p (t c) -> p t c", t=4),
                                       p_tmp[:, 1].rearrange("p (t c) -> p t c", t=4), ALU.subtract).then_inc(xr_ready, 1)
            loop(pool, PH["gates_b"], gates_b, 1, 1)
            pool.wait_ge(y_read, SC)
            for jj in range(4):
                if jj >= 2:
                    pool.dma_start(yt_v[32 * jj:32 * jj + 32, :, 3 * NB:4 * NB], u4[96:128, jj::4, NS:NS + NB]).then_inc(yl_loaded, 16)
                pool.dma_start(yt_v[32 * jj:32 * jj + 32, :, NT:T], u4[0:32, jj::4, 0:NS]).then_inc(yl_loaded, 16)
            pool.wait_ge(pv_done, NS)
            step = Chain(pool, xnew_step)
            ar, ai = (a_t[:, ri, None, :].to_broadcast([P, NS, NTILE]) for ri in range(2))
            tmp = [xtmp[:, k].rearrange("p (b t) -> p b t", b=NS) for k in range(2)]
            for ri, (x, y, op) in enumerate(((0, 1, ALU.subtract), (1, 0, ALU.add))):
                step(pool.tensor_tensor(tmp[0], ar, x0_t[:, x], ALU.mult))
                step(pool.tensor_tensor(tmp[1], ai, x0_t[:, y], ALU.mult))
                step(pool.tensor_tensor(tmp[0], tmp[0], tmp[1], op))
                step(pool.tensor_tensor(xnew[:, ri].rearrange("p (b t) -> p b t", b=NS), tmp[0],
                                        s_new[:, ri].rearrange("p t b -> p b t"), ALU.add))
            pool.wait_ge(yt_loaded, 16 * 14)
            pool.wait_ge(yl_loaded, 16 * 6)
            pool.wait_ge(att_lo_ready, 1)
            pool.dma_start(x_t[:].rearrange("p a t -> p (a t)"), x_dram).then_inc(x_back, 16)
            pool.wait_ge(st_rows_ready, 1)
            for ri, (sample, prompt) in enumerate((("ssm_re_s", "ssm_re_p"), ("ssm_im_s", "ssm_im_p"))):
                pool.dma_start(O[sample][0].rearrange("(k b) (t g) s -> (b t) k (g s)", k=2, g=2),
                               st_rows[:, 2 * ri:2 * ri + 2, :]).then_inc(rows_stored, 16)
                pool.dma_start(O[prompt][0, 0].rearrange("(t g) s -> t (g s)", g=2), st_rows[0:32, 4 + ri, :]).then_inc(rows_stored, 16)
            squares(2, lambda c: None)
            pool.wait_ge(rows_stored, stored_rows(8) + 64)


_OUTS = [("y_p", (1, 256, 2048)), ("y_s", (8, 1, 2048)),
         ("kv128_p", (1, 1, 2, 128, 4, 128)), ("kv512_p", (1, 1, 2, 256, 4, 128)), ("kv2048_p", (1, 1, 2, 256, 4, 128)),
         ("ssm_re_p", (1, 1, 64, 64)), ("ssm_im_p", (1, 1, 64, 64)),
         ("kv128_s", (1, 8, 2, 128, 4, 128)), ("kv512_s", (1, 8, 2, 512, 4, 128)), ("kv2048_s", (1, 8, 2, 2048, 4, 128)),
         ("ssm_re_s", (1, 8, 64, 64)), ("ssm_im_s", (1, 8, 64, 64))]


def kernel(**inputs):
    import concourse.bacc as _bacc
    from concourse.bass_utils import run_bass_kernel_spmd as _run

    nc = _bacc.Bacc("TRN2", target_bir_lowering=False, num_devices=1)
    arrays, args, outs = {}, {}, {}
    for name, a in {**inputs, "consts": shape_constants()}.items():
        a = np.ascontiguousarray(a)
        arrays[f"in_{name}"] = a
        args[name] = nc.dram_tensor(f"in_{name}", a.shape, mybir.dt.from_np(a.dtype), kind="ExternalInput").ap()
    for name, shape in _OUTS:
        outs[name] = nc.dram_tensor(f"out_{name}", shape, mybir.dt.float32, kind="ExternalOutput").ap()
    build_layer(nc, args, outs)
    r = _run(nc, [arrays], core_ids=[0])
    return tuple(r.results[0][f"out_{name}"] for name, _ in _OUTS)
```
